# Optimizing a Trainium2 kernel written in Bass

```python
import jax, jax.numpy as jnp
from jax import lax
import numpy as np
import math

D_MODEL = 2048
BATCH = 1
SEQ = 256
DEPTH = 1

HEAD_DIM = 64
N_FOX_HEADS = 16
N_DIL_HEADS = 16
FOX_WIDTH = N_FOX_HEADS * HEAD_DIM
DIL_WIDTH = N_DIL_HEADS * HEAD_DIM
MIX_WIDTH = FOX_WIDTH + DIL_WIDTH
ROPE_THETA = 500000.0
ROPE_DIM = HEAD_DIM // 4
DILATED_PAIRS = ((128, 1), (512, 4), (2048, 16))
Q_BLOCK = 128
PEER_HEADS = 8
PEER_N_KEYS = 128
PEER_N_EXPERTS = PEER_N_KEYS * PEER_N_KEYS
PEER_KEY_DIM = 256
PEER_HALF = PEER_KEY_DIM // 2
PEER_TOPK = 16
PEER_TOKEN_BLOCK = 128
RMS_EPS = 1e-6
IN_COLS = 3 * FOX_WIDTH + N_FOX_HEADS + 3 * DIL_WIDTH


def rms_norm(x, g):
    xf = x.astype(jnp.float32)
    y = xf * lax.rsqrt(jnp.mean(xf * xf, axis=-1, keepdims=True) + RMS_EPS)
    return y.astype(x.dtype) * g

def partial_rope(x, pos):
    inv = ROPE_THETA ** (-jnp.arange(0, ROPE_DIM, 2, dtype=jnp.float32) / ROPE_DIM)
    ang = pos.astype(jnp.float32)[:, None] * inv[None, :]
    cos = jnp.cos(ang)[None, :, None, :].astype(x.dtype)
    sin = jnp.sin(ang)[None, :, None, :].astype(x.dtype)
    xr, xp = x[..., :ROPE_DIM], x[..., ROPE_DIM:]
    x1, x2 = xr[..., :ROPE_DIM // 2], xr[..., ROPE_DIM // 2:]
    rot = jnp.concatenate([x1 * cos - x2 * sin, x2 * cos + x1 * sin], axis=-1)
    return jnp.concatenate([rot, xp], axis=-1)

def forgetting_attention(q, k, v, f_logit):
    B, S, H, hd = q.shape
    nb = S // Q_BLOCK
    log_f = jax.nn.log_sigmoid(f_logit.astype(jnp.float32))
    c = jnp.cumsum(log_f, axis=1).transpose(0, 2, 1)
    qh = q.transpose(0, 2, 1, 3) * (hd ** -0.5)
    kh = k.transpose(0, 2, 1, 3)
    vh = v.transpose(0, 2, 1, 3)
    q_blocks = qh.reshape(B, H, nb, Q_BLOCK, hd).transpose(2, 0, 1, 3, 4)
    c_blocks = c.reshape(B, H, nb, Q_BLOCK).transpose(2, 0, 1, 3)
    starts = jnp.arange(nb, dtype=jnp.int32) * Q_BLOCK
    k_pos = jnp.arange(S, dtype=jnp.int32)

    def block(args):
        qb, cb, s0 = args
        logits = jnp.einsum('bhqd,bhkd->bhqk', qb, kh).astype(jnp.float32)
        logits = logits + (cb[..., :, None] - c[..., None, :])
        q_pos = s0 + jnp.arange(Q_BLOCK, dtype=jnp.int32)
        mask = k_pos[None, :] <= q_pos[:, None]
        logits = jnp.where(mask, logits, -jnp.inf)
        p = jax.nn.softmax(logits, axis=-1).astype(vh.dtype)
        return jnp.einsum('bhqk,bhkd->bhqd', p, vh)

    o = lax.map(block, (q_blocks, c_blocks, starts))
    return o.transpose(1, 0, 3, 2, 4).reshape(B, S, H, hd)

def dilated_pattern(q, k, v, window, dilation):
    B, S, H, hd = q.shape
    span = window // dilation
    unit = dilation * Q_BLOCK
    s_pad = -(-S // unit) * unit
    L = s_pad // dilation
    nb = L // Q_BLOCK
    pad = ((0, 0), (0, s_pad - S), (0, 0), (0, 0))

    def to_sub(t):
        t = jnp.pad(t, pad).reshape(B, L, dilation, H, hd)
        return t.transpose(0, 2, 3, 1, 4).reshape(B, dilation, H, nb, Q_BLOCK, hd)

    def with_prev(t):
        prev = jnp.pad(t, ((0, 0), (0, 0), (0, 0), (1, 0), (0, 0), (0, 0)))[:, :, :, :-1]
        return jnp.concatenate([prev, t], axis=-2)

    qs = to_sub(q)
    kk = with_prev(to_sub(k))
    vv = with_prev(to_sub(v))
    logits = jnp.einsum('brhnqd,brhnkd->brhnqk', qs, kk).astype(jnp.float32) * (hd ** -0.5)
    qi = jnp.arange(Q_BLOCK)[:, None]
    kj = jnp.arange(2 * Q_BLOCK)[None, :]
    dist = qi + Q_BLOCK - kj
    band = (dist >= 0) & (dist <= span)
    has_prev = (jnp.arange(nb)[:, None, None] > 0) | (kj[None] >= Q_BLOCK)
    mask = band[None] & has_prev
    logits = jnp.where(mask, logits, -jnp.inf)
    m = jnp.max(logits, axis=-1, keepdims=True)
    e = jnp.exp(logits - m)
    den = jnp.sum(e, axis=-1, keepdims=True)
    o = jnp.einsum('brhnqk,brhnkd->brhnqd', (e / den).astype(v.dtype), vv)
    lse = (m + jnp.log(den))[..., 0]
    o = o.reshape(B, dilation, H, L, hd).transpose(0, 3, 1, 2, 4).reshape(B, s_pad, H, hd)[:, :S]
    lse = lse.reshape(B, dilation, H, L).transpose(0, 3, 1, 2).reshape(B, s_pad, H)[:, :S]
    return o, lse

def dilated_attention(q, k, v):
    outs = []
    lses = []
    for window, dilation in DILATED_PAIRS:
        o, lse = dilated_pattern(q, k, v, window, dilation)
        outs.append(o)
        lses.append(lse)
    wts = jax.nn.softmax(jnp.stack(lses, axis=0), axis=0)
    return jnp.sum(wts[..., None].astype(q.dtype) * jnp.stack(outs, axis=0), axis=0)

def peer(x, w_query, sub_keys, expert_down, expert_up):
    B, S, D = x.shape
    T = B * S
    xt = x.reshape(T, D)
    q = (xt @ w_query).reshape(T, PEER_HEADS, 2, PEER_HALF)
    scores = jnp.einsum('thpc,hpnc->thpn', q, sub_keys).astype(jnp.float32)
    vals, idx = lax.top_k(scores, PEER_TOPK)
    cand = (vals[..., 0, :, None] + vals[..., 1, None, :]).reshape(T, PEER_HEADS, PEER_TOPK * PEER_TOPK)
    top_vals, top_c = lax.top_k(cand, PEER_TOPK)
    i1 = jnp.take_along_axis(idx[..., 0, :], top_c // PEER_TOPK, axis=-1)
    i2 = jnp.take_along_axis(idx[..., 1, :], top_c % PEER_TOPK, axis=-1)
    experts = (i1 * PEER_N_KEYS + i2).reshape(T, PEER_HEADS * PEER_TOPK)
    gates = jax.nn.softmax(top_vals, axis=-1).reshape(T, PEER_HEADS * PEER_TOPK).astype(x.dtype)
    nc = T // PEER_TOKEN_BLOCK

    def block(args):
        xc, ec, gc = args
        u = jnp.take(expert_down, ec, axis=0)
        hdn = jax.nn.gelu(jnp.einsum('ted,td->te', u, xc))
        vsel = jnp.take(expert_up, ec, axis=0)
        return jnp.einsum('te,ted->td', gc * hdn, vsel)

    y = lax.map(block, (xt.reshape(nc, PEER_TOKEN_BLOCK, D),
                        experts.reshape(nc, PEER_TOKEN_BLOCK, PEER_HEADS * PEER_TOPK),
                        gates.reshape(nc, PEER_TOKEN_BLOCK, PEER_HEADS * PEER_TOPK)))
    return y.reshape(B, S, D)

def first_inputs(seed: int = 0) -> dict:
    key = jax.random.key(seed)
    ks = jax.random.split(key, 16)
    f32 = jnp.float32
    x = jax.random.normal(ks[0], (BATCH, SEQ, D_MODEL), f32)
    attn_norm_gain = 1.0 + 0.02 * jax.random.normal(ks[1], (DEPTH, D_MODEL), f32)
    w_in = jax.random.normal(ks[2], (DEPTH, D_MODEL, IN_COLS), f32) * D_MODEL ** -0.5
    forget_bias = jax.random.uniform(ks[3], (DEPTH, N_FOX_HEADS), f32, 1.0, 6.0)
    fox_out_gain = 1.0 + 0.02 * jax.random.normal(ks[4], (DEPTH, FOX_WIDTH), f32)
    dil_out_gain = 1.0 + 0.02 * jax.random.normal(ks[5], (DEPTH, DIL_WIDTH), f32)
    w_out = jax.random.normal(ks[6], (DEPTH, MIX_WIDTH, D_MODEL), f32) * MIX_WIDTH ** -0.5
    ffn_norm_gain = 1.0 + 0.02 * jax.random.normal(ks[7], (DEPTH, D_MODEL), f32)
    peer_query = jax.random.normal(ks[8], (DEPTH, D_MODEL, PEER_HEADS * PEER_KEY_DIM), f32) * D_MODEL ** -0.5
    peer_sub_keys = jax.random.normal(ks[9], (DEPTH, PEER_HEADS, 2, PEER_N_KEYS, PEER_HALF), f32) * PEER_HALF ** -0.5
    peer_down = jax.random.normal(ks[10], (DEPTH, PEER_N_EXPERTS, D_MODEL), f32) * D_MODEL ** -0.5
    peer_up = jax.random.normal(ks[11], (DEPTH, PEER_N_EXPERTS, D_MODEL), f32) * (PEER_HEADS * PEER_TOPK) ** -0.5
    final_norm_gain = 1.0 + 0.02 * jax.random.normal(ks[12], (D_MODEL,), f32)
    return {'x': x, 'attn_norm_gain': attn_norm_gain, 'w_in': w_in, 'forget_bias': forget_bias,
            'fox_out_gain': fox_out_gain, 'dil_out_gain': dil_out_gain, 'w_out': w_out,
            'ffn_norm_gain': ffn_norm_gain, 'peer_query': peer_query, 'peer_sub_keys': peer_sub_keys,
            'peer_down': peer_down, 'peer_up': peer_up, 'final_norm_gain': final_norm_gain}

def first_block(x, attn_norm_gain, w_in, forget_bias, fox_out_gain, dil_out_gain, w_out,
              ffn_norm_gain, peer_query, peer_sub_keys, peer_down, peer_up, final_norm_gain):
    B, S, _ = x.shape
    pos = jnp.arange(S, dtype=jnp.int32)
    splits = [FOX_WIDTH, 2 * FOX_WIDTH, 3 * FOX_WIDTH, 3 * FOX_WIDTH + N_FOX_HEADS,
              3 * FOX_WIDTH + N_FOX_HEADS + DIL_WIDTH, 3 * FOX_WIDTH + N_FOX_HEADS + 2 * DIL_WIDTH]
    h = x
    for layer in range(DEPTH):
        xn = rms_norm(h, attn_norm_gain[layer])
        proj = xn @ w_in[layer]
        fq, fk, fv, fg, dq, dk, dv = jnp.split(proj, splits, axis=-1)
        heads_f = (B, S, N_FOX_HEADS, HEAD_DIM)
        heads_d = (B, S, N_DIL_HEADS, HEAD_DIM)
        fox_o = forgetting_attention(fq.reshape(heads_f), fk.reshape(heads_f), fv.reshape(heads_f),
                                     fg + forget_bias[layer])
        dq = partial_rope(dq.reshape(heads_d), pos)
        dk = partial_rope(dk.reshape(heads_d), pos)
        dil_o = dilated_attention(dq, dk, dv.reshape(heads_d))
        mixed = jnp.concatenate([rms_norm(fox_o.reshape(B, S, FOX_WIDTH), fox_out_gain[layer]),
                                 rms_norm(dil_o.reshape(B, S, DIL_WIDTH), dil_out_gain[layer])], axis=-1)
        h = h + mixed @ w_out[layer]
        hn = rms_norm(h, ffn_norm_gain[layer])
        h = h + peer(hn, peer_query[layer], peer_sub_keys[layer], peer_down[layer], peer_up[layer])
    return rms_norm(h, final_norm_gain)


MIX_WIDTH_2 = D_MODEL
SWA_WIDTH = 3 * MIX_WIDTH_2 // 8
SWA_HEADS = SWA_WIDTH // HEAD_DIM
SWA_KV_HEADS = SWA_HEADS // 3
SWA_GROUP = SWA_HEADS // SWA_KV_HEADS
WINDOW = 128
SWA_BLOCK = 128
REL_BUCKETS = 32
REL_MAX_DIST = 128
GLA_WIDTH = 3 * MIX_WIDTH_2 // 8
GLA_HEADS = 4
GLA_DV = GLA_WIDTH // GLA_HEADS
GLA_DK = GLA_DV // 2
GLA_LOWRANK = 16
GLA_CHUNK = 64
GATE_NORMALIZER = 16.0
GATE_LOG_MIN = -1.0
SB_WIDTH = MIX_WIDTH_2 - SWA_WIDTH - GLA_WIDTH
SB_HEADS = SB_WIDTH // HEAD_DIM
SB_BLOCK = 128
D_FF = 4 * D_MODEL
NEG_INF = -1e30

PROJ_SIZES = (
    SWA_WIDTH, SWA_KV_HEADS * HEAD_DIM, SWA_KV_HEADS * HEAD_DIM,
    GLA_HEADS * GLA_DK, GLA_HEADS * GLA_DK, GLA_WIDTH, GLA_WIDTH, GLA_LOWRANK,
    SB_WIDTH, SB_WIDTH, SB_WIDTH,
)
PROJ_WIDTH = sum(PROJ_SIZES)


def rmsnorm(x, gain, eps=RMS_EPS):
    xf = x.astype(jnp.float32)
    y = xf * lax.rsqrt(jnp.mean(xf * xf, axis=-1, keepdims=True) + eps)
    return (y * gain.astype(jnp.float32)).astype(x.dtype)

def t5_causal_bucket(dist):
    max_exact = REL_BUCKETS // 2
    is_small = dist < max_exact
    ratio = jnp.log(jnp.maximum(dist, 1).astype(jnp.float32) / max_exact) / math.log(REL_MAX_DIST / max_exact)
    large = max_exact + (ratio * (REL_BUCKETS - max_exact)).astype(jnp.int32)
    large = jnp.minimum(large, REL_BUCKETS - 1)
    return jnp.where(is_small, dist, large)

def swa_sink_attention(q, k, v, sinks, rel_bias):
    B, S = q.shape[:2]
    nb = S // SWA_BLOCK
    qb = q.reshape(B, nb, SWA_BLOCK, SWA_KV_HEADS, SWA_GROUP, HEAD_DIM)
    kb = k.reshape(B, nb, SWA_BLOCK, SWA_KV_HEADS, HEAD_DIM)
    vb = v.reshape(B, nb, SWA_BLOCK, SWA_KV_HEADS, HEAD_DIM)
    pad = ((0, 0), (1, 0), (0, 0), (0, 0), (0, 0))
    kw = jnp.concatenate([jnp.pad(kb, pad)[:, :-1], kb], axis=2)
    vw = jnp.concatenate([jnp.pad(vb, pad)[:, :-1], vb], axis=2)
    logits = jnp.einsum('bnqhgd,bnkhd->bnhgqk', qb, kw).astype(jnp.float32) * (HEAD_DIM ** -0.5)
    qpos = jnp.arange(SWA_BLOCK) + SWA_BLOCK
    kpos = jnp.arange(2 * SWA_BLOCK)
    dist = qpos[:, None] - kpos[None, :]
    in_window = (dist >= 0) & (dist < WINDOW)
    key_abs = jnp.arange(nb)[:, None] * SWA_BLOCK - SWA_BLOCK + kpos[None, :]
    mask = in_window[None, :, :] & (key_abs >= 0)[:, None, :]
    bias = rel_bias.astype(jnp.float32)[t5_causal_bucket(jnp.maximum(dist, 0))]
    bias = bias.transpose(2, 0, 1).reshape(SWA_KV_HEADS, SWA_GROUP, SWA_BLOCK, 2 * SWA_BLOCK)
    logits = jnp.where(mask[None, :, None, None], logits + bias[None, None], NEG_INF)
    sink_col = jnp.broadcast_to(
        sinks.astype(jnp.float32).reshape(1, 1, SWA_KV_HEADS, SWA_GROUP, 1, 1),
        logits.shape[:-1] + (1,))
    probs = jax.nn.softmax(jnp.concatenate([logits, sink_col], axis=-1), axis=-1)[..., :-1]
    out = jnp.einsum('bnhgqk,bnkhd->bnqhgd', probs.astype(v.dtype), vw)
    return out.reshape(B, S, SWA_HEADS * HEAD_DIM)

def gla_chunked(q, k, v, log_gate):
    B, S, H, dk = q.shape
    dv = v.shape[-1]
    n = S // GLA_CHUNK
    f32 = jnp.float32
    q = (q.astype(f32) * dk ** -0.5).reshape(B, n, GLA_CHUNK, H, dk)
    k = k.astype(f32).reshape(B, n, GLA_CHUNK, H, dk)
    v = v.astype(f32).reshape(B, n, GLA_CHUNK, H, dv)
    b = jnp.cumsum(log_gate.reshape(B, n, GLA_CHUNK, H, dk), axis=2)
    b_last = b[:, :, -1:]
    q_dec = q * jnp.exp(b)
    k_inv = k * jnp.exp(-b)
    k_end = k * jnp.exp(b_last - b)
    causal = jnp.tril(jnp.ones((GLA_CHUNK, GLA_CHUNK), dtype=bool))
    scores = jnp.where(causal, jnp.einsum('bnthk,bnshk->bnhts', q_dec, k_inv), 0.0)
    o_intra = jnp.einsum('bnhts,bnshv->bnthv', scores, v)
    d_state = jnp.einsum('bnshk,bnshv->bnhkv', k_end, v)
    decay = jnp.exp(b_last[:, :, 0])

    def step(state, inp):
        dec, ds = inp
        return dec[..., None] * state + ds, state

    init = jnp.zeros((B, H, dk, dv), f32)
    _, s_prev = lax.scan(step, init, (decay.swapaxes(0, 1), d_state.swapaxes(0, 1)))
    s_prev = s_prev.swapaxes(0, 1)
    o_inter = jnp.einsum('bnthk,bnhkv->bnthv', q_dec, s_prev)
    return (o_intra + o_inter).reshape(B, S, H, dv)

def stick_breaking_attention(q, k, v):
    B, S, H, D = q.shape
    nb = S // SB_BLOCK
    qb = q.reshape(B, nb, SB_BLOCK, H, D).swapaxes(0, 1)
    kpos = jnp.arange(S)
    scale = D ** -0.5

    def block(args):
        q_blk, i = args
        z = jnp.einsum('bqhd,bshd->bhqs', q_blk, k).astype(jnp.float32) * scale
        qpos = i * SB_BLOCK + jnp.arange(SB_BLOCK)
        strict = kpos[None, :] < qpos[:, None]
        log_beta = jax.nn.log_sigmoid(z)
        log_1m_beta = jnp.where(strict, jax.nn.log_sigmoid(-z), 0.0)
        between = lax.cumsum(log_1m_beta, axis=3, reverse=True) - log_1m_beta
        w = jnp.where(strict, jnp.exp(log_beta + between), 0.0)
        return jnp.einsum('bhqs,bshd->bqhd', w.astype(v.dtype), v)

    out = lax.map(block, (qb, jnp.arange(nb)))
    return out.swapaxes(0, 1).reshape(B, S, H * D)

def token_mixing(h, w_in, sinks, rel_bias, gla_gate_w, gla_gate_b, gla_norm,
                 swa_out_norm, sb_out_norm, w_out):
    B, S, _ = h.shape
    proj = h @ w_in
    split_at = np.cumsum(PROJ_SIZES)[:-1].tolist()
    aq, ak, av, bq, bk, bv, br, blr, cq, ck, cv = jnp.split(proj, split_at, axis=-1)
    out_a = swa_sink_attention(
        aq.reshape(B, S, SWA_HEADS, HEAD_DIM),
        ak.reshape(B, S, SWA_KV_HEADS, HEAD_DIM),
        av.reshape(B, S, SWA_KV_HEADS, HEAD_DIM), sinks, rel_bias)
    out_a = rmsnorm(out_a, swa_out_norm)
    gate_pre = (blr @ gla_gate_w + gla_gate_b).astype(jnp.float32)
    log_gate = jnp.maximum(jax.nn.log_sigmoid(gate_pre) / GATE_NORMALIZER, GATE_LOG_MIN)
    o_b = gla_chunked(
        bq.reshape(B, S, GLA_HEADS, GLA_DK),
        bk.reshape(B, S, GLA_HEADS, GLA_DK),
        bv.reshape(B, S, GLA_HEADS, GLA_DV),
        log_gate.reshape(B, S, GLA_HEADS, GLA_DK))
    o_b = rmsnorm(o_b, gla_norm).reshape(B, S, GLA_WIDTH).astype(h.dtype)
    out_b = o_b * jax.nn.silu(br)
    out_c = stick_breaking_attention(
        cq.reshape(B, S, SB_HEADS, HEAD_DIM),
        ck.reshape(B, S, SB_HEADS, HEAD_DIM),
        cv.reshape(B, S, SB_HEADS, HEAD_DIM))
    out_c = rmsnorm(out_c, sb_out_norm)
    mixed = jnp.concatenate([out_a, out_b, out_c], axis=-1)
    return mixed @ w_out

def squared_relu_mlp(h, w1, w2):
    return jnp.square(jax.nn.relu(h @ w1)) @ w2

def second_inputs(seed: int = 0) -> dict:
    key = jax.random.key(seed)
    ks = jax.random.split(key, 15)
    f32 = jnp.float32

    def nrm(k, shape, scale):
        return jax.random.normal(k, shape, f32) * scale

    def gain(k, shape):
        return 1.0 + 0.05 * jax.random.normal(k, shape, f32)

    return {
        'x': nrm(ks[0], (BATCH, SEQ, D_MODEL), 1.0),
        'norm_mix': gain(ks[1], (DEPTH, D_MODEL)),
        'w_in': nrm(ks[2], (DEPTH, D_MODEL, PROJ_WIDTH), D_MODEL ** -0.5),
        'swa_sinks': nrm(ks[3], (DEPTH, SWA_HEADS), 0.5),
        'rel_bias': nrm(ks[4], (REL_BUCKETS, SWA_HEADS), 0.5),
        'gla_gate_w': nrm(ks[5], (DEPTH, GLA_LOWRANK, GLA_HEADS * GLA_DK), GLA_LOWRANK ** -0.5),
        'gla_gate_b': nrm(ks[6], (DEPTH, GLA_HEADS * GLA_DK), 0.1),
        'gla_norm': gain(ks[7], (DEPTH, GLA_DV)),
        'swa_out_norm': gain(ks[8], (DEPTH, SWA_WIDTH)),
        'sb_out_norm': gain(ks[9], (DEPTH, SB_WIDTH)),
        'w_out': nrm(ks[10], (DEPTH, MIX_WIDTH_2, D_MODEL), MIX_WIDTH_2 ** -0.5),
        'norm_mlp': gain(ks[11], (DEPTH, D_MODEL)),
        'w_mlp_in': nrm(ks[12], (DEPTH, D_MODEL, D_FF), D_MODEL ** -0.5),
        'w_mlp_out': nrm(ks[13], (DEPTH, D_FF, D_MODEL), D_FF ** -0.5),
        'norm_final': gain(ks[14], (D_MODEL,)),
    }

def second_block(x, norm_mix, w_in, swa_sinks, rel_bias, gla_gate_w, gla_gate_b, gla_norm,
              swa_out_norm, sb_out_norm, w_out, norm_mlp, w_mlp_in, w_mlp_out, norm_final):
    for l in range(DEPTH):
        h = rmsnorm(x, norm_mix[l])
        x = x + token_mixing(h, w_in[l], swa_sinks[l], rel_bias, gla_gate_w[l], gla_gate_b[l],
                             gla_norm[l], swa_out_norm[l], sb_out_norm[l], w_out[l])
        h = rmsnorm(x, norm_mlp[l])
        x = x + squared_relu_mlp(h, w_mlp_in[l], w_mlp_out[l])
    return rmsnorm(x, norm_final)


def setup_inputs(seed=0):
    out = dict(first_inputs(seed))
    for name, value in second_inputs(seed + 1).items():
        if name != "x":
            out[name + "_2"] = value
    return out


def reference(
    x, attn_norm_gain, w_in, forget_bias, fox_out_gain, dil_out_gain, w_out, ffn_norm_gain,
    peer_query, peer_sub_keys, peer_down, peer_up, final_norm_gain, norm_mix_2, w_in_2,
    swa_sinks_2, rel_bias_2, gla_gate_w_2, gla_gate_b_2, gla_norm_2, swa_out_norm_2,
    sb_out_norm_2, w_out_2, norm_mlp_2, w_mlp_in_2, w_mlp_out_2, norm_final_2,
):
    x = first_block(
        x, attn_norm_gain, w_in, forget_bias, fox_out_gain, dil_out_gain, w_out, ffn_norm_gain,
        peer_query, peer_sub_keys, peer_down, peer_up, final_norm_gain,
    )
    return second_block(
        x, norm_mix_2, w_in_2, swa_sinks_2, rel_bias_2, gla_gate_w_2, gla_gate_b_2, gla_norm_2,
        swa_out_norm_2, sb_out_norm_2, w_out_2, norm_mlp_2, w_mlp_in_2, w_mlp_out_2,
        norm_final_2,
    )


_drawn_inputs = setup_inputs


def setup_inputs(seed=0):
    import zlib

    import numpy as np

    out = dict(_drawn_inputs(seed))
    spreads = {}
    factors = {'fox_out_gain': 4.153,
     'dil_out_gain': 3.711,
     'ffn_norm_gain': 22.267,
     'swa_sinks_2': 8.0,
     'gla_gate_b_2': 3.729,
     'gla_norm_2': 10.525,
     'sb_out_norm_2': 8.475,
     'swa_out_norm_2': 4.149,
     'norm_mlp_2': 2.997}
    for name, (base, spread) in spreads.items():
        noise = np.random.default_rng([zlib.crc32(name.encode()), seed]).standard_normal(out[name].shape)
        drawn = base * np.exp(spread * noise) if base else spread * noise
        out[name] = __import__('jax').numpy.asarray(drawn.astype(out[name].dtype))
    for name, factor in factors.items():
        out[name] = (out[name] * factor).astype(out[name].dtype)
    return out
```

```python
from contextlib import ExitStack

import numpy as np

import concourse.bass as bass
from concourse import mybir

ALU = mybir.AluOpType
ACT = mybir.ActivationFunctionType
F32 = mybir.dt.float32
F32R = mybir.dt.float32r
BF16 = mybir.dt.bfloat16
U32 = mybir.dt.uint32
AX = mybir.AxisListType.X

P = 128
S = 256
NT = S // P
D = 2048
KT = D // P
HD = 64
EPS = 1e-6
NEG = -1e30

SUB = 8
RING = 4
WIDE = 512

IN1 = 6160
FQ, FK, FV, FG, DQ, DK, DV = 0, 1024, 2048, 3072, 3088, 4112, 5136
FOX_H = DIL_H = 16
IN2 = 5136
AQ, AK, AV, BQ, BK, BV, BR, BL, CQ, CK, CV = 0, 768, 1024, 1280, 1664, 2048, 2816, 3584, 3600, 4112, 4624
SWA_H, SWA_G = 12, 3
GLA_H, GLA_K, GLA_V, GLA_R = 4, 96, 192, 16
SB_H = 8

PH, TOPK, NKEY = 8, 16, 128
HALF_J = 64

N1, NB1 = 440, 14
N2, NB2 = 428, 12
ROUNDS_HALF, MLP_ROUNDS = 4, 4

C_IDENT, C_IOTA = 0, 128
K_UTRI, K_ONES, K_SUF, K_GTRI, K_GBLK, K_COS, K_SIN, K_HALF, K_MASK, K_COUNT, K_STRICT = (
    0, 128, 256, 384, 512, 640, 656, 672, 674, 1058, 1442)
K_COLS = 1570
TW = 383


def fixed_constants():
    out = np.zeros((P, 256), np.float32)
    out[:, C_IDENT:C_IDENT + P] = np.eye(P)
    out[:, C_IOTA:C_IOTA + P] = np.arange(P)
    return out


def attention_constants():
    i, j = np.arange(P)[:, None], np.arange(P)[None, :]
    out = np.zeros((P, K_COLS), np.float32)
    out[:, K_UTRI:K_UTRI + P] = i <= j
    out[:, K_ONES:K_ONES + P] = 1
    out[:, K_SUF:K_SUF + P] = i > j
    same = i // 64 == j // 64
    out[:, K_GTRI:K_GTRI + P] = same & (i <= j)
    out[:, K_GBLK:K_GBLK + P] = same
    inv = (np.float32(500000.0) ** (-np.arange(0, 16, 2, dtype=np.float32) / np.float32(16))).astype(np.float32)
    for t in range(NT):
        ang = (np.arange(P, dtype=np.float32)[:, None] + t * P) * inv[None]
        out[:, K_COS + 8 * t:K_COS + 8 * t + 8] = np.cos(ang)
        out[:, K_SIN + 8 * t:K_SIN + 8 * t + 8] = np.sin(ang)
    out[:64, K_HALF] = 1
    out[64:, K_HALF + 1] = 1
    for n, (qt, kt) in enumerate(((0, 0), (1, 0), (1, 1))):
        q, k = qt * P + i, kt * P + j
        dist = q - k
        count = (dist >= 0) * ((dist <= 128) * 1.0 + (dist % 4 == 0) + (dist % 16 == 0))
        out[:, K_MASK + n * P:K_MASK + n * P + P] = np.where(count > 0, 0, NEG)
        out[:, K_COUNT + n * P:K_COUNT + n * P + P] = count
    out[:, K_STRICT:K_STRICT + P] = i < j
    return out


def bucket_constants():
    out = np.zeros((33, TW + 1), np.float32)
    for x in range(TW):
        dist = 255 - x
        if not 0 <= dist < 128:
            out[32, x] = NEG
            continue
        if dist < 16:
            b = dist
        else:
            ratio = np.float32(np.log(np.float32(dist) / np.float32(16))) / np.float32(np.log(8.0))
            b = min(16 + int(np.float32(ratio * np.float32(16))), 31)
        out[b, x] = 1
    return out


def build(nc, a, out):
    ctx = ExitStack()
    with ctx:
        def sb(name, shape, dt=F32, stack=ctx):
            return stack.enter_context(nc.sbuf_tensor(name, shape, dt))

        def sem(name):
            return ctx.enter_context(nc.semaphore(name))

        raw = sb("raw", [P, RING, 2 * WIDE])
        w_hi = sb("w_hi", [P, RING, 2 * WIDE], F32R)
        w_lo = sb("w_lo", [P, RING, 2 * WIDE], F32R)
        h = sb("h", [P, NT, D])
        fix = sb("fix", [P, 256])
        ident_b = sb("ident_b", [P, P], BF16)
        stats = sb("stats", [P, 4, 16])
        big = sb("big", [P, 18464])
        proj1 = big[:, 0:NT * IN1].rearrange("p (t n) -> p t n", t=NT)
        proj2 = big[:, 0:NT * IN2].rearrange("p (t n) -> p t n", t=NT)
        mix = big[:, 12320:16416].rearrange("p (t n) -> p t n", t=NT)
        gain = big[:, 16416:18464]
        last_gain = big[:, 0:D]
        pq = big[:, 0:4096].rearrange("p (t n) -> p t n", t=NT)
        pqT = big[:, 4096:8192].rearrange("p (g s) -> p g s", g=16)
        skT = big[:, 8192:10240].rearrange("p (g n) -> p g n", g=16)
        sc = big[:, 10240:14336].rearrange("p (t g n) -> p t g n", t=NT, g=16)
        cand = big[:, 14336:16384]
        top_v = big[:, 0:512].rearrange("p (t g k) -> p t g k", t=NT, g=16)
        top_i = big[:, 512:1024].rearrange("p (t g k) -> p t g k", t=NT, g=16)
        top_f = big[:, 1024:1536].rearrange("p (t g k) -> p t g k", t=NT, g=16)
        best_v = big[:, 1536:1792].rearrange("p (t g k) -> p t g k", t=NT, g=PH)
        best_c = big[:, 1792:2048].rearrange("p (t g k) -> p t g k", t=NT, g=PH)
        rank = big[:, 2048:2560].rearrange("p (s t n) -> p s t n", s=2, t=NT)
        ranku = big[:, 2560:2816]
        chosen = big[:, 2816:3584].rearrange("p (s t n) -> p s t n", s=3, t=NT)
        gsum = big[:, 3584:3616].rearrange("p (s n) -> p s n", s=2)
        scr = big[:, 3616:3872]
        chosenT = big[:, 16416:17184].rearrange("p (s n) -> p s n", s=3)
        gates = big[:, 0:S * HALF_J].rearrange("p (s j) -> p j s", j=HALF_J)
        gates_w = big[:, 0:S * HALF_J]
        hid = big[:, 17184:18208].rearrange("p (t n) -> p t n", t=NT)

        with ExitStack() as part:
            x_hi = sb("x_hi", [P, KT, S], F32R, part)
            x_lo = sb("x_lo", [P, KT, S], F32R, part)
            a_hi = sb("a_hi", [P, KT, S], F32R, part)
            a_lo = sb("a_lo", [P, KT, S], F32R, part)
        with ExitStack() as part:
            sb("beside", [P, 2 * KT * S], F32, part)
            one1 = sb("one1", [P, 2, 8, P], F32, part)
            is2 = sb("is2", [P, 2, 8, HALF_J], F32, part)
            one2 = sb("one2", [P, 2, 8, HALF_J], F32, part)
        with ExitStack() as part:
            qkT = sb("qkT", [HD, 2, 2 * S], F32, part)
            prob = sb("prob", [P, 2, 3 * P], F32, part)
            probT = sb("probT", [P, 2, 3 * P], F32, part)
            hs = sb("hs", [P, 4, 5, 2], F32, part)
            fg = sb("fg", [P, 4, 2, 16], F32, part)
            cumT = sb("cumT", [16, 2, S], F32, part)
            rope = sb("rope", [P, 4, 32, 8], F32, part)
            biased = sb("biased", [P, 2, 3 * P], F32, part)
            g_log = sb("g_log", [P, NT, 384], F32, part)
            g_tmp = sb("g_tmp", [P, 384], F32, part)
            q_dec = sb("q_dec", [P, NT, 384], F32, part)
            k_inv = sb("k_inv", [P, NT, 384], F32, part)
        with ExitStack() as part:
            sb("beside_x", [P, 2 * KT * S], F32, part)
            kc = sb("kc", [P, K_COLS], F32, part)
            mask_b = sb("mask_b", [P, 3 * P], BF16, part)
            fbias = sb("fbias", [P, 16], F32, part)
            sinks = sb("sinks", [P, SWA_H], F32, part)
            buck = sb("buck", [33, TW + 1], F32, part)
            rel = sb("rel", [33, SWA_H], F32, part)
            relrow = sb("relrow", [SWA_H, TW + 1], F32, part)
            gw = sb("gw", [33, 384], F32, part)
            blT = sb("blT", [33, S], F32, part)
            k_end = sb("k_end", [P, NT, 2, 384], F32, part)
            with ExitStack() as swa:
                bias_t = sb("bias_t", [P, SWA_H, S], F32, swa)
            g_dec = sb("g_dec", [GLA_K, 4], F32, part)
            qdT = sb("qdT", [GLA_K, 4, P], F32, part)
            state = sb("state", [GLA_K, 4, GLA_V], F32, part)
            g_sc = sb("g_sc", [P, P], F32, part)
            sbw = sb("sbw", [P, 4, 3 * P], F32, part)
        with ExitStack() as part:
            sb("beside_qk", [P, 1024], F32, part)
            sbz = sb("sbz", [P, 4, 3 * P], F32, part)
            sbt = sb("sbt", [P, 4, 3 * P], F32, part)
            sbb = sb("sbb", [P, 4, 3 * P], F32, part)
            sb1 = sb("sb1", [P, 4, 3 * P], F32, part)

        ps = ctx.enter_context(nc.psum_tensor("ps", [P, 8, 512], F32))
        ps_flat = ps[:].rearrange("p b n -> p (b n)")
        rel_rows = nc.dram_tensor("rel_rows", (SWA_H, P, TW + 1), F32, kind="Internal").ap()

        ident = fix[:, C_IDENT:C_IDENT + P]
        iota = fix[:, C_IOTA:C_IOTA + P]

        def KC(at, n=P):
            return kc[:, at:at + n]

        raw_loaded = [sem(f"raw_loaded{i}") for i in range(RING)]
        hi_made, lo_made, chunk_used = sem("hi_made"), sem("lo_made"), sem("chunk_used")
        copied_out, added_out = sem("copied_out"), sem("added_out")
        hid_turned, hid_full = sem("hid_turned"), sem("hid_full")
        hid_hi, hid_lo = sem("hid_hi"), sem("hid_lo")
        fix_loaded, kc_loaded, x_loaded = sem("fix_loaded"), sem("kc_loaded"), sem("x_loaded")
        gain_loaded, small_loaded, stats_set = sem("gain_loaded"), sem("small_loaded"), sem("stats_set")
        rows_stored, bias_loaded = sem("rows_stored"), sem("bias_loaded")
        squared, var_made, rooted, normed = sem("squared"), sem("var_made"), sem("rooted"), sem("normed")
        x_turned, x_hi_made, x_lo_made = sem("x_turned"), sem("x_hi_made"), sem("x_lo_made")
        qk_turned, qk_copied, scored = sem("qk_turned"), sem("qk_copied"), sem("scored")
        max_made, exp_made, counted = sem("max_made"), sem("exp_made"), sem("counted")
        p_turned, p_copied, pv_made, head_out = sem("p_turned"), sem("p_copied"), sem("pv_made"), sem("head_out")
        gate_abs, gate_soft, gate_log = sem("gate_abs"), sem("gate_soft"), sem("gate_log")
        cum_made, cum_copied, roped = sem("cum_made"), sem("cum_copied"), sem("roped")
        act_step, dve_step, pool_step = sem("act_step"), sem("dve_step"), sem("pool_step")
        masks_made, rel_ready, rel_made, row_copied = sem("masks_made"), sem("rel_ready"), sem("rel_made"), sem("row_copied")
        pq_turned, pq_copied, sc_made, sc_copied = sem("pq_turned"), sem("pq_copied"), sem("sc_made"), sem("sc_copied")
        gate_diff, gate_exp, chosen_made = sem("gate_diff"), sem("gate_exp"), sem("chosen_made")
        ch_turned, ch_copied = sem("ch_turned"), sem("ch_copied")
        one1_made, is2_made, one2_made, g_summed, g_copied = sem("one1_made"), sem("is2_made"), sem("one2_made"), sem("g_summed"), sem("g_copied")
        bl_turned, bl_copied, gpre_made = sem("bl_turned"), sem("bl_copied"), sem("gpre_made")
        gla_abs, gla_soft, gla_log = sem("gla_abs"), sem("gla_soft"), sem("gla_log")
        gla_sum, gla_exp, gla_ops = sem("gla_sum"), sem("gla_exp"), sem("gla_ops")
        gla_dec, gla_decexp = sem("gla_dec"), sem("gla_decexp")
        gt_made, gt_copied, gs_made, gs_masked = sem("gt_made"), sem("gt_copied"), sem("gs_made"), sem("gs_masked")
        gd_made, state_made, go_made, go_copied = sem("gd_made"), sem("state_made"), sem("go_made"), sem("go_copied")
        sb_abs, sb_soft, sb_log, sb_sum = sem("sb_abs"), sem("sb_soft"), sem("sb_log"), sem("sb_sum")
        sb_add, sb_exp, sb_w = sem("sb_add"), sem("sb_exp"), sem("sb_w")
        br_exp, mixed2 = sem("br_exp"), sem("mixed2")
        out_stored = sem("out_stored")

        sections = {}
        blocks = acts = adds = 0
        for name, nb, kind in (("in1", NB1, "act"), ("out1", 4, "add"), ("query", 4, "act"),
                               ("peer0", 8 * ROUNDS_HALF, "both"), ("peer1", 8 * ROUNDS_HALF, "both"),
                               ("in2", NB2, "act"), ("out2", 4, "add"), ("mlp", 8 * MLP_ROUNDS, "both")):
            sections[name] = (blocks, acts, adds, nb)
            blocks += nb
            acts += {"act": nb, "add": 0, "both": nb // 2}[kind]
            adds += {"act": 0, "add": nb, "both": nb // 2}[kind]
        all_blocks, all_acts, all_adds = blocks, acts, adds

        def after(name):
            b, x, y, nb = sections[name]
            kind = {"in1": (1, 0), "query": (1, 0), "in2": (1, 0), "out1": (0, 1), "out2": (0, 1)}.get(name, (.5, .5))
            return b + nb, x + int(nb * kind[0]), y + int(nb * kind[1])

        def bank(parity, t):
            return 2 * parity + t

        def over_blocks(eng, nb, block):
            block(0, 0)
            block(1, 1)
            if nb == 4:
                block(2, 0)
                block(3, 1)
            else:
                with eng.Fori(0, nb // 2 - 1) as i:
                    block(2 * i + 2, 0)
                    block(2 * i + 3, 1)

        def static(v):
            return isinstance(v, int)

        whole = [(0, D)]
        mix1_segs = [(0, 1024), (1024, 1024)]
        mix2_segs = [(0, 768)] + [(768 + GLA_V * i, GLA_V) for i in range(GLA_H)] + [(1536, 512)]
        norms = [(h, mix, whole), (mix, mix, mix1_segs), (h, mix, whole), (h, h, whole),
                 (h, mix, whole), (mix, mix, mix2_segs), (h, mix, whole), (h, h, whole)]

        block = ctx.enter_context(nc.Block())

        @block.sync
        def _(sp):
            def load(B, c, src):
                q = SUB * B + c
                if not static(q) or q >= RING:
                    sp.wait_ge(lo_made, q - RING + 1)
                n = src.shape[1] * src.shape[2]
                sp.dma_start(raw[:, c % RING, 0:n], src.rearrange("p k n -> p (k n)")).then_inc(raw_loaded[c % RING], 16)

            def gemm(name, w):
                b0, _, _, nb = sections[name]

                def blk(b, parity):
                    for c in range(SUB):
                        load(b0 + b, c, w[b, c])
                over_blocks(sp, nb, blk)

            def rounds(name, first_round, count, w_in, w_out):
                b0 = sections[name][0]

                def one(r):
                    for i in range(8):
                        for c in range(SUB):
                            w = w_in if i < 4 else w_out
                            load(b0 + 8 * r + i, c, w[4 * (first_round + r) + i % 4, c])
                one(0)
                with sp.Fori(1, count) as r:
                    one(r)

            gemm("in1", a["w_in"])
            gemm("out1", a["w_out"])
            gemm("query", a["peer_query"])
            rounds("peer0", 0, ROUNDS_HALF, a["peer_down"], a["peer_up"])
            rounds("peer1", ROUNDS_HALF, ROUNDS_HALF, a["peer_down"], a["peer_up"])
            gemm("in2", a["w_in_2"])
            gemm("out2", a["w_out_2"])
            rounds("mlp", 0, MLP_ROUNDS, a["w_mlp_in_2"], a["w_mlp_out_2"])
            sp.wait_ge(normed, NT * len(norms))
            sp.dma_start(out[0].rearrange("(t p) d -> p t d", p=P), h[:]).then_inc(out_stored, 16)
            sp.wait_ge(out_stored, 16)

        @block.gpsimd
        def _(pool):
            steps = [0]

            def step(ins):
                steps[0] += 1
                ins.then_inc(pool_step, 1)
                pool.wait_ge(pool_step, steps[0])

            def spread(dst, row):
                return pool.dma_start(dst, row.partition_broadcast(P))

            pool.dma_start(fix[:], a["fix"]).then_inc(fix_loaded, 16)
            pool.dma_start(h[:], a["x"][0].rearrange("(t p) d -> p t d", p=P)).then_inc(x_loaded, 16)
            spread(gain, a["attn_norm_gain"][0]).then_inc(gain_loaded, 16)
            pool.dma_start(kc[:], a["kc"]).then_inc(kc_loaded, 16)
            spread(fbias[:], a["forget_bias"][0]).then_inc(small_loaded, 16)
            pool.wait_ge(normed, NT * 1)
            spread(gain[:, 0:1024], a["fox_out_gain"][0]).then_inc(gain_loaded, 16)
            spread(gain[:, 1024:2048], a["dil_out_gain"][0]).then_inc(gain_loaded, 16)
            pool.wait_ge(normed, NT * 2)
            spread(gain, a["ffn_norm_gain"][0]).then_inc(gain_loaded, 16)
            pool.wait_ge(chunk_used, SUB * after("query")[0])
            pool.dma_start(skT, a["peer_sub_keys"]).then_inc(small_loaded, 16)

            for half in range(2):
                base = 32 * half

                def batch(n, slot, half=half, base=base):
                    pool.wait_ge(is2_made, base + n + 1)
                    at = bass.ds(8 * n, 8)
                    nc.gpsimd.tensor_tensor(
                        one2[:, slot], is2[:, slot],
                        chosenT[:, 2, at].unsqueeze(2).to_broadcast([P, 8, HALF_J]), ALU.mult).then_inc(one2_made, 1)
                batch(0, 0)
                batch(1, 1)
                with pool.Fori(0, 15) as i:
                    batch(2 * i + 2, 0)
                    batch(2 * i + 3, 1)
            pool.wait_ge(added_out, after("peer1")[2])
            spread(gain, a["final_norm_gain"]).then_inc(gain_loaded, 16)
            pool.wait_ge(normed, NT * 4)
            spread(gain, a["norm_mix_2"][0]).then_inc(gain_loaded, 16)
            step(nc.gpsimd.memset(gw[:], 0.0))
            step(nc.gpsimd.memset(blT[:], 0.0))
            step(nc.gpsimd.memset(blT[32:33, :], 1.0))
            nc.gpsimd.memset(rel[32:33, :], 1.0).then_inc(rel_ready, 1)
            pool.dma_start(kc[:], a["kc"]).then_inc(kc_loaded, 16)
            pool.dma_start(rel[0:32, :], a["rel_bias_2"]).then_inc(small_loaded, 16)
            pool.dma_start(buck[:], a["buck"]).then_inc(small_loaded, 16)
            pool.dma_start(gw[0:GLA_R, :], a["gla_gate_w_2"][0]).then_inc(small_loaded, 16)
            pool.dma_start(gw[32:33, :], a["gla_gate_b_2"]).then_inc(small_loaded, 16)
            spread(sinks[:], a["swa_sinks_2"][0]).then_inc(small_loaded, 16)
            pool.wait_ge(row_copied, 1)
            for p in range(4):
                pool.dma_start(rel_rows[:, 32 * p:32 * p + 32, :],
                               relrow[:].unsqueeze(1).to_broadcast([SWA_H, 32, TW + 1])).then_inc(rows_stored, 16)
            pool.wait_ge(rows_stored, 64)
            sheared = rel_rows.rearrange("h q x -> h (q x)")[:, 127:127 + P * TW]
            sheared = sheared.rearrange("h (q x) -> q h x", x=TW)[:, :, 0:S]
            pool.dma_start(bias_t[:], sheared).then_inc(bias_loaded, 16)

            pool.wait_ge(normed, NT * 5)
            spread(gain[:, 0:768], a["swa_out_norm_2"][0]).then_inc(gain_loaded, 16)
            for i in range(GLA_H):
                spread(gain[:, 768 + GLA_V * i:768 + GLA_V * (i + 1)], a["gla_norm_2"][0]).then_inc(gain_loaded, 16)
            spread(gain[:, 1536:2048], a["sb_out_norm_2"][0]).then_inc(gain_loaded, 16)
            pool.wait_ge(normed, NT * 6)
            spread(gain, a["norm_mlp_2"][0]).then_inc(gain_loaded, 16)
            pool.wait_ge(normed, NT * 7)
            spread(last_gain, a["norm_final_2"]).then_inc(gain_loaded, 16)

        def split_hi(act, B, c, n):
            q = SUB * B + c
            act.wait_ge(raw_loaded[c % RING], 16 * (2 * B + c // RING + 1))
            if not static(q) or q >= RING:
                act.wait_ge(chunk_used, q - RING + 1)
            act.activation(w_hi[:, c % RING, 0:2 * n], raw[:, c % RING, 0:2 * n], ACT.Copy).then_inc(hi_made, 1)

        def split_lo(dve, B, c, n):
            q = SUB * B + c
            dve.wait_ge(hi_made, q + 1)
            nc.vector.tensor_tensor(w_lo[:, c % RING, 0:2 * n], raw[:, c % RING, 0:2 * n],
                                    w_hi[:, c % RING, 0:2 * n].bitcast(F32), ALU.subtract).then_inc(lo_made, 1)

        @block.scalar
        def _(act):
            steps = [0]

            def step(ins):
                steps[0] += 1
                ins.then_inc(act_step, 1)
                act.wait_ge(act_step, steps[0])

            def norm(k):
                src, _, segs = norms[k]
                if k in (0,):
                    act.wait_ge(x_loaded, 16)
                if k in (1,):
                    act.wait_ge(head_out, FOX_H + DIL_H)
                if k in (2, 3, 6, 7):
                    act.wait_ge(added_out, after({2: "out1", 3: "peer1", 6: "out2", 7: "mlp"}[k])[2])
                if k == 4:
                    act.wait_ge(normed, NT * 4)
                if k == 5:
                    act.wait_ge(head_out, FOX_H + DIL_H + SWA_H + SB_H)
                    act.wait_ge(go_copied, GLA_H * NT)
                last = None
                for t in range(NT):
                    for n, (at, w) in enumerate(segs):
                        last = act.activation(ps_flat[:, t * D + at:t * D + at + w], src[:, t, at:at + w],
                                              ACT.Square, accum_out=stats[:, 0, t * 8 + n:t * 8 + n + 1])
                last.then_inc(squared, 1)
                act.wait_ge(var_made, k + 1)
                act.activation(stats[:, 2, :], stats[:, 1, :], ACT.Sqrt).then_inc(rooted, 1)

            def turn_hi(k):
                for g in range(8):
                    act.wait_ge(x_turned, 8 * k + g + 1)
                    act.activation(x_hi[:, 2 * g:2 * g + 2, :].rearrange("p k s -> p (k s)"), ps[:, 4 + g % 2, :],
                                   ACT.Copy).then_inc(x_hi_made, 1)

            def drain(B, parity, n, dst):
                act.wait_ge(chunk_used, SUB * (B + 1))
                for t in range(NT):
                    last = act.activation(dst(t), ps[:, bank(parity, t), 0:n], ACT.Copy)
                last.then_inc(copied_out, 1)

            def gemm(name, n, dst):
                b0, _, _, nb = sections[name]

                def place(b):
                    return lambda t: dst[:, t, bass.ds(b * n, n)]

                def blk(b, parity):
                    for c in range(SUB):
                        if c == 3 and dst is not None and not (static(b) and b == 0):
                            drain(b0 + b - 1, 1 - parity, n, place(b - 1))
                        split_hi(act, b0 + b, c, n)
                over_blocks(act, nb, blk)
                if dst is not None:
                    drain(b0 + nb - 1, 1, n, place(nb - 1))

            def rounds(name, h0, count, func):
                b0 = sections[name][0]

                def one(r):
                    for i in range(8):
                        B = b0 + 8 * r + i
                        for c in range(SUB):
                            if c == 3 and 1 <= i <= 4:
                                act.wait_ge(chunk_used, SUB * B)
                                before = h0 + 4 * r + i - 1
                                if not static(before) or before > 0:
                                    act.wait_ge(hid_turned, before)
                                for t in range(NT):
                                    last = act.activation(hid[:, t], ps[:, bank((i - 1) % 2, t), :], func)
                                last.then_inc(copied_out, 1)
                            split_hi(act, B, c, WIDE)
                            if c == 4 and 2 <= i <= 4:
                                split_hidden(r, i - 2)
                            if c == 7 and i == 4:
                                split_hidden(r, 3)

                def split_hidden(r, i):
                    pair = ps[:, 4 + 2 * (i % 2):6 + 2 * (i % 2), :].rearrange("p b n -> p (b n)")
                    if func == ACT.Relu:
                        act.wait_ge(hid_turned, h0 + 4 * r + i + 1)
                        act.activation(pair, pair, ACT.Square).then_inc(hid_full, 1)
                    act.wait_ge(hid_full, h0 + 4 * r + i + 1)
                    act.activation(a_hi[:, 4 * i:4 * i + 4, :].rearrange("p k s -> p (k s)"), pair,
                                   ACT.Copy).then_inc(hid_hi, 1)
                one(0)
                with act.Fori(1, count) as r:
                    one(r)

            def copy_qk(i):
                act.wait_ge(qk_turned, i + 1)
                if i >= 2:
                    act.wait_ge(scored, i - 1)
                act.activation(qkT[:, i % 2, :], ps[0:HD, 6 + i % 2, :], ACT.Copy).then_inc(qk_copied, 1)

            def exp_head(i, sink=None):
                act.wait_ge(max_made, i + 1)
                if i >= 2:
                    act.wait_ge(p_turned, i - 1)
                s = hs[:, i % 4]
                src, scale = (ps[:, 4 + i % 2], HD ** -0.5) if sink is None else (biased[:, i % 2], 1.0)
                act.activation(prob[:, i % 2, 0:P], src[:, 0:P], ACT.Exp, bias=s[:, 1, 0:1],
                               scale=scale, accum_out=s[:, 2, 0:1])
                last = act.activation(prob[:, i % 2, P:3 * P], src[:, P:3 * P], ACT.Exp, bias=s[:, 1, 1:2],
                                      scale=scale, accum_out=s[:, 2, 1:2])
                if sink is not None:
                    last = act.activation(s[:, 4, :], s[:, 1, :], ACT.Exp, bias=sink)
                last.then_inc(exp_made, 1)

            act.wait_ge(fix_loaded, 16)
            act.activation(ident_b[:], ident, ACT.Copy).then_inc(masks_made, 1)
            act.wait_ge(stats_set, 1)
            norm(0)
            turn_hi(0)
            gemm("in1", N1, proj1)
            act.wait_ge(gate_abs, 1)
            step(act.activation(fg[:, 2], fg[:, 1], ACT.Exp, scale=-1.0))
            act.activation(fg[:, 3], fg[:, 2], ACT.Ln, bias=1.0).then_inc(gate_soft, 1)
            act.wait_ge(cum_made, 1)
            act.activation(cumT[:, 0, :], ps[0:16, 0, 0:S], ACT.Copy, scale=8.0)
            act.activation(cumT[:, 1, :], ps[0:16, 0, 0:S], ACT.Copy, scale=-8.0).then_inc(cum_copied, 1)
            for n in range(FOX_H + DIL_H + 1):
                if n < FOX_H + DIL_H:
                    copy_qk(n)
                if n >= 1:
                    exp_head(n - 1)
            norm(1)
            turn_hi(1)
            gemm("out1", WIDE, None)
            norm(2)
            turn_hi(2)
            gemm("query", WIDE, pq)

            for g in range(8):
                act.wait_ge(pq_turned, g + 1)
                act.activation(pqT[:, 2 * g:2 * g + 2, :].rearrange("p k s -> p (k s)"), ps[:, 4 + g % 2, :],
                               ACT.Copy).then_inc(pq_copied, 1)
            for n in range(8):
                t, g = n // 4, n % 4
                act.wait_ge(sc_made, n + 1)
                act.activation(sc[:, t, 4 * g:4 * g + 4, :].rearrange("p g n -> p (g n)"), ps[:, 6 + n % 2, :],
                               ACT.Copy).then_inc(sc_copied, 1)
            act.wait_ge(gate_diff, 1)
            act.activation(big[:, 1536:1792], big[:, 1536:1792], ACT.Exp).then_inc(gate_exp, 1)
            for s in range(3):
                act.wait_ge(ch_turned, s + 1)
                act.activation(chosenT[:, s, :], ps[:, s, 0:S], ACT.Copy).then_inc(ch_copied, 1)

            for half in range(2):
                base = 32 * half

                def batch(n, slot, base=base, half=half):
                    act.wait_ge(g_summed, base + n + 1)
                    act.activation(gates_w[:, bass.ds(8 * HALF_J * n, 8 * HALF_J)], ps[:, 6 + slot, :],
                                   ACT.Copy).then_inc(g_copied, 1)
                if half:
                    act.wait_ge(hid_full, 4 * ROUNDS_HALF)
                with act.Fori(0, 16) as i:
                    batch(2 * i, 0)
                    batch(2 * i + 1, 1)
                rounds(f"peer{half}", 4 * ROUNDS_HALF * half, ROUNDS_HALF, ACT.Gelu_apprx_tanh)
            norm(3)

            act.wait_ge(rel_made, 1)
            act.activation(relrow[:], ps[0:SWA_H, 0, 0:TW + 1], ACT.Copy).then_inc(row_copied, 1)
            act.wait_ge(row_copied, 1)
            norm(4)
            turn_hi(3)
            gemm("in2", N2, proj2)
            for n in range(FOX_H + DIL_H, FOX_H + DIL_H + SWA_H + 1):
                if n < FOX_H + DIL_H + SWA_H:
                    copy_qk(n)
                if n > FOX_H + DIL_H:
                    i = n - 1 - FOX_H - DIL_H
                    exp_head(n - 1, sinks[:, i:i + 1])
            act.wait_ge(bl_turned, 1)
            act.wait_ge(pool_step, 3)
            act.activation(blT[0:GLA_R, :], ps[0:GLA_R, 0, 0:S], ACT.Copy).then_inc(bl_copied, 1)
            for t in range(NT):
                act.wait_ge(gla_abs, t + 1)
                step(act.activation(k_inv[:, t], g_log[:, t], ACT.Exp, scale=-1.0))
                act.activation(q_dec[:, t], k_inv[:, t], ACT.Ln, bias=1.0).then_inc(gla_soft, 1)
            for t in range(NT):
                act.wait_ge(gla_sum, t + 1)
                act.activation(q_dec[:, t], ps[:, 0, 0:384], ACT.Exp)
                act.activation(k_inv[:, t], ps[:, 0, 0:384], ACT.Exp, scale=-1.0).then_inc(gla_exp, 1)
                act.wait_ge(gla_ops, 2 * t + 1)
                act.activation(k_end[:, t, 1], k_end[:, t, 0], ACT.Exp).then_inc(gla_exp, 1)
            for hh in range(GLA_H):
                act.wait_ge(gla_dec, hh + 1)
                act.activation(g_dec[:], ps[0:GLA_K, 0, 0:4], ACT.Exp).then_inc(gla_decexp, 1)
                for t in range(NT):
                    n = NT * hh + t
                    act.wait_ge(gt_made, n + 1)
                    act.activation(qdT[:, 2:4, :].rearrange("p a s -> p (a s)"), ps[0:GLA_K, 1, 0:S], ACT.Copy).then_inc(gt_copied, 1)
                    act.wait_ge(go_made, n + 1)
                    act.activation(mix[:, t, 768 + GLA_V * hh:768 + GLA_V * (hh + 1)], ps[:, 4, 0:GLA_V],
                                   ACT.Copy).then_inc(go_copied, 1)
            first = FOX_H + DIL_H + SWA_H
            for n in range(SB_H + 4):
                if n < SB_H:
                    copy_qk(first + n)
                if 1 <= n <= SB_H:
                    i = n - 1
                    act.wait_ge(sb_abs, i + 1)
                    step(act.activation(sbt[:, i % 4], sbt[:, i % 4], ACT.Exp, scale=-1.0))
                    act.activation(sbt[:, i % 4], sbt[:, i % 4], ACT.Ln, bias=1.0).then_inc(sb_soft, 1)
                if 3 <= n <= SB_H + 2:
                    i = n - 3
                    act.wait_ge(sb_add, i + 1)
                    act.activation(sbw[:, i % 4], sbb[:, i % 4], ACT.Exp).then_inc(sb_exp, 1)
            norm(5)
            for t in range(NT):
                act.activation(proj2[:, t, BQ:BQ + 768], proj2[:, t, BR:BR + 768], ACT.Exp, scale=-1.0).then_inc(br_exp, 1)
            turn_hi(4)
            gemm("out2", WIDE, None)
            norm(6)
            turn_hi(5)
            rounds("mlp", 8 * ROUNDS_HALF, MLP_ROUNDS, ACT.Relu)
            norm(7)

        @block.vector
        def _(dve):
            V = nc.vector
            steps = [0]

            def step(ins):
                steps[0] += 1
                ins.then_inc(dve_step, 1)
                dve.wait_ge(dve_step, steps[0])

            gains_due = [16, 48, 64, 80, 96, 192, 208, 224]

            def norm(k):
                src, dst, segs = norms[k]
                dve.wait_ge(squared, k + 1)
                if len(segs) == 1:
                    V.tensor_scalar(stats[:, 1, :], stats[:, 0, :], 1.0 / D, EPS, ALU.mult, ALU.add).then_inc(var_made, 1)
                elif len(segs) == 2:
                    V.tensor_scalar(stats[:, 1, :], stats[:, 0, :], 1.0 / 1024, EPS, ALU.mult, ALU.add).then_inc(var_made, 1)
                else:
                    var, ssq = (stats[:, n].rearrange("p (t n) -> p t n", t=NT) for n in (1, 0))
                    V.tensor_scalar(var[:, :, 0:1], ssq[:, :, 0:1], 1.0 / 768, EPS, ALU.mult, ALU.add)
                    V.tensor_scalar(var[:, :, 5:6], ssq[:, :, 5:6], 1.0 / 512, EPS, ALU.mult, ALU.add)
                    V.tensor_scalar(var[:, :, 1:5], ssq[:, :, 1:5], 1.0 / GLA_V, EPS, ALU.mult, ALU.add).then_inc(var_made, 1)
                dve.wait_ge(rooted, k + 1)
                step(V.reciprocal(stats[:, 3, :], stats[:, 2, :]))
                dve.wait_ge(gain_loaded, gains_due[k])
                for t in range(NT):
                    for n, (at, w) in enumerate(segs):
                        last = V.scalar_tensor_tensor(out=dst[:, t, at:at + w], in0=src[:, t, at:at + w],
                                                      scalar=stats[:, 3, t * 8 + n:t * 8 + n + 1],
                                                      in1=(last_gain if k == 7 else gain)[:, at:at + w], op0=ALU.mult, op1=ALU.mult)
                    last.then_inc(normed, 1)
                dve.wait_ge(normed, NT * (k + 1))

            def turn_lo(k):
                for g in range(8):
                    dve.wait_ge(x_hi_made, 8 * k + g + 1)
                    V.tensor_tensor(x_lo[:, 2 * g:2 * g + 2, :].rearrange("p k s -> p (k s)"), ps[:, 4 + g % 2, :],
                                    x_hi[:, 2 * g:2 * g + 2, :].rearrange("p k s -> p (k s)").bitcast(F32),
                                    ALU.subtract).then_inc(x_lo_made, 1)

            def add_block(B, parity, at):
                dve.wait_ge(chunk_used, SUB * (B + 1))
                for t in range(NT):
                    last = V.tensor_tensor(h[:, t, at * WIDE:(at + 1) * WIDE], ps[:, bank(parity, t), :],
                                           h[:, t, at * WIDE:(at + 1) * WIDE], ALU.add)
                last.then_inc(added_out, 1)

            def gemm(name, n, adds):
                b0, _, _, nb = sections[name]

                def blk(b, parity):
                    for c in range(SUB):
                        if c == 3 and adds and b > 0:
                            add_block(b0 + b - 1, 1 - parity, b - 1)
                        split_lo(dve, b0 + b, c, n)
                over_blocks(dve, nb, blk)
                if adds:
                    add_block(b0 + nb - 1, 1, nb - 1)

            def rounds(name, h0, count, table):
                b0 = sections[name][0]

                def fill(r, i):
                    if not table:
                        return
                    dve.wait_ge(hid_turned, h0 + 4 * r + i + 1)
                    pair = ps[:, 4 + 2 * (i % 2):6 + 2 * (i % 2), :].rearrange("p b (k s) -> p (b k) s", s=S)
                    V.tensor_tensor(pair, pair, gates[:, bass.ds(16 * r + 4 * i, 4), :], ALU.mult).then_inc(hid_full, 1)

                def rest(r, i):
                    dve.wait_ge(hid_hi, h0 + 4 * r + i + 1)
                    pair = ps[:, 4 + 2 * (i % 2):6 + 2 * (i % 2), :].rearrange("p b n -> p (b n)")
                    V.tensor_tensor(a_lo[:, 4 * i:4 * i + 4, :].rearrange("p k s -> p (k s)"), pair,
                                    a_hi[:, 4 * i:4 * i + 4, :].rearrange("p k s -> p (k s)").bitcast(F32),
                                    ALU.subtract).then_inc(hid_lo, 1)

                def one(r, first):
                    for i in range(8):
                        B = b0 + 8 * r + i
                        for c in range(SUB):
                            if c == 3 and (i >= 5 or (i == 0 and not first)):
                                add_block(B - 1, (i - 1) % 2, (i - 5) % 4 if i else 3)
                            if c == 7 and i == 4:
                                fill(r, 3)
                            split_lo(dve, B, c, WIDE)
                            if c == 3 and 2 <= i <= 4:
                                fill(r, i - 2)
                            if c == 4 and 2 <= i <= 4:
                                rest(r, i - 2)
                            if c == 7 and i == 4:
                                rest(r, 3)
                one(0, True)
                with dve.Fori(1, count) as r:
                    one(r, False)
                add_block(b0 + 8 * count - 1, 1, 3)

            def max_head(i):
                dve.wait_ge(scored, i + 1)
                if i >= 4:
                    dve.wait_ge(head_out, i - 3)
                s, src = hs[:, i % 4], ps[:, 4 + i % 2]
                V.reduce_max(s[:, 0, 0:1], src[:, 0:P], AX)
                step(V.reduce_max(s[:, 0, 1:2], src[:, P:3 * P], AX))
                V.tensor_scalar(s[:, 1, :], s[:, 0, :], -(HD ** -0.5), None, ALU.mult).then_inc(max_made, 1)

            def max_swa(i):
                j = i - FOX_H - DIL_H
                dve.wait_ge(scored, i + 1)
                dve.wait_ge(head_out, i - 3)
                s, src, dst = hs[:, i % 4], ps[:, 4 + i % 2], biased[:, i % 2]
                V.scalar_tensor_tensor(out=dst[:, 0:P], in0=src[:, 0:P], scalar=HD ** -0.5, in1=bias_t[:, j, P:2 * P],
                                       op0=ALU.mult, op1=ALU.add)
                step(V.scalar_tensor_tensor(out=dst[:, P:3 * P], in0=src[:, P:3 * P], scalar=HD ** -0.5,
                                            in1=bias_t[:, j, :], op0=ALU.mult, op1=ALU.add))
                V.reduce_max(s[:, 0, 0:1], dst[:, 0:P], AX)
                step(V.reduce_max(s[:, 0, 1:2], dst[:, P:3 * P], AX))
                V.tensor_scalar(s[:, 1, :], s[:, 0, :], sinks[:, j:j + 1], -1.0, ALU.max, ALU.mult).then_inc(max_made, 1)

            def count_head(i):
                dve.wait_ge(exp_made, i + 1)
                s = hs[:, i % 4]
                for n, (at, w) in enumerate(((0, P), (P, 2 * P))):
                    last = V.tensor_tensor_reduce(prob[:, i % 2, at:at + w], prob[:, i % 2, at:at + w],
                                                  KC(K_COUNT + at, w), 1.0, 0.0, ALU.mult, ALU.add, s[:, 2, n:n + 1])
                last.then_inc(counted, 1)

            def copy_p(i):
                dve.wait_ge(p_turned, i + 1)
                if i >= 2:
                    dve.wait_ge(pv_made, i - 1)
                V.tensor_copy(probT[:, i % 2, :], ps[:, i % 2, 0:3 * P]).then_inc(p_copied, 1)

            def out_head(i, at, sink=False):
                s = hs[:, i % 4]
                dve.wait_ge(pv_made, i + 1)
                if sink:
                    step(V.tensor_tensor(s[:, 2, :], s[:, 2, :], s[:, 4, :], ALU.add))
                step(V.reciprocal(s[:, 3, :], s[:, 2, :]))
                for t in range(NT):
                    last = V.tensor_scalar(mix[:, t, at:at + HD], ps[:, 2 + i % 2, HD * t:HD * t + HD],
                                           s[:, 3, t:t + 1], None, ALU.mult)
                last.then_inc(head_out, 1)

            V.memset(stats[:], 1.0).then_inc(stats_set, 1)
            norm(0)
            turn_lo(0)
            gemm("in1", N1, False)
            dve.wait_ge(copied_out, after("in1")[1])
            dve.wait_ge(small_loaded, 16)
            step(V.tensor_tensor(fg[:, 0], proj1[:, :, FG:FG + 16], fbias[:].unsqueeze(1).to_broadcast([P, NT, 16]), ALU.add))
            step(V.tensor_scalar(fg[:, 1], fg[:, 0], -1.0, None, ALU.mult))
            V.tensor_tensor(fg[:, 1], fg[:, 1], fg[:, 0], ALU.max).then_inc(gate_abs, 1)
            dve.wait_ge(gate_soft, 1)
            V.scalar_tensor_tensor(out=fg[:, 0], in0=fg[:, 0], scalar=0.0, in1=fg[:, 3], op0=ALU.min,
                                   op1=ALU.subtract).then_inc(gate_log, 1)
            dve.wait_ge(kc_loaded, 16)
            V.tensor_copy(mask_b[:], KC(K_MASK, 3 * P)).then_inc(masks_made, 1)
            for t in range(NT):
                qk = proj1[:, t, DQ:DQ + 2 * 1024].rearrange("p (n d) -> p n d", d=HD)
                x1, x2 = qk[:, :, 0:8], qk[:, :, 8:16]
                cos = KC(K_COS + 8 * t, 8).unsqueeze(1).to_broadcast([P, 32, 8])
                sin = KC(K_SIN + 8 * t, 8).unsqueeze(1).to_broadcast([P, 32, 8])
                V.tensor_tensor(rope[:, 0], x1, cos, ALU.mult)
                V.tensor_tensor(rope[:, 1], x2, sin, ALU.mult)
                V.tensor_tensor(rope[:, 2], x2, cos, ALU.mult)
                step(V.tensor_tensor(rope[:, 3], x1, sin, ALU.mult))
                V.tensor_tensor(x1, rope[:, 0], rope[:, 1], ALU.subtract)
                V.tensor_tensor(x2, rope[:, 2], rope[:, 3], ALU.add).then_inc(roped, 1)
                dve.wait_ge(roped, t + 1)
            for n in range(1, FOX_H + DIL_H + 3):
                if n <= FOX_H + DIL_H:
                    max_head(n - 1)
                if 2 <= n <= FOX_H + DIL_H + 1:
                    copy_p(n - 2)
                if n >= 3:
                    i = n - 3
                    out_head(i, HD * i)
                if FOX_H < n <= FOX_H + DIL_H:
                    count_head(n - 1)
            norm(1)
            turn_lo(1)
            gemm("out1", WIDE, True)
            norm(2)
            turn_lo(2)
            gemm("query", WIDE, False)

            def best(v, i, vals, work):
                step(V.max(v[:, 0:8], vals))
                V.max_index(i[:, 0:8].bitcast(U32), v[:, 0:8], vals)
                step(V.match_replace(work, v[:, 0:8], vals, -3.0e38))
                step(V.max(v[:, 8:16], work))
                step(V.max_index(i[:, 8:16].bitcast(U32), v[:, 8:16], work))

            for t in range(NT):
                for g in range(16):
                    if g % 4 == 0:
                        dve.wait_ge(sc_copied, 4 * t + g // 4 + 1)
                    best(top_v[:, t, g], top_i[:, t, g], sc[:, t, g, :], scr[:, 0:NKEY])
            step(V.tensor_copy(big[:, 1024:1536], big[:, 512:1024].bitcast(U32)))
            for t in range(NT):
                sums = cand.rearrange("p (g a b) -> p g a b", g=PH, a=TOPK)
                for g in range(PH):
                    last = V.tensor_tensor(sums[:, g], top_v[:, t, 2 * g].unsqueeze(2).to_broadcast([P, TOPK, TOPK]),
                                    top_v[:, t, 2 * g + 1].unsqueeze(1).to_broadcast([P, TOPK, TOPK]), ALU.add)
                step(last)
                for g in range(PH):
                    best(best_v[:, t, g], best_c[:, t, g], cand[:, 256 * g:256 * g + 256], scr)
            code = big[:, 1792:2048].bitcast(U32)
            step(V.tensor_scalar(ranku.bitcast(U32), code, 4, None, ALU.logical_shift_right))
            step(V.tensor_copy(big[:, 2048:2304], ranku.bitcast(U32)))
            step(V.tensor_scalar(ranku.bitcast(U32), code, 15, None, ALU.bitwise_and))
            step(V.tensor_copy(big[:, 2304:2560], ranku.bitcast(U32)))
            for s in range(2):
                for t in range(NT):
                    hot = cand.rearrange("p (n k) -> p n k", k=TOPK)
                    step(V.tensor_tensor(hot, rank[:, s, t].unsqueeze(2).to_broadcast([P, P, TOPK]),
                                         iota[:, 0:TOPK].unsqueeze(1).to_broadcast([P, P, TOPK]), ALU.is_equal))
                    for g in range(PH):
                        hg = hot[:, TOPK * g:TOPK * g + TOPK, :]
                        last = V.tensor_tensor(hg, hg, top_f[:, t, 2 * g + s].unsqueeze(1).to_broadcast([P, TOPK, TOPK]), ALU.mult)
                    step(last)
                    step(V.tensor_reduce(chosen[:, s, t], hot, AX, ALU.add))
            bv = big[:, 1536:1792].rearrange("p (g k) -> p g k", k=TOPK)
            step(V.tensor_copy(gsum[:, 0, :].unsqueeze(2), bv[:, :, 0:1]))
            V.tensor_tensor(bv, bv, gsum[:, 0, :].unsqueeze(2).to_broadcast([P, 16, TOPK]), ALU.subtract).then_inc(gate_diff, 1)
            dve.wait_ge(gate_exp, 1)
            step(V.tensor_reduce(gsum[:, 0, :], bv, AX, ALU.add))
            step(V.reciprocal(gsum[:, 1, :], gsum[:, 0, :]))
            V.tensor_tensor(chosen[:, 2].rearrange("p t (g k) -> p (t g) k", k=TOPK), bv,
                            gsum[:, 1, :].unsqueeze(2).to_broadcast([P, 16, TOPK]), ALU.mult).then_inc(chosen_made, 1)

            for half in range(2):
                base = 32 * half
                if half == 0:
                    dve.wait_ge(ch_copied, 3)
                else:
                    dve.wait_ge(chunk_used, SUB * after("peer0")[0])

                def batch(n, slot, base=base, half=half):
                    if half or not static(n) or n >= 2:
                        dve.wait_ge(g_summed, base + n - 1)
                    V.tensor_tensor(one1[:, slot], iota.unsqueeze(1).to_broadcast([P, 8, P]),
                                    chosenT[:, 0, bass.ds(8 * n, 8)].unsqueeze(2).to_broadcast([P, 8, P]),
                                    ALU.is_equal).then_inc(one1_made, 1)
                    V.tensor_tensor(is2[:, slot],
                                    iota[:, HALF_J * half:HALF_J * half + HALF_J].unsqueeze(1).to_broadcast([P, 8, HALF_J]),
                                    chosenT[:, 1, bass.ds(8 * n, 8)].unsqueeze(2).to_broadcast([P, 8, HALF_J]),
                                    ALU.is_equal).then_inc(is2_made, 1)
                batch(0, 0)
                batch(1, 1)
                with dve.Fori(0, 15) as i:
                    batch(2 * i + 2, 0)
                    batch(2 * i + 3, 1)
                dve.wait_ge(g_copied, base + 32)
                rounds(f"peer{half}", 4 * ROUNDS_HALF * half, ROUNDS_HALF, True)
            norm(3)

            norm(4)
            turn_lo(3)
            gemm("in2", N2, False)
            dve.wait_ge(copied_out, after("in2")[1])
            dve.wait_ge(kc_loaded, 32)
            V.tensor_copy(mask_b[:], KC(K_MASK, 3 * P)).then_inc(masks_made, 1)
            dve.wait_ge(small_loaded, 16 * 7)
            dve.wait_ge(bias_loaded, 16)
            i0, i1 = FOX_H + DIL_H, FOX_H + DIL_H + SWA_H
            for n in range(i0 + 1, i1 + 3):
                if n <= i1:
                    max_swa(n - 1)
                if i0 + 2 <= n <= i1 + 1:
                    copy_p(n - 2)
                if n >= i0 + 3:
                    out_head(n - 3, HD * (n - 3 - i0), True)
            for t in range(NT):
                dve.wait_ge(gpre_made, t + 1)
                step(V.tensor_copy(q_dec[:, t], ps[:, 1 + t, 0:384]))
                step(V.tensor_scalar(g_log[:, t], q_dec[:, t], -1.0, None, ALU.mult))
                V.tensor_tensor(g_log[:, t], g_log[:, t], q_dec[:, t], ALU.max).then_inc(gla_abs, 1)
                dve.wait_ge(gla_soft, t + 1)
                step(V.scalar_tensor_tensor(out=g_tmp[:], in0=ps[:, 1 + t, 0:384], scalar=0.0, in1=q_dec[:, t],
                                            op0=ALU.min, op1=ALU.subtract))
                V.tensor_scalar(g_log[:, t], g_tmp[:], 1.0 / 16.0, -1.0, ALU.mult, ALU.max).then_inc(gla_log, 1)
            for t in range(NT):
                dve.wait_ge(gla_exp, 2 * t + 1)
                step(V.tensor_copy(g_tmp[:], ps[:, 1, 0:384]))
                V.tensor_tensor(k_end[:, t, 0], g_tmp[:], ps[:, 0, 0:384], ALU.subtract).then_inc(gla_ops, 1)
                step(V.scalar_tensor_tensor(out=q_dec[:, t], in0=q_dec[:, t], scalar=GLA_K ** -0.5,
                                            in1=proj2[:, t, BQ:BQ + 384], op0=ALU.mult, op1=ALU.mult))
                step(V.tensor_tensor(k_inv[:, t], k_inv[:, t], proj2[:, t, BK:BK + 384], ALU.mult))
                dve.wait_ge(gla_exp, 2 * t + 2)
                step(V.tensor_tensor(g_tmp[:], k_end[:, t, 1], proj2[:, t, BK:BK + 384], ALU.mult))
                step(V.tensor_scalar(k_end[:, t, 0], g_tmp[:], KC(K_HALF, 1), None, ALU.mult))
                V.tensor_scalar(k_end[:, t, 1], g_tmp[:], KC(K_HALF + 1, 1), None, ALU.mult).then_inc(gla_ops, 1)
            for hh in range(GLA_H):
                dve.wait_ge(gla_decexp, hh + 1)
                if hh == 0:
                    step(V.memset(qdT[:, 0:2, :], 0.0))
                for t in range(NT):
                    n = NT * hh + t
                    dve.wait_ge(gt_copied, n + 1)
                    V.tensor_copy(qdT[:, 0, 0:64], qdT[:, 2, 0:64])
                    V.tensor_copy(qdT[:, 1, 64:128], qdT[:, 2, 64:128])
                    dve.wait_ge(gs_made, n + 1)
                    V.tensor_tensor(g_sc[:], ps[:, 2, 0:P], KC(K_GTRI), ALU.mult).then_inc(gs_masked, 1)
                    dve.wait_ge(gd_made, n + 1)
                    if t == 0:
                        step(V.tensor_copy(state[:, 1], ps[0:GLA_K, 3, 0:GLA_V]))
                        V.scalar_tensor_tensor(out=state[:, 2], in0=state[:, 1], scalar=g_dec[:, 1:2],
                                               in1=ps[0:GLA_K, 3, GLA_V:2 * GLA_V], op0=ALU.mult,
                                               op1=ALU.add).then_inc(state_made, 1)
                    else:
                        V.scalar_tensor_tensor(out=state[:, 3], in0=state[:, 2], scalar=g_dec[:, 2:3],
                                               in1=ps[0:GLA_K, 3, 0:GLA_V], op0=ALU.mult,
                                               op1=ALU.add).then_inc(state_made, 1)
                    dve.wait_ge(go_made, n + 1)
            for n in range(1, SB_H + 6):
                if n <= SB_H:
                    i = n - 1
                    g = i1 + i
                    dve.wait_ge(scored, g + 1)
                    if i >= 4:
                        dve.wait_ge(pv_made, g - 3)
                    V.tensor_scalar(sbz[:, i % 4], ps[:, 4 + g % 2, 0:3 * P], HD ** -0.5, None, ALU.mult)
                    step(V.tensor_scalar(sbt[:, i % 4], ps[:, 4 + g % 2, 0:3 * P], -(HD ** -0.5), None, ALU.mult))
                    V.tensor_tensor(sbt[:, i % 4], sbt[:, i % 4], sbz[:, i % 4], ALU.max).then_inc(sb_abs, 1)
                if 3 <= n <= SB_H + 2:
                    i = n - 3
                    dve.wait_ge(sb_sum, i + 1)
                    V.tensor_tensor(sbb[:, i % 4], ps[:, i % 2, 0:3 * P], sbb[:, i % 4], ALU.add).then_inc(sb_add, 1)
                if 2 <= n <= SB_H + 1:
                    i = n - 2
                    dve.wait_ge(sb_soft, i + 1)
                    step(V.scalar_tensor_tensor(out=sbb[:, i % 4], in0=sbz[:, i % 4], scalar=0.0, in1=sbt[:, i % 4],
                                                op0=ALU.min, op1=ALU.subtract))
                    step(V.tensor_tensor(sb1[:, i % 4], sbb[:, i % 4], sbz[:, i % 4], ALU.subtract))
                    V.tensor_tensor(sb1[:, i % 4, 0:P], sb1[:, i % 4, 0:P], KC(K_STRICT), ALU.mult)
                    V.tensor_tensor(sb1[:, i % 4, 2 * P:3 * P], sb1[:, i % 4, 2 * P:3 * P], KC(K_STRICT),
                                    ALU.mult).then_inc(sb_log, 1)
                if 4 <= n <= SB_H + 3:
                    i = n - 4
                    dve.wait_ge(sb_exp, i + 1)
                    V.tensor_tensor(sbw[:, i % 4, 0:P], sbw[:, i % 4, 0:P], KC(K_STRICT), ALU.mult)
                    V.tensor_tensor(sbw[:, i % 4, 2 * P:3 * P], sbw[:, i % 4, 2 * P:3 * P], KC(K_STRICT),
                                    ALU.mult).then_inc(sb_w, 1)
                if n >= 6:
                    i = n - 6
                    g = i1 + i
                    dve.wait_ge(pv_made, g + 1)
                    for t in range(NT):
                        last = V.tensor_copy(mix[:, t, 1536 + HD * i:1536 + HD * i + HD], ps[:, 2 + g % 2, HD * t:HD * t + HD])
                    last.then_inc(head_out, 1)
            norm(5)
            for t in range(NT):
                dve.wait_ge(br_exp, t + 1)
                e, r = proj2[:, t, BQ:BQ + 768], proj2[:, t, BR:BR + 768]
                step(V.tensor_scalar(e, e, 1.0, None, ALU.add))
                step(V.reciprocal(e, e))
                step(V.tensor_tensor(e, e, r, ALU.mult))
                V.tensor_tensor(mix[:, t, 768:1536], mix[:, t, 768:1536], e, ALU.mult).then_inc(mixed2, 1)
            turn_lo(4)
            gemm("out2", WIDE, True)
            norm(6)
            turn_lo(5)
            rounds("mlp", 8 * ROUNDS_HALF, MLP_ROUNDS, False)
            norm(7)

        @block.tensor
        def _(pe):
            mm = pe.matmul

            def turn(k, due):
                due()
                for g in range(8):
                    if g >= 2 or k > 0:
                        pe.wait_ge(x_lo_made, 8 * k + g - 1)
                    for kk in range(2):
                        for t in range(NT):
                            at = 2 * g + kk
                            last = pe.transpose(ps[:, 4 + g % 2, kk * S + t * P:kk * S + t * P + P],
                                                mix[:, t, at * P:at * P + P], ident)
                    last.then_inc(x_turned, 1)

            def chunk(B, parity, c, n, hi, lo):
                pe.wait_ge(lo_made, SUB * B + c + 1)
                for kk in range(2):
                    k = 2 * c + kk
                    wh = w_hi[:, c % RING, kk * n:kk * n + n]
                    wl = w_lo[:, c % RING, kk * n:kk * n + n]
                    for t in range(NT):
                        o = ps[:, bank(parity, t), 0:n]
                        xh, xl = hi[:, k, t * P:t * P + P], lo[:, k, t * P:t * P + P]
                        mm(o, xh, wh, start=(k == 0), stop=False)
                        mm(o, xh, wl, start=False, stop=False)
                        last = mm(o, xl, wh, start=False, stop=(k == KT - 1))
                last.then_inc(chunk_used, 1)

            def gemm(name, k, n, kind):
                b0, acts, adds, nb = sections[name]
                pe.wait_ge(x_lo_made, 8 * k + 8)
                sem_, base = (copied_out, acts) if kind == "act" else (added_out, adds)

                def blk(b, parity):
                    if not static(b) or b >= 2:
                        pe.wait_ge(sem_, base + b - 1)
                    for c in range(SUB):
                        chunk(b0 + b, parity, c, n, x_hi, x_lo)
                over_blocks(pe, nb, blk)

            def rounds(name, h0, count):
                b0, acts, adds, _ = sections[name]

                def turn_hidden(r, i):
                    pe.wait_ge(copied_out, acts + 4 * r + i + 1)
                    free = h0 + 4 * r + i - 1
                    if not static(free) or free > 0:
                        pe.wait_ge(hid_lo, free)
                    for jj in range(4):
                        for t in range(NT):
                            last = pe.transpose(ps[:, 4 + 2 * (i % 2) + jj // 2, (jj % 2) * S + t * P:(jj % 2) * S + t * P + P],
                                                hid[:, t, jj * P:jj * P + P], ident)
                    last.then_inc(hid_turned, 1)

                def one(r, first):
                    for i in range(8):
                        if i < 2 and first:
                            pe.wait_ge(copied_out, acts)
                            pe.wait_ge(added_out, adds)
                        elif 2 <= i < 6:
                            pe.wait_ge(copied_out, acts + 4 * r + i - 1)
                        else:
                            pe.wait_ge(added_out, adds + 4 * r + (i - 5 if i >= 6 else i - 1))
                        for c in range(SUB):
                            if i == 4 and c % 2 == 0:
                                if c == 4:
                                    turn_hidden(r, 3)
                                pe.wait_ge(hid_lo, h0 + 4 * r + c // 2 + 1)
                            chunk(b0 + 8 * r + i, i % 2, c, WIDE, x_hi if i < 4 else a_hi, x_lo if i < 4 else a_lo)
                        if 1 <= i < 4:
                            turn_hidden(r, i - 1)
                one(0, True)
                with pe.Fori(1, count) as r:
                    one(r, False)

            def turn_qk(i, src, q, k):
                if i >= 2:
                    pe.wait_ge(qk_copied, i - 1)
                for n, at in enumerate((q, k)):
                    for t in range(NT):
                        last = pe.transpose(ps[0:HD, 6 + i % 2, n * S + t * P:n * S + t * P + P], src[:, t, at:at + HD], ident)
                last.then_inc(qk_turned, 1)

            def score(i, fox=None, masked=True):
                pe.wait_ge(qk_copied, i + 1)
                if i >= 2:
                    pe.wait_ge(exp_made, i - 1)
                o, q, k = ps[:, 4 + i % 2], qkT[:, i % 2, 0:S], qkT[:, i % 2, S:2 * S]
                for t, at, w in ((0, 0, P), (1, P, S)):
                    o_t = o[:, at:at + w]
                    last = mm(o_t, q[:, t * P:t * P + P], k[:, 0:w], start=True, stop=not (masked or fox is not None))
                    if fox is not None:
                        hot = fix[0:16, C_IDENT + fox:C_IDENT + fox + 1]
                        mm(o_t, cumT[:, 0, t * P:t * P + P], hot.to_broadcast([16, w]), start=False, stop=False)
                        mm(o_t, hot.to_broadcast([16, P]), cumT[:, 1, 0:w], start=False, stop=False)
                        last = mm(o[:, at + w - P:at + w], ident_b[:], caus, start=False, stop=True)
                    elif masked:
                        last = mm(o_t, ident_b[:], mask_b[:, at:at + w], start=False, stop=True)
                last.then_inc(scored, 1)

            def turn_p(i, due, count):
                pe.wait_ge(due, count)
                if i >= 2:
                    pe.wait_ge(p_copied, i - 1)
                for b in range(3):
                    last = pe.transpose(ps[:, i % 2, b * P:b * P + P], prob[:, i % 2, b * P:b * P + P], ident)
                last.then_inc(p_turned, 1)

            def pv(i, due, count, pT, v0, v1):
                pe.wait_ge(due, count)
                if i >= 2:
                    pe.wait_ge(head_out, i - 1)
                o = ps[:, 2 + i % 2]
                mm(o[:, 0:HD], pT[:, 0:P], v0, start=True, stop=True)
                mm(o[:, HD:2 * HD], pT[:, P:2 * P], v0, start=True, stop=False)
                mm(o[:, HD:2 * HD], pT[:, 2 * P:3 * P], v1, start=False, stop=True).then_inc(pv_made, 1)

            pe.wait_ge(fix_loaded, 16)
            turn(0, lambda: pe.wait_ge(normed, NT * 1))
            gemm("in1", 0, N1, "act")
            pe.wait_ge(gate_log, 1)
            lf = fg[:, 0]
            mm(ps[0:16, 0, 0:P], lf[:, 0, :], KC(K_UTRI), start=True, stop=True)
            mm(ps[0:16, 0, P:S], lf[:, 0, :], KC(K_ONES), start=True, stop=False)
            mm(ps[0:16, 0, P:S], lf[:, 1, :], KC(K_UTRI), start=False, stop=True).then_inc(cum_made, 1)
            pe.wait_ge(cum_copied, 1)
            pe.wait_ge(masks_made, 2)
            caus = mask_b[:, 0:P]
            pe.wait_ge(roped, NT)
            heads = FOX_H + DIL_H
            for n in range(heads + 3):
                if n < heads:
                    f = n < FOX_H
                    m = n if f else n - FOX_H
                    turn_qk(n, proj1, (FQ if f else DQ) + HD * m, (FK if f else DK) + HD * m)
                if 1 <= n <= heads:
                    score(n - 1, n - 1 if n - 1 < FOX_H else None)
                if 2 <= n <= heads + 1:
                    i = n - 2
                    if i < FOX_H:
                        turn_p(i, exp_made, i + 1)
                    else:
                        turn_p(i, counted, i - FOX_H + 1)
                if n >= 3:
                    i = n - 3
                    at = FV + HD * i if i < FOX_H else DV + HD * (i - FOX_H)
                    pv(i, p_copied, i + 1, probT[:, i % 2], proj1[:, 0, at:at + HD], proj1[:, 1, at:at + HD])
            turn(1, lambda: pe.wait_ge(normed, NT * 2))
            gemm("out1", 1, WIDE, "add")
            turn(2, lambda: pe.wait_ge(normed, NT * 3))
            gemm("query", 2, WIDE, "act")

            pe.wait_ge(copied_out, after("query")[1])
            for g in range(8):
                if g >= 2:
                    pe.wait_ge(pq_copied, g - 1)
                for kk in range(2):
                    for t in range(NT):
                        at = 2 * g + kk
                        last = pe.transpose(ps[:, 4 + g % 2, kk * S + t * P:kk * S + t * P + P], pq[:, t, at * P:at * P + P], ident)
                last.then_inc(pq_turned, 1)
            pe.wait_ge(pq_copied, 8)
            pe.wait_ge(small_loaded, 32)
            for n in range(8):
                t, g = n // 4, n % 4
                if n >= 2:
                    pe.wait_ge(sc_copied, n - 1)
                for j in range(4):
                    last = mm(ps[:, 6 + n % 2, j * P:j * P + P], pqT[:, 4 * g + j, t * P:t * P + P], skT[:, 4 * g + j, :],
                              start=True, stop=True)
                last.then_inc(sc_made, 1)
            pe.wait_ge(chosen_made, 1)
            for s in range(3):
                for t in range(NT):
                    last = pe.transpose(ps[:, s, t * P:t * P + P], chosen[:, s, t], ident)
                last.then_inc(ch_turned, 1)
            for half in range(2):
                base = 32 * half

                def batch(n, slot, base=base, half=half):
                    pe.wait_ge(one1_made, base + n + 1)
                    pe.wait_ge(one2_made, base + n + 1)
                    if half or not static(n) or n >= 2:
                        pe.wait_ge(g_copied, base + n - 1)
                    for j in range(8):
                        last = mm(ps[:, 6 + slot, HALF_J * j:HALF_J * (j + 1)], one1[:, slot, j, :], one2[:, slot, j, :],
                                  start=True, stop=True)
                    last.then_inc(g_summed, 1)
                batch(0, 0)
                batch(1, 1)
                with pe.Fori(0, 15) as i:
                    batch(2 * i + 2, 0)
                    batch(2 * i + 3, 1)
                pe.wait_ge(g_copied, base + 32)
                rounds(f"peer{half}", 4 * ROUNDS_HALF * half, ROUNDS_HALF)

            pe.wait_ge(rel_ready, 1)
            pe.wait_ge(small_loaded, 16 * 7)
            mm(ps[0:SWA_H, 0, 0:TW + 1], rel[:], buck[:], start=True, stop=True).then_inc(rel_made, 1)
            turn(3, lambda: pe.wait_ge(normed, NT * 5))
            gemm("in2", 3, N2, "act")
            pe.wait_ge(copied_out, after("in2")[1])
            pe.wait_ge(masks_made, 3)
            i0, i1 = heads, heads + SWA_H
            for n in range(i0, i1 + 3):
                if n < i1:
                    m = n - i0
                    turn_qk(n, proj2, AQ + HD * m, AK + HD * (m // SWA_G))
                if i0 + 1 <= n <= i1:
                    score(n - 1, None, False)
                if i0 + 2 <= n <= i1 + 1:
                    turn_p(n - 2, exp_made, n - 1)
                if n >= i0 + 3:
                    i = n - 3
                    at = AV + HD * ((i - i0) // SWA_G)
                    pv(i, p_copied, i + 1, probT[:, i % 2], proj2[:, 0, at:at + HD], proj2[:, 1, at:at + HD])
            pe.wait_ge(head_out, i1)
            for t in range(NT):
                last = pe.transpose(ps[0:GLA_R, 0, t * P:t * P + P], proj2[:, t, BL:BL + GLA_R], ident)
            last.then_inc(bl_turned, 1)
            pe.wait_ge(bl_copied, 1)
            pe.wait_ge(pool_step, 3)
            for t in range(NT):
                mm(ps[:, 1 + t, 0:384], blT[:, t * P:t * P + P], gw[:], start=True, stop=True).then_inc(gpre_made, 1)
            pe.wait_ge(gla_log, NT)
            for t in range(NT):
                if t:
                    pe.wait_ge(gla_ops, 2 * t)
                mm(ps[:, 0, 0:384], KC(K_GTRI), g_log[:, t], start=True, stop=True)
                mm(ps[:, 1, 0:384], KC(K_GBLK), g_log[:, t], start=True, stop=True).then_inc(gla_sum, 1)
            pe.wait_ge(gla_ops, 2 * NT)
            for hh in range(GLA_H):
                c0 = GLA_K * hh
                if hh:
                    pe.wait_ge(gla_decexp, hh)
                for t in range(NT):
                    last = mm(ps[0:GLA_K, 0, 2 * t:2 * t + 2], g_log[:, t, c0:c0 + GLA_K], KC(K_HALF, 2), start=True, stop=True)
                last.then_inc(gla_dec, 1)
                for t in range(NT):
                    n = NT * hh + t
                    v = proj2[:, t, BV + GLA_V * hh:BV + GLA_V * (hh + 1)]
                    pe.transpose(ps[0:GLA_K, 1, 0:P], q_dec[:, t, c0:c0 + GLA_K], ident)
                    pe.transpose(ps[0:GLA_K, 1, P:S], k_inv[:, t, c0:c0 + GLA_K], ident).then_inc(gt_made, 1)
                    if n:
                        pe.wait_ge(state_made, n)
                    for c in range(2):
                        last = mm(ps[0:GLA_K, 3, GLA_V * c:GLA_V * (c + 1)], k_end[:, t, c, c0:c0 + GLA_K], v, start=True, stop=True)
                    last.then_inc(gd_made, 1)
                    pe.wait_ge(gt_copied, n + 1)
                    mm(ps[:, 2, 0:P], qdT[:, 3, :], qdT[:, 2, :], start=True, stop=True).then_inc(gs_made, 1)
                    pe.wait_ge(gs_masked, n + 1)
                    pe.wait_ge(state_made, n + 1)
                    if n:
                        pe.wait_ge(go_copied, n)
                    o = ps[:, 4, 0:GLA_V]
                    mm(o, g_sc[:], v, start=True, stop=False)
                    if t:
                        mm(o, qdT[:, 0, :], state[:, 2], start=False, stop=False)
                    last = mm(o, qdT[:, 1, :], state[:, 1 if t == 0 else 3], start=False, stop=True)
                    last.then_inc(go_made, 1)
            pe.wait_ge(go_copied, GLA_H * NT)
            for n in range(SB_H + 6):
                g = i1 + n
                if n < SB_H:
                    turn_qk(g, proj2, CQ + HD * n, CK + HD * n)
                if 1 <= n <= SB_H:
                    i = n - 1
                    g = i1 + i
                    pe.wait_ge(qk_copied, g + 1)
                    if i >= 2:
                        pe.wait_ge(sb_abs, i - 1)
                    o, q, k = ps[:, 4 + g % 2], qkT[:, g % 2, 0:S], qkT[:, g % 2, S:2 * S]
                    mm(o[:, 0:S], k[:, 0:P], q, start=True, stop=True)
                    mm(o[:, S:3 * P], k[:, P:S], q[:, P:S], start=True, stop=True).then_inc(scored, 1)
                if 3 <= n <= SB_H + 2:
                    i = n - 3
                    pe.wait_ge(sb_log, i + 1)
                    if i >= 2:
                        pe.wait_ge(sb_add, i - 1)
                    o, l1 = ps[:, i % 2], sb1[:, i % 4]
                    mm(o[:, 0:P], KC(K_SUF), l1[:, 0:P], start=True, stop=True)
                    mm(o[:, P:S], KC(K_SUF), l1[:, P:S], start=True, stop=False)
                    mm(o[:, P:S], KC(K_ONES), l1[:, S:3 * P], start=False, stop=True)
                    mm(o[:, S:3 * P], KC(K_SUF), l1[:, S:3 * P], start=True, stop=True).then_inc(sb_sum, 1)
                if 5 <= n <= SB_H + 4:
                    i = n - 5
                    at = CV + HD * i
                    pv(i1 + i, sb_w, i + 1, sbw[:, i % 4], proj2[:, 0, at:at + HD], proj2[:, 1, at:at + HD])
            turn(4, lambda: pe.wait_ge(mixed2, NT))
            gemm("out2", 4, WIDE, "add")
            turn(5, lambda: pe.wait_ge(normed, NT * 7))
            pe.wait_ge(x_lo_made, 48)
            rounds("mlp", 8 * ROUNDS_HALF, MLP_ROUNDS)


def blocks_of(w, n):
    k, m = w.shape
    return w.reshape(k // 256, 2, P, m // n, n).transpose(3, 0, 2, 1, 4)


def kernel(**inputs):
    import concourse.bacc as _bacc
    from concourse.bass_utils import run_bass_kernel_spmd as _run

    w = {k: np.asarray(v) for k, v in inputs.items()}
    arrays = {
        "w_in": blocks_of(w["w_in"][0], N1),
        "w_out": blocks_of(w["w_out"][0], WIDE),
        "peer_query": blocks_of(w["peer_query"][0], WIDE),
        "peer_down": w["peer_down"][0].reshape(P, 32, 4, SUB, 2, P).transpose(1, 3, 5, 4, 2, 0).reshape(32, SUB, P, 2, WIDE),
        "peer_up": w["peer_up"][0].reshape(P, 8, SUB, 2, 4, WIDE).transpose(1, 4, 2, 0, 3, 5).reshape(32, SUB, P, 2, WIDE),
        "w_in_2": blocks_of(w["w_in_2"][0], N2),
        "w_out_2": blocks_of(w["w_out_2"][0], WIDE),
        "w_mlp_in_2": blocks_of(w["w_mlp_in_2"][0], WIDE),
        "w_mlp_out_2": w["w_mlp_out_2"][0].reshape(4, SUB, 2, P, 4, WIDE).transpose(0, 4, 1, 3, 2, 5).reshape(16, SUB, P, 2, WIDE),
        "peer_sub_keys": w["peer_sub_keys"][0].reshape(16, NKEY, P).transpose(2, 0, 1),
        "fix": fixed_constants(), "kc": attention_constants(), "buck": bucket_constants(),
    }
    for name in ("x", "attn_norm_gain", "forget_bias", "fox_out_gain", "dil_out_gain", "ffn_norm_gain", "final_norm_gain",
                 "norm_mix_2", "swa_sinks_2", "rel_bias_2", "gla_gate_w_2", "gla_gate_b_2", "gla_norm_2", "swa_out_norm_2",
                 "sb_out_norm_2", "norm_mlp_2", "norm_final_2"):
        arrays[name] = w[name]
    nc = _bacc.Bacc("TRN2", target_bir_lowering=False, num_devices=1)
    maps, aps = {}, {}
    for name, v in arrays.items():
        maps[f"in_{name}"] = v = np.ascontiguousarray(v)
        aps[name] = nc.dram_tensor(f"in_{name}", v.shape, mybir.dt.from_np(v.dtype), kind="ExternalInput").ap()
    out = nc.dram_tensor("out_0", (1, S, D), F32, kind="ExternalOutput").ap()
    build(nc, aps, out)
    return _run(nc, [maps], core_ids=[0]).results[0]["out_0"]
```

```python
from contextlib import ExitStack

import numpy as np

import concourse.bass as bass
from concourse import mybir

ALU = mybir.AluOpType
ACT = mybir.ActivationFunctionType
F32 = mybir.dt.float32
F32R = mybir.dt.float32r
BF16 = mybir.dt.bfloat16
U32 = mybir.dt.uint32
AX = mybir.AxisListType.X

P = 128
S = 256
NT = S // P
D = 2048
KT = D // P
HD = 64
EPS = 1e-6
NEG = -1e30

SUB = 8
RING = 4
WIDE = 512

IN1 = 6160
FQ, FK, FV, FG, DQ, DK, DV = 0, 1024, 2048, 3072, 3088, 4112, 5136
FOX_H = DIL_H = 16
IN2 = 5136
AQ, AK, AV, BQ, BK, BV, BR, BL, CQ, CK, CV = 0, 768, 1024, 1280, 1664, 2048, 2816, 3584, 3600, 4112, 4624
SWA_H, SWA_G = 12, 3
GLA_H, GLA_K, GLA_V, GLA_R = 4, 96, 192, 16
SB_H = 8

PH, TOPK, NKEY = 8, 16, 128
HALF_J = 64

N1, NB1 = 440, 14
N2, NB2 = 428, 12
PEER_ROUNDS, MLP_ROUNDS = 8, 4

C_IDENT, C_IOTA = 0, 128
K_UTRI, K_ONES, K_SUF, K_GTRI, K_GBLK, K_COS, K_SIN, K_HALF, K_MASK, K_COUNT, K_STRICT = (
    0, 128, 256, 384, 512, 640, 656, 672, 674, 1058, 1442)
K_COLS = 1570
TW = 383


def fixed_constants():
    out = np.zeros((P, 256), np.float32)
    out[:, C_IDENT:C_IDENT + P] = np.eye(P)
    out[:, C_IOTA:C_IOTA + P] = np.arange(P)
    return out


def attention_constants():
    i, j = np.arange(P)[:, None], np.arange(P)[None, :]
    out = np.zeros((P, K_COLS), np.float32)
    out[:, K_UTRI:K_UTRI + P] = i <= j
    out[:, K_ONES:K_ONES + P] = 1
    out[:, K_SUF:K_SUF + P] = i > j
    same = i // 64 == j // 64
    out[:, K_GTRI:K_GTRI + P] = same & (i <= j)
    out[:, K_GBLK:K_GBLK + P] = same
    inv = (np.float32(500000.0) ** (-np.arange(0, 16, 2, dtype=np.float32) / np.float32(16))).astype(np.float32)
    for t in range(NT):
        ang = (np.arange(P, dtype=np.float32)[:, None] + t * P) * inv[None]
        out[:, K_COS + 8 * t:K_COS + 8 * t + 8] = np.cos(ang)
        out[:, K_SIN + 8 * t:K_SIN + 8 * t + 8] = np.sin(ang)
    out[:64, K_HALF] = 1
    out[64:, K_HALF + 1] = 1
    for n, (qt, kt) in enumerate(((0, 0), (1, 0), (1, 1))):
        q, k = qt * P + i, kt * P + j
        dist = q - k
        count = (dist >= 0) * ((dist <= 128) * 1.0 + (dist % 4 == 0) + (dist % 16 == 0))
        out[:, K_MASK + n * P:K_MASK + n * P + P] = np.where(count > 0, 0, NEG)
        out[:, K_COUNT + n * P:K_COUNT + n * P + P] = count
    out[:, K_STRICT:K_STRICT + P] = i < j
    return out


def bucket_constants():
    out = np.zeros((33, TW + 1), np.float32)
    for x in range(TW):
        dist = 255 - x
        if not 0 <= dist < 128:
            out[32, x] = NEG
            continue
        if dist < 16:
            b = dist
        else:
            ratio = np.float32(np.log(np.float32(dist) / np.float32(16))) / np.float32(np.log(8.0))
            b = min(16 + int(np.float32(ratio * np.float32(16))), 31)
        out[b, x] = 1
    return out


def build(nc, a, out):
    ctx = ExitStack()
    with ctx:
        def sb(name, shape, dt=F32, stack=ctx):
            return stack.enter_context(nc.sbuf_tensor(name, shape, dt))

        def sem(name):
            return ctx.enter_context(nc.semaphore(name))

        raw = sb("raw", [P, RING, 2 * WIDE])
        w_hi = sb("w_hi", [P, RING, 2 * WIDE], F32R)
        w_lo = sb("w_lo", [P, RING, 2 * WIDE], F32R)
        h = sb("h", [P, NT, D])
        fix = sb("fix", [P, 256])
        ident_b = sb("ident_b", [P, P], BF16)
        back = sb("back", [P, NT, WIDE])
        stats = sb("stats", [P, 4, 16])
        big = sb("big", [P, 18464])
        proj1 = big[:, 0:NT * IN1].rearrange("p (t n) -> p t n", t=NT)
        proj2 = big[:, 0:NT * IN2].rearrange("p (t n) -> p t n", t=NT)
        mix = big[:, 12320:16416].rearrange("p (t n) -> p t n", t=NT)
        gain = big[:, 16416:18464]
        last_gain = big[:, 0:D]
        pq = big[:, 0:4096].rearrange("p (t n) -> p t n", t=NT)
        pqT = big[:, 4096:8192].rearrange("p (g s) -> p g s", g=16)
        skT = big[:, 8192:10240].rearrange("p (g n) -> p g n", g=16)
        sc = big[:, 10240:14336].rearrange("p (t g n) -> p t g n", t=NT, g=16)
        cand = big[:, 14336:16384]
        top_v = big[:, 0:512].rearrange("p (t g k) -> p t g k", t=NT, g=16)
        top_i = big[:, 512:1024].rearrange("p (t g k) -> p t g k", t=NT, g=16)
        top_f = big[:, 1024:1536].rearrange("p (t g k) -> p t g k", t=NT, g=16)
        best_v = big[:, 1536:1792].rearrange("p (t g k) -> p t g k", t=NT, g=PH)
        best_c = big[:, 1792:2048].rearrange("p (t g k) -> p t g k", t=NT, g=PH)
        rank = big[:, 2048:2560].rearrange("p (s t n) -> p s t n", s=2, t=NT)
        ranku = big[:, 2560:2816]
        chosen = big[:, 2816:3584].rearrange("p (s t n) -> p s t n", s=3, t=NT)
        gsum = big[:, 3584:3616].rearrange("p (s n) -> p s n", s=2)
        scr = big[:, 3616:3872]
        chosenT = big[:, 16416:17184].rearrange("p (s n) -> p s n", s=3)
        gates = big[:, 0:S * HALF_J].rearrange("p (s j) -> p j s", j=HALF_J)
        gates_w = big[:, 0:S * HALF_J]
        hid = big[:, 17184:18208].rearrange("p (t n) -> p t n", t=NT)

        with ExitStack() as part:
            x_hi = sb("x_hi", [P, KT, S], F32R, part)
            x_lo = sb("x_lo", [P, KT, S], F32R, part)
            a_hi = sb("a_hi", [P, KT, S], F32R, part)
            a_lo = sb("a_lo", [P, KT, S], F32R, part)
        with ExitStack() as part:
            sb("beside", [P, 2 * KT * S], F32, part)
            one1 = sb("one1", [P, 4, 8, P], F32, part)
            is2 = sb("is2", [P, 4, 8, HALF_J], F32, part)
            one2 = sb("one2", [P, 4, 8, HALF_J], F32, part)
        with ExitStack() as part:
            qkT = sb("qkT", [HD, 2, 2 * S], F32, part)
            prob = sb("prob", [P, 2, 3 * P], F32, part)
            probT = sb("probT", [P, 2, 3 * P], F32, part)
            hs = sb("hs", [P, 4, 5, 2], F32, part)
            fg = sb("fg", [P, 4, 2, 16], F32, part)
            c8 = sb("c8", [16, S], F32, part)
            c_rest = sb("c_rest", [16, S], F32, part)
            c_mid = sb("c_mid", [16, S], BF16, part)
            c_parts = sb("c_parts", [80, 2, S], BF16, part)
            rope = sb("rope", [P, 4, 32, 8], F32, part)
            biased = sb("biased", [P, 2, 3 * P], F32, part)
            g_log = sb("g_log", [P, NT, 384], F32, part)
            g_tmp = sb("g_tmp", [P, 384], F32, part)
            q_dec = sb("q_dec", [P, NT, 384], F32, part)
            k_inv = sb("k_inv", [P, NT, 384], F32, part)
        with ExitStack() as part:
            sb("beside_x", [P, 2 * KT * S], F32, part)
            kc = sb("kc", [P, K_COLS], F32, part)
            mask_b = sb("mask_b", [P, 3 * P], BF16, part)
            fbias = sb("fbias", [P, 16], F32, part)
            sinks = sb("sinks", [P, SWA_H], F32, part)
            buck = sb("buck", [33, TW + 1], F32, part)
            rel = sb("rel", [33, SWA_H], F32, part)
            relrow = sb("relrow", [SWA_H, TW + 1], F32, part)
            gw = sb("gw", [33, 384], F32, part)
            blT = sb("blT", [33, S], F32, part)
            k_end = sb("k_end", [P, NT, 2, 384], F32, part)
            with ExitStack() as fox:
                pick = sb("pick", [80, FOX_H, S], BF16, fox)
            with ExitStack() as swa:
                bias_t = sb("bias_t", [P, SWA_H, S], F32, swa)
            g_dec = sb("g_dec", [GLA_K, 4], F32, part)
            qdT = sb("qdT", [GLA_K, 4, P], F32, part)
            state = sb("state", [GLA_K, 4, GLA_V], F32, part)
            g_sc = sb("g_sc", [P, P], F32, part)
            sbw = sb("sbw", [P, 4, 3 * P], F32, part)
        with ExitStack() as part:
            sb("beside_qk", [P, 1024], F32, part)
            sbz = sb("sbz", [P, 4, 3 * P], F32, part)
            sbt = sb("sbt", [P, 4, 3 * P], F32, part)
            sbb = sb("sbb", [P, 4, 3 * P], F32, part)
            sb1 = sb("sb1", [P, 4, 3 * P], F32, part)

        ps = ctx.enter_context(nc.psum_tensor("ps", [P, 8, 512], F32))
        ps_flat = ps[:].rearrange("p b n -> p (b n)")
        rel_rows = nc.dram_tensor("rel_rows", (SWA_H, P, TW + 1), F32, kind="Internal").ap()

        hid_rows = nc.dram_tensor("hid_rows", (4 * PEER_ROUNDS, P, NT * WIDE), F32, kind="Internal").ap()

        ident = fix[:, C_IDENT:C_IDENT + P]
        iota = fix[:, C_IOTA:C_IOTA + P]

        def KC(at, n=P):
            return kc[:, at:at + n]

        raw_loaded = [sem(f"raw_loaded{i}") for i in range(RING)]
        hi_made, lo_made, chunk_used = sem("hi_made"), sem("lo_made"), sem("chunk_used")
        copied_out, added_out = sem("copied_out"), sem("added_out")
        hid_turned, hid_full = sem("hid_turned"), sem("hid_full")
        hid_hi, hid_lo = sem("hid_hi"), sem("hid_lo")
        spilled, reloaded = sem("spilled"), sem("reloaded")
        fix_loaded, kc_loaded, x_loaded = sem("fix_loaded"), sem("kc_loaded"), sem("x_loaded")
        gain_loaded, small_loaded, stats_set = sem("gain_loaded"), sem("small_loaded"), sem("stats_set")
        rows_stored, bias_loaded = sem("rows_stored"), sem("bias_loaded")
        squared, var_made, rooted, normed = sem("squared"), sem("var_made"), sem("rooted"), sem("normed")
        x_turned, x_hi_made, x_lo_made = sem("x_turned"), sem("x_hi_made"), sem("x_lo_made")
        qk_turned, qk_copied, scored = sem("qk_turned"), sem("qk_copied"), sem("scored")
        max_made, exp_made, counted = sem("max_made"), sem("exp_made"), sem("counted")
        p_turned, p_copied, pv_made, head_out = sem("p_turned"), sem("p_copied"), sem("pv_made"), sem("head_out")
        gate_abs, gate_soft, gate_log = sem("gate_abs"), sem("gate_soft"), sem("gate_log")
        cum_made, cum_copied, roped = sem("cum_made"), sem("cum_copied"), sem("roped")
        pick_made, c_split = sem("pick_made"), sem("c_split")
        act_step, dve_step, pool_step = sem("act_step"), sem("dve_step"), sem("pool_step")
        masks_made, rel_ready, rel_made, row_copied = sem("masks_made"), sem("rel_ready"), sem("rel_made"), sem("row_copied")
        pq_turned, pq_copied, sc_made, sc_copied = sem("pq_turned"), sem("pq_copied"), sem("sc_made"), sem("sc_copied")
        gate_diff, gate_exp, chosen_made = sem("gate_diff"), sem("gate_exp"), sem("chosen_made")
        ch_turned, ch_copied = sem("ch_turned"), sem("ch_copied")
        one1_made, is2_made, one2_made, g_summed, g_copied = sem("one1_made"), sem("is2_made"), sem("one2_made"), sem("g_summed"), sem("g_copied")
        bl_turned, bl_copied, gpre_made = sem("bl_turned"), sem("bl_copied"), sem("gpre_made")
        gla_abs, gla_soft, gla_log = sem("gla_abs"), sem("gla_soft"), sem("gla_log")
        gla_sum, gla_exp, gla_ops = sem("gla_sum"), sem("gla_exp"), sem("gla_ops")
        gla_dec, gla_decexp = sem("gla_dec"), sem("gla_decexp")
        gt_made, gt_copied, gs_made, gs_masked = sem("gt_made"), sem("gt_copied"), sem("gs_made"), sem("gs_masked")
        gd_made, state_made, go_made, go_copied = sem("gd_made"), sem("state_made"), sem("go_made"), sem("go_copied")
        sb_abs, sb_soft, sb_log, sb_sum = sem("sb_abs"), sem("sb_soft"), sem("sb_log"), sem("sb_sum")
        sb_add, sb_exp, sb_w = sem("sb_add"), sem("sb_exp"), sem("sb_w")
        br_exp, mixed2 = sem("br_exp"), sem("mixed2")
        out_stored = sem("out_stored")

        sections = {}
        blocks = acts = adds = 0
        for name, nb, kind in (("in1", NB1, "act"), ("out1", 4, "add"), ("query", 4, "act"),
                               ("peer", 8 * PEER_ROUNDS, "both"),
                               ("in2", NB2, "act"), ("out2", 4, "add"), ("mlp", 8 * MLP_ROUNDS, "both")):
            sections[name] = (blocks, acts, adds, nb)
            blocks += nb
            acts += {"act": nb, "add": 0, "both": nb // 2}[kind]
            adds += {"act": 0, "add": nb, "both": nb // 2}[kind]
        all_blocks, all_acts, all_adds = blocks, acts, adds

        def after(name):
            b, x, y, nb = sections[name]
            kind = {"in1": (1, 0), "query": (1, 0), "in2": (1, 0), "out1": (0, 1), "out2": (0, 1)}.get(name, (.5, .5))
            return b + nb, x + int(nb * kind[0]), y + int(nb * kind[1])

        def bank(parity, t):
            return 2 * parity + t

        def over_blocks(eng, nb, block):
            block(0, 0)
            block(1, 1)
            if nb == 4:
                block(2, 0)
                block(3, 1)
            else:
                with eng.Fori(0, nb // 2 - 1) as i:
                    block(2 * i + 2, 0)
                    block(2 * i + 3, 1)

        GATES_AT = {0: 74, 1: 4}

        def batches_at(half, pos):
            return [m for m in range(32) if GATES_AT[half] + 3 * m // 2 == pos]

        def static(v):
            return isinstance(v, int)

        whole = [(0, D)]
        mix1_segs = [(0, 1024), (1024, 1024)]
        mix2_segs = [(0, 768)] + [(768 + GLA_V * i, GLA_V) for i in range(GLA_H)] + [(1536, 512)]
        norms = [(h, mix, whole), (mix, mix, mix1_segs), (h, mix, whole), (h, h, whole),
                 (h, mix, whole), (mix, mix, mix2_segs), (h, mix, whole), (h, h, whole)]

        block = ctx.enter_context(nc.Block())

        @block.sync
        def _(sp):
            def load(B, c, src):
                q = SUB * B + c
                if not static(q) or q >= RING:
                    sp.wait_ge(lo_made, q - RING + 1)
                n = src.shape[1] * src.shape[2]
                sp.dma_start(raw[:, c % RING, 0:n], src.rearrange("p k n -> p (k n)")).then_inc(raw_loaded[c % RING], 16)

            def gemm(name, w):
                b0, _, _, nb = sections[name]

                def blk(b, parity):
                    for c in range(SUB):
                        load(b0 + b, c, w[b, c])
                over_blocks(sp, nb, blk)

            def rounds(name, first_round, count, w_in, w_out):
                b0 = sections[name][0]

                def one(r):
                    for i in range(8):
                        for c in range(SUB):
                            w = w_in if i < 4 else w_out
                            load(b0 + 8 * r + i, c, w[4 * (first_round + r) + i % 4, c])
                one(0)
                with sp.Fori(1, count) as r:
                    one(r)

            gemm("in1", a["w_in"])
            gemm("out1", a["w_out"])
            gemm("query", a["peer_query"])
            b0 = sections["peer"][0]

            def phase(up, nd, nu):
                for i in range(4):
                    for c in range(SUB):
                        w = a["peer_up"][4 * nu + i, c] if up else a["peer_down"][4 * nd + i, c]
                        load(b0 + 4 * (nd + nu) + i, c, w)
            with sp.Fori(0, 4) as r:
                phase(False, r, 0)
            with sp.Fori(0, 2) as r:
                phase(True, r + 4, r)
                phase(False, r + 4, r + 1)
            with sp.Fori(0, 2) as r:
                phase(True, 6, r + 2)
            with sp.Fori(0, 2) as r:
                phase(False, r + 6, 4)
            with sp.Fori(0, 4) as r:
                phase(True, 8, r + 4)
            gemm("in2", a["w_in_2"])
            gemm("out2", a["w_out_2"])
            rounds("mlp", 0, MLP_ROUNDS, a["w_mlp_in_2"], a["w_mlp_out_2"])
            sp.wait_ge(normed, NT * len(norms))
            sp.dma_start(out[0].rearrange("(t p) d -> p t d", p=P), h[:]).then_inc(out_stored, 16)
            sp.wait_ge(out_stored, 16)

        @block.gpsimd
        def _(pool):
            steps = [0]

            def step(ins):
                steps[0] += 1
                ins.then_inc(pool_step, 1)
                pool.wait_ge(pool_step, steps[0])

            def spread(dst, row):
                return pool.dma_start(dst, row.partition_broadcast(P))

            pool.dma_start(fix[:], a["fix"]).then_inc(fix_loaded, 16)
            pool.dma_start(h[:], a["x"][0].rearrange("(t p) d -> p t d", p=P)).then_inc(x_loaded, 16)
            spread(gain, a["attn_norm_gain"][0]).then_inc(gain_loaded, 16)
            pool.dma_start(kc[:], a["kc"]).then_inc(kc_loaded, 16)
            spread(fbias[:], a["forget_bias"][0]).then_inc(small_loaded, 16)
            pool.wait_ge(fix_loaded, 16)
            nc.gpsimd.memset(pick[:], 0.0).then_inc(pick_made, 1)
            pool.wait_ge(pick_made, 1)
            for at in (0, 32, 64):
                nc.gpsimd.tensor_copy(pick[at:at + 16], fix[at:at + 16, C_IDENT + at:C_IDENT + at + 16].unsqueeze(2)
                                      .to_broadcast([16, FOX_H, S])).then_inc(pick_made, 1)
            pool.wait_ge(normed, NT * 1)
            spread(gain[:, 0:1024], a["fox_out_gain"][0]).then_inc(gain_loaded, 16)
            spread(gain[:, 1024:2048], a["dil_out_gain"][0]).then_inc(gain_loaded, 16)
            pool.wait_ge(normed, NT * 2)
            spread(gain, a["ffn_norm_gain"][0]).then_inc(gain_loaded, 16)
            pool.wait_ge(chunk_used, SUB * after("query")[0])
            pool.dma_start(skT, a["peer_sub_keys"]).then_inc(small_loaded, 16)

            for half in range(2):
                base = 32 * half

                def batch(n, slot, half=half, base=base):
                    pool.wait_ge(is2_made, base + n + 1)
                    at = bass.ds(8 * n, 8)
                    nc.gpsimd.tensor_tensor(
                        one2[:, slot], is2[:, slot],
                        chosenT[:, 2, at].unsqueeze(2).to_broadcast([P, 8, HALF_J]), ALU.mult).then_inc(one2_made, 1)
                with pool.Fori(0, 8) as i:
                    for slot in range(4):
                        batch(4 * i + slot, slot)

            pool.wait_ge(added_out, after("peer")[2])
            spread(gain, a["final_norm_gain"]).then_inc(gain_loaded, 16)
            pool.wait_ge(normed, NT * 4)
            spread(gain, a["norm_mix_2"][0]).then_inc(gain_loaded, 16)
            step(nc.gpsimd.memset(gw[:], 0.0))
            step(nc.gpsimd.memset(blT[:], 0.0))
            step(nc.gpsimd.memset(blT[32:33, :], 1.0))
            nc.gpsimd.memset(rel[32:33, :], 1.0).then_inc(rel_ready, 1)
            pool.dma_start(kc[:], a["kc"]).then_inc(kc_loaded, 16)
            pool.dma_start(rel[0:32, :], a["rel_bias_2"]).then_inc(small_loaded, 16)
            pool.dma_start(buck[:], a["buck"]).then_inc(small_loaded, 16)
            pool.dma_start(gw[0:GLA_R, :], a["gla_gate_w_2"][0]).then_inc(small_loaded, 16)
            pool.dma_start(gw[32:33, :], a["gla_gate_b_2"]).then_inc(small_loaded, 16)
            spread(sinks[:], a["swa_sinks_2"][0]).then_inc(small_loaded, 16)
            pool.wait_ge(row_copied, 1)
            for p in range(4):
                pool.dma_start(rel_rows[:, 32 * p:32 * p + 32, :],
                               relrow[:].unsqueeze(1).to_broadcast([SWA_H, 32, TW + 1])).then_inc(rows_stored, 16)
            pool.wait_ge(rows_stored, 64)
            sheared = rel_rows.rearrange("h q x -> h (q x)")[:, 127:127 + P * TW]
            sheared = sheared.rearrange("h (q x) -> q h x", x=TW)[:, :, 0:S]
            pool.dma_start(bias_t[:], sheared).then_inc(bias_loaded, 16)

            pool.wait_ge(normed, NT * 5)
            spread(gain[:, 0:768], a["swa_out_norm_2"][0]).then_inc(gain_loaded, 16)
            for i in range(GLA_H):
                spread(gain[:, 768 + GLA_V * i:768 + GLA_V * (i + 1)], a["gla_norm_2"][0]).then_inc(gain_loaded, 16)
            spread(gain[:, 1536:2048], a["sb_out_norm_2"][0]).then_inc(gain_loaded, 16)
            pool.wait_ge(normed, NT * 6)
            spread(gain, a["norm_mlp_2"][0]).then_inc(gain_loaded, 16)
            pool.wait_ge(normed, NT * 7)
            spread(last_gain, a["norm_final_2"]).then_inc(gain_loaded, 16)

        def split_hi(act, B, c, n):
            q = SUB * B + c
            act.wait_ge(raw_loaded[c % RING], 16 * (2 * B + c // RING + 1))
            if not static(q) or q >= RING:
                act.wait_ge(chunk_used, q - RING + 1)
            act.activation(w_hi[:, c % RING, 0:2 * n], raw[:, c % RING, 0:2 * n], ACT.Copy).then_inc(hi_made, 1)

        def split_lo(dve, B, c, n):
            q = SUB * B + c
            dve.wait_ge(hi_made, q + 1)
            nc.vector.tensor_tensor(w_lo[:, c % RING, 0:2 * n], raw[:, c % RING, 0:2 * n],
                                    w_hi[:, c % RING, 0:2 * n].bitcast(F32), ALU.subtract).then_inc(lo_made, 1)

        @block.scalar
        def _(act):
            steps = [0]

            def step(ins):
                steps[0] += 1
                ins.then_inc(act_step, 1)
                act.wait_ge(act_step, steps[0])

            def norm(k):
                src, _, segs = norms[k]
                if k in (0,):
                    act.wait_ge(x_loaded, 16)
                if k in (1,):
                    act.wait_ge(head_out, FOX_H + DIL_H)
                if k in (2, 3, 6, 7):
                    act.wait_ge(added_out, after({2: "out1", 3: "peer", 6: "out2", 7: "mlp"}[k])[2])
                if k == 4:
                    act.wait_ge(normed, NT * 4)
                if k == 5:
                    act.wait_ge(head_out, FOX_H + DIL_H + SWA_H + SB_H)
                    act.wait_ge(go_copied, GLA_H * NT)
                last = None
                for t in range(NT):
                    for n, (at, w) in enumerate(segs):
                        last = act.activation(ps_flat[:, t * D + at:t * D + at + w], src[:, t, at:at + w],
                                              ACT.Square, accum_out=stats[:, 0, t * 8 + n:t * 8 + n + 1])
                last.then_inc(squared, 1)
                act.wait_ge(var_made, k + 1)
                act.activation(stats[:, 2, :], stats[:, 1, :], ACT.Sqrt).then_inc(rooted, 1)

            def turn_hi(k):
                for g in range(8):
                    act.wait_ge(x_turned, 8 * k + g + 1)
                    act.activation(x_hi[:, 2 * g:2 * g + 2, :].rearrange("p k s -> p (k s)"), ps[:, 4 + g % 2, :],
                                   ACT.Copy).then_inc(x_hi_made, 1)

            def drain(B, parity, n, dst):
                act.wait_ge(chunk_used, SUB * (B + 1))
                for t in range(NT):
                    last = act.activation(dst(t), ps[:, bank(parity, t), 0:n], ACT.Copy)
                last.then_inc(copied_out, 1)

            def gemm(name, n, dst):
                b0, _, _, nb = sections[name]

                def place(b):
                    return lambda t: dst[:, t, bass.ds(b * n, n)]

                def blk(b, parity):
                    for c in range(SUB):
                        if c == 3 and dst is not None and not (static(b) and b == 0):
                            drain(b0 + b - 1, 1 - parity, n, place(b - 1))
                        split_hi(act, b0 + b, c, n)
                over_blocks(act, nb, blk)
                if dst is not None:
                    drain(b0 + nb - 1, 1, n, place(nb - 1))

            def rounds(name, h0, count, func):
                b0 = sections[name][0]

                def one(r):
                    for i in range(8):
                        B = b0 + 8 * r + i
                        for c in range(SUB):
                            if c == 3 and 1 <= i <= 4:
                                act.wait_ge(chunk_used, SUB * B)
                                before = h0 + 4 * r + i - 1
                                if not static(before) or before > 0:
                                    act.wait_ge(hid_turned, before)
                                for t in range(NT):
                                    last = act.activation(hid[:, t], ps[:, bank((i - 1) % 2, t), :], func)
                                last.then_inc(copied_out, 1)
                            split_hi(act, B, c, WIDE)
                            if c == 4 and 2 <= i <= 4:
                                split_hidden(r, i - 2)
                            if c == 7 and i == 4:
                                split_hidden(r, 3)

                def split_hidden(r, i):
                    pair = ps[:, 4 + 2 * (i % 2):6 + 2 * (i % 2), :].rearrange("p b n -> p (b n)")
                    act.wait_ge(hid_turned, h0 + 4 * r + i + 1)
                    act.activation(pair, pair, ACT.Square).then_inc(hid_full, 1)
                    act.wait_ge(hid_full, h0 + 4 * r + i + 1)
                    act.activation(a_hi[:, 4 * i:4 * i + 4, :].rearrange("p k s -> p (k s)"), pair,
                                   ACT.Copy).then_inc(hid_hi, 1)
                one(0)
                with act.Fori(1, count) as r:
                    one(r)

            def copy_qk(i):
                act.wait_ge(qk_turned, i + 1)
                if i >= 2:
                    act.wait_ge(scored, i - 1)
                act.activation(qkT[:, i % 2, :], ps[0:HD, 6 + i % 2, :], ACT.Copy).then_inc(qk_copied, 1)

            def exp_head(i, sink=None):
                act.wait_ge(max_made, i + 1)
                if i >= 2:
                    act.wait_ge(p_turned, i - 1)
                s = hs[:, i % 4]
                src, scale = (ps[:, 4 + i % 2], HD ** -0.5) if sink is None else (biased[:, i % 2], 1.0)
                act.activation(prob[:, i % 2, 0:P], src[:, 0:P], ACT.Exp, bias=s[:, 1, 0:1],
                               scale=scale, accum_out=s[:, 2, 0:1])
                last = act.activation(prob[:, i % 2, P:3 * P], src[:, P:3 * P], ACT.Exp, bias=s[:, 1, 1:2],
                                      scale=scale, accum_out=s[:, 2, 1:2])
                if sink is not None:
                    last = act.activation(s[:, 4, :], s[:, 1, :], ACT.Exp, bias=sink)
                last.then_inc(exp_made, 1)

            act.wait_ge(fix_loaded, 16)
            act.activation(ident_b[:], ident, ACT.Copy).then_inc(masks_made, 1)
            act.wait_ge(stats_set, 1)
            norm(0)
            turn_hi(0)
            gemm("in1", N1, proj1)
            act.wait_ge(gate_abs, 1)
            step(act.activation(fg[:, 2], fg[:, 1], ACT.Exp, scale=-1.0))
            act.activation(fg[:, 3], fg[:, 2], ACT.Ln, bias=1.0).then_inc(gate_soft, 1)
            act.wait_ge(cum_made, 1)
            act.activation(c8[:], ps[0:16, 0, 0:S], ACT.Copy, scale=8.0).then_inc(cum_copied, 1)
            for n in range(FOX_H + DIL_H + 1):
                if n < FOX_H + DIL_H:
                    copy_qk(n)
                if n >= 1:
                    exp_head(n - 1)
            norm(1)
            turn_hi(1)
            gemm("out1", WIDE, None)
            norm(2)
            turn_hi(2)
            gemm("query", WIDE, pq)

            for g in range(8):
                act.wait_ge(pq_turned, g + 1)
                act.activation(pqT[:, 2 * g:2 * g + 2, :].rearrange("p k s -> p (k s)"), ps[:, 4 + g % 2, :],
                               ACT.Copy).then_inc(pq_copied, 1)
            for n in range(8):
                t, g = n // 4, n % 4
                act.wait_ge(sc_made, n + 1)
                act.activation(sc[:, t, 4 * g:4 * g + 4, :].rearrange("p g n -> p (g n)"), ps[:, 6 + n % 2, :],
                               ACT.Copy).then_inc(sc_copied, 1)
            b0, c0, _, _ = sections["peer"]

            def spill(n):
                act.wait_ge(copied_out, c0 + n + 1)
                act.dma_start(hid_rows[n], hid.rearrange("p t n -> p (t n)")).then_inc(spilled, 16)

            def reload(n):
                act.wait_ge(spilled, 16 * (n + 1))
                if not static(n) or n > 0:
                    act.wait_ge(hid_turned, n)
                act.dma_start(back[:].rearrange("p t n -> p (t n)"), hid_rows[n]).then_inc(reloaded, 16)

            def split_gated(n, pair):
                act.wait_ge(hid_full, n + 1)
                act.activation(a_hi[:, 4 * pair[0]:4 * pair[0] + 4, :].rearrange("p k s -> p (k s)"),
                               ps[:, pair[1]:pair[1] + 2, :].rearrange("p b n -> p (b n)"), ACT.Copy).then_inc(hid_hi, 1)

            def copy_gates(half, n):
                act.wait_ge(g_summed, 32 * half + n + 1)
                act.activation(gates_w[:, 8 * HALF_J * n:8 * HALF_J * (n + 1)], ps[:, 6 + n % 2, :], ACT.Copy).then_inc(g_copied, 1)

            def phase(up, nd, nu, prev_up, fill_next, extra=None, more=True):
                for i in range(4):
                    for c in range(SUB):
                        if c == 3 and not (prev_up if i == 0 else up) and not (static(nd) and nd == 0 and i == 0):
                            n = 4 * nd + i - 1
                            act.wait_ge(chunk_used, SUB * (b0 + 4 * (nd + nu) + i))
                            if not static(n) or n > 0:
                                act.wait_ge(spilled, 16 * n)
                            for t in range(NT):
                                last = act.activation(hid[:, t], ps[:, bank((i - 1) % 2, t), :], ACT.Gelu_apprx_tanh)
                            last.then_inc(copied_out, 1)
                            spill(n)
                        split_hi(act, b0 + 4 * (nd + nu) + i, c, WIDE)
                        if i == 3 and fill_next:
                            f = 4 * (nu + 1 if up else nu)
                            if c == 5:
                                reload(f + 1)
                            if c == 6:
                                split_gated(f, (0, 4))
                            if c == 7:
                                reload(f + 2)
                        if i == 0 and up:
                            f = 4 * nu
                            if c == 0:
                                split_gated(f + 1, (1, 6))
                            if c == 1:
                                reload(f + 3)
                            if c == 2:
                                split_gated(f + 2, (2, 4))
                            if c == 3 and more:
                                reload(f + 4)
                            if c == 4:
                                split_gated(f + 3, (3, 6))
                        if extra:
                            extra(SUB * i + c)

            def beside(base, half):
                def extra(pos):
                    pos += base
                    if half == 0 and pos == 12:
                        reload(0)
                    if half == 0 and pos == 56:
                        act.wait_ge(gate_diff, 1)
                        act.activation(big[:, 1536:1792], big[:, 1536:1792], ACT.Exp).then_inc(gate_exp, 1)
                    if half == 0 and pos == 71:
                        act.wait_ge(ch_turned, 3)
                        for s in range(3):
                            act.activation(chosenT[:, s, :], ps[:, 4 + s // 2, S * (s % 2):S * (s % 2) + S], ACT.Copy).then_inc(ch_copied, 1)
                    for n in batches_at(half, pos - 4):
                        copy_gates(half, n)
                return extra

            for r in range(4):
                phase(False, r, 0, False, r == 3, beside(32 * r, 0))
            with act.Fori(0, 2) as r:
                phase(True, r + 4, r, False, False)
                phase(False, r + 4, r + 1, True, True)
            phase(True, 6, 2, False, True)
            phase(True, 6, 3, True, False)
            for r in range(2):
                phase(False, 6 + r, 4, r == 0, r == 1, beside(32 * r, 1))
            phase(True, 8, 4, False, True)
            with act.Fori(0, 2) as r:
                phase(True, 8, r + 5, True, True)
            phase(True, 8, 7, True, False, more=False)
            norm(3)

            act.wait_ge(rel_made, 1)
            act.activation(relrow[:], ps[0:SWA_H, 0, 0:TW + 1], ACT.Copy).then_inc(row_copied, 1)
            act.wait_ge(row_copied, 1)
            norm(4)
            turn_hi(3)
            gemm("in2", N2, proj2)
            for n in range(FOX_H + DIL_H, FOX_H + DIL_H + SWA_H + 1):
                if n < FOX_H + DIL_H + SWA_H:
                    copy_qk(n)
                if n > FOX_H + DIL_H:
                    i = n - 1 - FOX_H - DIL_H
                    exp_head(n - 1, sinks[:, i:i + 1])
            act.wait_ge(bl_turned, 1)
            act.wait_ge(pool_step, 3)
            act.activation(blT[0:GLA_R, :], ps[0:GLA_R, 0, 0:S], ACT.Copy).then_inc(bl_copied, 1)
            for t in range(NT):
                act.wait_ge(gla_abs, t + 1)
                step(act.activation(k_inv[:, t], g_log[:, t], ACT.Exp, scale=-1.0))
                act.activation(q_dec[:, t], k_inv[:, t], ACT.Ln, bias=1.0).then_inc(gla_soft, 1)
            for t in range(NT):
                act.wait_ge(gla_sum, t + 1)
                act.activation(q_dec[:, t], ps[:, 0, 0:384], ACT.Exp)
                act.activation(k_inv[:, t], ps[:, 0, 0:384], ACT.Exp, scale=-1.0).then_inc(gla_exp, 1)
                act.wait_ge(gla_ops, 2 * t + 1)
                act.activation(k_end[:, t, 1], k_end[:, t, 0], ACT.Exp).then_inc(gla_exp, 1)
            for hh in range(GLA_H):
                act.wait_ge(gla_dec, hh + 1)
                act.activation(g_dec[:], ps[0:GLA_K, 0, 0:4], ACT.Exp).then_inc(gla_decexp, 1)
                for t in range(NT):
                    n = NT * hh + t
                    act.wait_ge(gt_made, n + 1)
                    act.activation(qdT[:, 2:4, :].rearrange("p a s -> p (a s)"), ps[0:GLA_K, 1, 0:S], ACT.Copy).then_inc(gt_copied, 1)
                    act.wait_ge(go_made, n + 1)
                    act.activation(mix[:, t, 768 + GLA_V * hh:768 + GLA_V * (hh + 1)], ps[:, 4, 0:GLA_V],
                                   ACT.Copy).then_inc(go_copied, 1)
            first = FOX_H + DIL_H + SWA_H
            for n in range(SB_H + 4):
                if n < SB_H:
                    copy_qk(first + n)
                if 1 <= n <= SB_H:
                    i = n - 1
                    act.wait_ge(sb_abs, i + 1)
                    step(act.activation(sbt[:, i % 4], sbt[:, i % 4], ACT.Exp, scale=-1.0))
                    act.activation(sbt[:, i % 4], sbt[:, i % 4], ACT.Ln, bias=1.0).then_inc(sb_soft, 1)
                if 3 <= n <= SB_H + 2:
                    i = n - 3
                    act.wait_ge(sb_add, i + 1)
                    act.activation(sbw[:, i % 4], sbb[:, i % 4], ACT.Exp).then_inc(sb_exp, 1)
            norm(5)
            for t in range(NT):
                act.activation(proj2[:, t, BQ:BQ + 768], proj2[:, t, BR:BR + 768], ACT.Exp, scale=-1.0).then_inc(br_exp, 1)
            turn_hi(4)
            gemm("out2", WIDE, None)
            norm(6)
            turn_hi(5)
            rounds("mlp", 4 * PEER_ROUNDS, MLP_ROUNDS, ACT.Relu)
            norm(7)

        @block.vector
        def _(dve):
            V = nc.vector
            steps = [0]

            def step(ins):
                steps[0] += 1
                ins.then_inc(dve_step, 1)
                dve.wait_ge(dve_step, steps[0])

            gains_due = [16, 48, 64, 80, 96, 192, 208, 224]

            def norm(k):
                src, dst, segs = norms[k]
                dve.wait_ge(squared, k + 1)
                if len(segs) == 1:
                    V.tensor_scalar(stats[:, 1, :], stats[:, 0, :], 1.0 / D, EPS, ALU.mult, ALU.add).then_inc(var_made, 1)
                elif len(segs) == 2:
                    V.tensor_scalar(stats[:, 1, :], stats[:, 0, :], 1.0 / 1024, EPS, ALU.mult, ALU.add).then_inc(var_made, 1)
                else:
                    var, ssq = (stats[:, n].rearrange("p (t n) -> p t n", t=NT) for n in (1, 0))
                    V.tensor_scalar(var[:, :, 0:1], ssq[:, :, 0:1], 1.0 / 768, EPS, ALU.mult, ALU.add)
                    V.tensor_scalar(var[:, :, 5:6], ssq[:, :, 5:6], 1.0 / 512, EPS, ALU.mult, ALU.add)
                    V.tensor_scalar(var[:, :, 1:5], ssq[:, :, 1:5], 1.0 / GLA_V, EPS, ALU.mult, ALU.add).then_inc(var_made, 1)
                dve.wait_ge(rooted, k + 1)
                step(V.reciprocal(stats[:, 3, :], stats[:, 2, :]))
                dve.wait_ge(gain_loaded, gains_due[k])
                for t in range(NT):
                    for n, (at, w) in enumerate(segs):
                        last = V.scalar_tensor_tensor(out=dst[:, t, at:at + w], in0=src[:, t, at:at + w],
                                                      scalar=stats[:, 3, t * 8 + n:t * 8 + n + 1],
                                                      in1=(last_gain if k == 7 else gain)[:, at:at + w], op0=ALU.mult, op1=ALU.mult)
                    last.then_inc(normed, 1)
                dve.wait_ge(normed, NT * (k + 1))

            def turn_lo(k):
                for g in range(8):
                    dve.wait_ge(x_hi_made, 8 * k + g + 1)
                    V.tensor_tensor(x_lo[:, 2 * g:2 * g + 2, :].rearrange("p k s -> p (k s)"), ps[:, 4 + g % 2, :],
                                    x_hi[:, 2 * g:2 * g + 2, :].rearrange("p k s -> p (k s)").bitcast(F32),
                                    ALU.subtract).then_inc(x_lo_made, 1)

            def add_block(B, parity, at):
                dve.wait_ge(chunk_used, SUB * (B + 1))
                for t in range(NT):
                    last = V.tensor_tensor(h[:, t, at * WIDE:(at + 1) * WIDE], ps[:, bank(parity, t), :],
                                           h[:, t, at * WIDE:(at + 1) * WIDE], ALU.add)
                last.then_inc(added_out, 1)

            def gemm(name, n, adds):
                b0, _, _, nb = sections[name]

                def blk(b, parity):
                    for c in range(SUB):
                        if c == 3 and adds and b > 0:
                            add_block(b0 + b - 1, 1 - parity, b - 1)
                        split_lo(dve, b0 + b, c, n)
                over_blocks(dve, nb, blk)
                if adds:
                    add_block(b0 + nb - 1, 1, nb - 1)

            def rounds(name, h0, count):
                b0 = sections[name][0]

                def rest(r, i):
                    dve.wait_ge(hid_hi, h0 + 4 * r + i + 1)
                    pair = ps[:, 4 + 2 * (i % 2):6 + 2 * (i % 2), :].rearrange("p b n -> p (b n)")
                    V.tensor_tensor(a_lo[:, 4 * i:4 * i + 4, :].rearrange("p k s -> p (k s)"), pair,
                                    a_hi[:, 4 * i:4 * i + 4, :].rearrange("p k s -> p (k s)").bitcast(F32),
                                    ALU.subtract).then_inc(hid_lo, 1)

                def one(r, first):
                    for i in range(8):
                        B = b0 + 8 * r + i
                        for c in range(SUB):
                            if c == 3 and (i >= 5 or (i == 0 and not first)):
                                add_block(B - 1, (i - 1) % 2, (i - 5) % 4 if i else 3)
                            split_lo(dve, B, c, WIDE)
                            if c == 4 and 2 <= i <= 4:
                                rest(r, i - 2)
                            if c == 7 and i == 4:
                                rest(r, 3)
                one(0, True)
                with dve.Fori(1, count) as r:
                    one(r, False)
                add_block(b0 + 8 * count - 1, 1, 3)

            def max_head(i):
                dve.wait_ge(scored, i + 1)
                if i >= 4:
                    dve.wait_ge(head_out, i - 3)
                s, src = hs[:, i % 4], ps[:, 4 + i % 2]
                V.reduce_max(s[:, 0, 0:1], src[:, 0:P], AX)
                step(V.reduce_max(s[:, 0, 1:2], src[:, P:3 * P], AX))
                V.tensor_scalar(s[:, 1, :], s[:, 0, :], -(HD ** -0.5), None, ALU.mult).then_inc(max_made, 1)

            def max_swa(i):
                j = i - FOX_H - DIL_H
                dve.wait_ge(scored, i + 1)
                dve.wait_ge(head_out, i - 3)
                s, src, dst = hs[:, i % 4], ps[:, 4 + i % 2], biased[:, i % 2]
                V.scalar_tensor_tensor(out=dst[:, 0:P], in0=src[:, 0:P], scalar=HD ** -0.5, in1=bias_t[:, j, P:2 * P],
                                       op0=ALU.mult, op1=ALU.add)
                step(V.scalar_tensor_tensor(out=dst[:, P:3 * P], in0=src[:, P:3 * P], scalar=HD ** -0.5,
                                            in1=bias_t[:, j, :], op0=ALU.mult, op1=ALU.add))
                V.reduce_max(s[:, 0, 0:1], dst[:, 0:P], AX)
                step(V.reduce_max(s[:, 0, 1:2], dst[:, P:3 * P], AX))
                V.tensor_scalar(s[:, 1, :], s[:, 0, :], sinks[:, j:j + 1], -1.0, ALU.max, ALU.mult).then_inc(max_made, 1)

            def count_head(i):
                dve.wait_ge(exp_made, i + 1)
                s = hs[:, i % 4]
                for n, (at, w) in enumerate(((0, P), (P, 2 * P))):
                    last = V.tensor_tensor_reduce(prob[:, i % 2, at:at + w], prob[:, i % 2, at:at + w],
                                                  KC(K_COUNT + at, w), 1.0, 0.0, ALU.mult, ALU.add, s[:, 2, n:n + 1])
                last.then_inc(counted, 1)

            def copy_p(i):
                dve.wait_ge(p_turned, i + 1)
                if i >= 2:
                    dve.wait_ge(pv_made, i - 1)
                V.tensor_copy(probT[:, i % 2, :], ps[:, i % 2, 0:3 * P]).then_inc(p_copied, 1)

            def out_head(i, at, sink=False):
                s = hs[:, i % 4]
                dve.wait_ge(pv_made, i + 1)
                if sink:
                    step(V.tensor_tensor(s[:, 2, :], s[:, 2, :], s[:, 4, :], ALU.add))
                step(V.reciprocal(s[:, 3, :], s[:, 2, :]))
                for t in range(NT):
                    last = V.tensor_scalar(mix[:, t, at:at + HD], ps[:, 2 + i % 2, HD * t:HD * t + HD],
                                           s[:, 3, t:t + 1], None, ALU.mult)
                last.then_inc(head_out, 1)

            V.memset(stats[:], 1.0).then_inc(stats_set, 1)
            norm(0)
            turn_lo(0)
            gemm("in1", N1, False)
            dve.wait_ge(copied_out, after("in1")[1])
            dve.wait_ge(small_loaded, 16)
            step(V.tensor_tensor(fg[:, 0], proj1[:, :, FG:FG + 16], fbias[:].unsqueeze(1).to_broadcast([P, NT, 16]), ALU.add))
            step(V.tensor_scalar(fg[:, 1], fg[:, 0], -1.0, None, ALU.mult))
            V.tensor_tensor(fg[:, 1], fg[:, 1], fg[:, 0], ALU.max).then_inc(gate_abs, 1)
            dve.wait_ge(gate_soft, 1)
            V.scalar_tensor_tensor(out=fg[:, 0], in0=fg[:, 0], scalar=0.0, in1=fg[:, 3], op0=ALU.min,
                                   op1=ALU.subtract).then_inc(gate_log, 1)
            step(V.memset(c_parts[:], 0.0))
            dve.wait_ge(kc_loaded, 16)
            V.tensor_copy(mask_b[:], KC(K_MASK, 3 * P)).then_inc(masks_made, 1)
            dve.wait_ge(cum_copied, 1)
            step(V.tensor_copy(c_parts[0:16, 0], c8[:]))
            step(V.tensor_tensor(c_rest[:], c8[:], c_parts[0:16, 0], ALU.subtract))
            step(V.tensor_copy(c_mid[:], c_rest[:]))
            V.tensor_copy(c_parts[32:48, 0], c_mid[:])
            step(V.tensor_tensor(c8[:], c_rest[:], c_mid[:], ALU.subtract))
            step(V.tensor_copy(c_parts[64:80, 0], c8[:]))
            V.tensor_scalar(c_parts[:, 1], c_parts[:, 0], -1.0, None, ALU.mult).then_inc(c_split, 1)
            for t in range(NT):
                qk = proj1[:, t, DQ:DQ + 2 * 1024].rearrange("p (n d) -> p n d", d=HD)
                x1, x2 = qk[:, :, 0:8], qk[:, :, 8:16]
                cos = KC(K_COS + 8 * t, 8).unsqueeze(1).to_broadcast([P, 32, 8])
                sin = KC(K_SIN + 8 * t, 8).unsqueeze(1).to_broadcast([P, 32, 8])
                V.tensor_tensor(rope[:, 0], x1, cos, ALU.mult)
                V.tensor_tensor(rope[:, 1], x2, sin, ALU.mult)
                V.tensor_tensor(rope[:, 2], x2, cos, ALU.mult)
                step(V.tensor_tensor(rope[:, 3], x1, sin, ALU.mult))
                V.tensor_tensor(x1, rope[:, 0], rope[:, 1], ALU.subtract)
                V.tensor_tensor(x2, rope[:, 2], rope[:, 3], ALU.add).then_inc(roped, 1)
                dve.wait_ge(roped, t + 1)
            for n in range(1, FOX_H + DIL_H + 3):
                if n <= FOX_H + DIL_H:
                    max_head(n - 1)
                if 2 <= n <= FOX_H + DIL_H + 1:
                    copy_p(n - 2)
                if n >= 3:
                    i = n - 3
                    out_head(i, HD * i)
                if FOX_H < n <= FOX_H + DIL_H:
                    count_head(n - 1)
            norm(1)
            turn_lo(1)
            gemm("out1", WIDE, True)
            norm(2)
            turn_lo(2)
            gemm("query", WIDE, False)

            def best(v, i, vals, work):
                step(V.max(v[:, 0:8], vals))
                V.max_index(i[:, 0:8].bitcast(U32), v[:, 0:8], vals)
                step(V.match_replace(work, v[:, 0:8], vals, -3.0e38))
                step(V.max(v[:, 8:16], work))
                step(V.max_index(i[:, 8:16].bitcast(U32), v[:, 8:16], work))

            def best_keys(t, g):
                if g % 4 == 0:
                    dve.wait_ge(sc_copied, 4 * t + g // 4 + 1)
                best(top_v[:, t, g], top_i[:, t, g], sc[:, t, g, :], scr[:, 0:NKEY])

            def all_sums(t):
                sums = cand.rearrange("p (g a b) -> p g a b", g=PH, a=TOPK)
                for g in range(PH):
                    last = V.tensor_tensor(sums[:, g], top_v[:, t, 2 * g].unsqueeze(2).to_broadcast([P, TOPK, TOPK]),
                                           top_v[:, t, 2 * g + 1].unsqueeze(1).to_broadcast([P, TOPK, TOPK]), ALU.add)
                step(last)

            def best_pairs(t, g):
                best(best_v[:, t, g], best_c[:, t, g], cand[:, 256 * g:256 * g + 256], scr)

            bv = big[:, 1536:1792].rearrange("p (g k) -> p g k", k=TOPK)

            def ranks():
                step(V.tensor_copy(big[:, 1024:1536], big[:, 512:1024].bitcast(U32)))
                code = big[:, 1792:2048].bitcast(U32)
                step(V.tensor_scalar(ranku.bitcast(U32), code, 4, None, ALU.logical_shift_right))
                step(V.tensor_copy(big[:, 2048:2304], ranku.bitcast(U32)))
                step(V.tensor_scalar(ranku.bitcast(U32), code, 15, None, ALU.bitwise_and))
                step(V.tensor_copy(big[:, 2304:2560], ranku.bitcast(U32)))
                step(V.tensor_copy(gsum[:, 0, :].unsqueeze(2), bv[:, :, 0:1]))
                V.tensor_tensor(bv, bv, gsum[:, 0, :].unsqueeze(2).to_broadcast([P, 16, TOPK]), ALU.subtract).then_inc(gate_diff, 1)

            def look_up(s, t, part):
                hot = cand.rearrange("p (n k) -> p n k", k=TOPK)
                if part == 0:
                    step(V.tensor_tensor(hot, rank[:, s, t].unsqueeze(2).to_broadcast([P, P, TOPK]),
                                         iota[:, 0:TOPK].unsqueeze(1).to_broadcast([P, P, TOPK]), ALU.is_equal))
                if part == 1:
                    for g in range(PH):
                        hg = hot[:, TOPK * g:TOPK * g + TOPK, :]
                        last = V.tensor_tensor(hg, hg, top_f[:, t, 2 * g + s].unsqueeze(1).to_broadcast([P, TOPK, TOPK]), ALU.mult)
                    step(last)
                if part == 2:
                    step(V.tensor_reduce(chosen[:, s, t], hot, AX, ALU.add))

            def softmax_gates():
                dve.wait_ge(gate_exp, 1)
                step(V.tensor_reduce(gsum[:, 0, :], bv, AX, ALU.add))
                step(V.reciprocal(gsum[:, 1, :], gsum[:, 0, :]))
                V.tensor_tensor(chosen[:, 2].rearrange("p t (g k) -> p (t g) k", k=TOPK), bv,
                                gsum[:, 1, :].unsqueeze(2).to_broadcast([P, 16, TOPK]), ALU.mult).then_inc(chosen_made, 1)

            def search(pos):
                if pos < 32:
                    best_keys(pos // 16, pos % 16)
                elif pos < 50:
                    t, g = divmod(pos - 32, 9)
                    all_sums(t) if g == 0 else best_pairs(t, g - 1)
                elif pos == 50:
                    ranks()
                elif pos < 63:
                    n = pos - 51
                    look_up(n // 6, n // 3 % 2, n % 3)
                elif pos == 63:
                    softmax_gates()

            def batch(half, n):
                if half == 0 and n == 0:
                    dve.wait_ge(ch_copied, 3)
                if half == 1 and n == 0:
                    dve.wait_ge(chunk_used, SUB * (b0 + 40))
                if half or n >= 4:
                    dve.wait_ge(g_summed, 32 * half + n - 3)
                at = slice(8 * n, 8 * n + 8)
                V.tensor_tensor(one1[:, n % 4], iota.unsqueeze(1).to_broadcast([P, 8, P]),
                                chosenT[:, 0, at].unsqueeze(2).to_broadcast([P, 8, P]), ALU.is_equal).then_inc(one1_made, 1)
                V.tensor_tensor(is2[:, n % 4],
                                iota[:, HALF_J * half:HALF_J * half + HALF_J].unsqueeze(1).to_broadcast([P, 8, HALF_J]),
                                chosenT[:, 1, at].unsqueeze(2).to_broadcast([P, 8, HALF_J]), ALU.is_equal).then_inc(is2_made, 1)

            b0 = sections["peer"][0]

            def fill(n, g, local):
                dve.wait_ge(hid_turned, n + 1)
                pair = ps[:, 4 + 2 * (g % 2):6 + 2 * (g % 2), :].rearrange("p b (k s) -> p (b k) s", s=S)
                V.tensor_tensor(pair, pair, gates[:, bass.ds(16 * local + 4 * g, 4), :], ALU.mult).then_inc(hid_full, 1)

            def rest(n, g):
                dve.wait_ge(hid_hi, n + 1)
                pair = ps[:, 4 + 2 * (g % 2):6 + 2 * (g % 2), :].rearrange("p b n -> p (b n)")
                V.tensor_tensor(a_lo[:, 4 * g:4 * g + 4, :].rearrange("p k s -> p (k s)"), pair,
                                a_hi[:, 4 * g:4 * g + 4, :].rearrange("p k s -> p (k s)").bitcast(F32),
                                ALU.subtract).then_inc(hid_lo, 1)

            def phase(up, nd, nu, prev_up, fill_next, half, extra=None):
                for i in range(4):
                    B = b0 + 4 * (nd + nu) + i
                    for c in range(SUB):
                        if c == 3 and (prev_up if i == 0 else up):
                            add_block(B - 1, (i - 1) % 2, (i - 1) % 4)
                        split_lo(dve, B, c, WIDE)
                        if i == 3 and fill_next:
                            f = nu + 1 if up else nu
                            if c == 5:
                                fill(4 * f, 0, f - 4 * half)
                            if c == 6:
                                rest(4 * f, 0)
                            if c == 7:
                                fill(4 * f + 1, 1, f - 4 * half)
                        if i == 0 and up:
                            if c == 0:
                                rest(4 * nu + 1, 1)
                            if c == 1:
                                fill(4 * nu + 2, 2, nu - 4 * half)
                            if c == 2:
                                rest(4 * nu + 2, 2)
                            if c == 3:
                                fill(4 * nu + 3, 3, nu - 4 * half)
                            if c == 4:
                                rest(4 * nu + 3, 3)
                        if extra:
                            extra(SUB * i + c)

            def beside(base, half):
                def extra(pos):
                    pos += base
                    if half == 0:
                        search(pos)
                    for n in batches_at(half, pos):
                        batch(half, n)
                    if half == 0 and pos == 124 or half == 1 and pos == 60:
                        dve.wait_ge(g_copied, 32 * half + 32)
                return extra

            for r in range(4):
                phase(False, r, 0, False, r == 3, 0, beside(32 * r, 0))
            with dve.Fori(0, 2) as r:
                phase(True, r + 4, r, False, False, 0)
                phase(False, r + 4, r + 1, True, True, 0)
            phase(True, 6, 2, False, True, 0)
            phase(True, 6, 3, True, False, 0)
            for r in range(2):
                phase(False, 6 + r, 4, r == 0, r == 1, 1, beside(32 * r, 1))
            phase(True, 8, 4, False, True, 1)
            with dve.Fori(0, 2) as r:
                phase(True, 8, r + 5, True, True, 1)
            phase(True, 8, 7, True, False, 1)
            add_block(b0 + 63, 1, 3)
            norm(3)

            norm(4)
            turn_lo(3)
            gemm("in2", N2, False)
            dve.wait_ge(copied_out, after("in2")[1])
            dve.wait_ge(kc_loaded, 32)
            V.tensor_copy(mask_b[:], KC(K_MASK, 3 * P)).then_inc(masks_made, 1)
            dve.wait_ge(small_loaded, 16 * 7)
            dve.wait_ge(bias_loaded, 16)
            i0, i1 = FOX_H + DIL_H, FOX_H + DIL_H + SWA_H
            for n in range(i0 + 1, i1 + 3):
                if n <= i1:
                    max_swa(n - 1)
                if i0 + 2 <= n <= i1 + 1:
                    copy_p(n - 2)
                if n >= i0 + 3:
                    out_head(n - 3, HD * (n - 3 - i0), True)
            for t in range(NT):
                dve.wait_ge(gpre_made, t + 1)
                step(V.tensor_copy(q_dec[:, t], ps[:, 1 + t, 0:384]))
                step(V.tensor_scalar(g_log[:, t], q_dec[:, t], -1.0, None, ALU.mult))
                V.tensor_tensor(g_log[:, t], g_log[:, t], q_dec[:, t], ALU.max).then_inc(gla_abs, 1)
                dve.wait_ge(gla_soft, t + 1)
                step(V.scalar_tensor_tensor(out=g_tmp[:], in0=ps[:, 1 + t, 0:384], scalar=0.0, in1=q_dec[:, t],
                                            op0=ALU.min, op1=ALU.subtract))
                V.tensor_scalar(g_log[:, t], g_tmp[:], 1.0 / 16.0, -1.0, ALU.mult, ALU.max).then_inc(gla_log, 1)
            for t in range(NT):
                dve.wait_ge(gla_exp, 2 * t + 1)
                step(V.tensor_copy(g_tmp[:], ps[:, 1, 0:384]))
                V.tensor_tensor(k_end[:, t, 0], g_tmp[:], ps[:, 0, 0:384], ALU.subtract).then_inc(gla_ops, 1)
                step(V.scalar_tensor_tensor(out=q_dec[:, t], in0=q_dec[:, t], scalar=GLA_K ** -0.5,
                                            in1=proj2[:, t, BQ:BQ + 384], op0=ALU.mult, op1=ALU.mult))
                step(V.tensor_tensor(k_inv[:, t], k_inv[:, t], proj2[:, t, BK:BK + 384], ALU.mult))
                dve.wait_ge(gla_exp, 2 * t + 2)
                step(V.tensor_tensor(g_tmp[:], k_end[:, t, 1], proj2[:, t, BK:BK + 384], ALU.mult))
                step(V.tensor_scalar(k_end[:, t, 0], g_tmp[:], KC(K_HALF, 1), None, ALU.mult))
                V.tensor_scalar(k_end[:, t, 1], g_tmp[:], KC(K_HALF + 1, 1), None, ALU.mult).then_inc(gla_ops, 1)
            for hh in range(GLA_H):
                dve.wait_ge(gla_decexp, hh + 1)
                if hh == 0:
                    step(V.memset(qdT[:, 0:2, :], 0.0))
                for t in range(NT):
                    n = NT * hh + t
                    dve.wait_ge(gt_copied, n + 1)
                    V.tensor_copy(qdT[:, 0, 0:64], qdT[:, 2, 0:64])
                    V.tensor_copy(qdT[:, 1, 64:128], qdT[:, 2, 64:128])
                    dve.wait_ge(gs_made, n + 1)
                    V.tensor_tensor(g_sc[:], ps[:, 2, 0:P], KC(K_GTRI), ALU.mult).then_inc(gs_masked, 1)
                    dve.wait_ge(gd_made, n + 1)
                    if t == 0:
                        step(V.tensor_copy(state[:, 1], ps[0:GLA_K, 3, 0:GLA_V]))
                        V.scalar_tensor_tensor(out=state[:, 2], in0=state[:, 1], scalar=g_dec[:, 1:2],
                                               in1=ps[0:GLA_K, 3, GLA_V:2 * GLA_V], op0=ALU.mult,
                                               op1=ALU.add).then_inc(state_made, 1)
                    else:
                        V.scalar_tensor_tensor(out=state[:, 3], in0=state[:, 2], scalar=g_dec[:, 2:3],
                                               in1=ps[0:GLA_K, 3, 0:GLA_V], op0=ALU.mult,
                                               op1=ALU.add).then_inc(state_made, 1)
                    dve.wait_ge(go_made, n + 1)
            for n in range(1, SB_H + 6):
                if n <= SB_H:
                    i = n - 1
                    g = i1 + i
                    dve.wait_ge(scored, g + 1)
                    if i >= 4:
                        dve.wait_ge(pv_made, g - 3)
                    V.tensor_scalar(sbz[:, i % 4], ps[:, 4 + g % 2, 0:3 * P], HD ** -0.5, None, ALU.mult)
                    step(V.tensor_scalar(sbt[:, i % 4], ps[:, 4 + g % 2, 0:3 * P], -(HD ** -0.5), None, ALU.mult))
                    V.tensor_tensor(sbt[:, i % 4], sbt[:, i % 4], sbz[:, i % 4], ALU.max).then_inc(sb_abs, 1)
                if 3 <= n <= SB_H + 2:
                    i = n - 3
                    dve.wait_ge(sb_sum, i + 1)
                    V.tensor_tensor(sbb[:, i % 4], ps[:, i % 2, 0:3 * P], sbb[:, i % 4], ALU.add).then_inc(sb_add, 1)
                if 2 <= n <= SB_H + 1:
                    i = n - 2
                    dve.wait_ge(sb_soft, i + 1)
                    step(V.scalar_tensor_tensor(out=sbb[:, i % 4], in0=sbz[:, i % 4], scalar=0.0, in1=sbt[:, i % 4],
                                                op0=ALU.min, op1=ALU.subtract))
                    step(V.tensor_tensor(sb1[:, i % 4], sbb[:, i % 4], sbz[:, i % 4], ALU.subtract))
                    V.tensor_tensor(sb1[:, i % 4, 0:P], sb1[:, i % 4, 0:P], KC(K_STRICT), ALU.mult)
                    V.tensor_tensor(sb1[:, i % 4, 2 * P:3 * P], sb1[:, i % 4, 2 * P:3 * P], KC(K_STRICT),
                                    ALU.mult).then_inc(sb_log, 1)
                if 4 <= n <= SB_H + 3:
                    i = n - 4
                    dve.wait_ge(sb_exp, i + 1)
                    V.tensor_tensor(sbw[:, i % 4, 0:P], sbw[:, i % 4, 0:P], KC(K_STRICT), ALU.mult)
                    V.tensor_tensor(sbw[:, i % 4, 2 * P:3 * P], sbw[:, i % 4, 2 * P:3 * P], KC(K_STRICT),
                                    ALU.mult).then_inc(sb_w, 1)
                if n >= 6:
                    i = n - 6
                    g = i1 + i
                    dve.wait_ge(pv_made, g + 1)
                    for t in range(NT):
                        last = V.tensor_copy(mix[:, t, 1536 + HD * i:1536 + HD * i + HD], ps[:, 2 + g % 2, HD * t:HD * t + HD])
                    last.then_inc(head_out, 1)
            norm(5)
            for t in range(NT):
                dve.wait_ge(br_exp, t + 1)
                e, r = proj2[:, t, BQ:BQ + 768], proj2[:, t, BR:BR + 768]
                step(V.tensor_scalar(e, e, 1.0, None, ALU.add))
                step(V.reciprocal(e, e))
                step(V.tensor_tensor(e, e, r, ALU.mult))
                V.tensor_tensor(mix[:, t, 768:1536], mix[:, t, 768:1536], e, ALU.mult).then_inc(mixed2, 1)
            turn_lo(4)
            gemm("out2", WIDE, True)
            norm(6)
            turn_lo(5)
            rounds("mlp", 4 * PEER_ROUNDS, MLP_ROUNDS)
            norm(7)

        @block.tensor
        def _(pe):
            mm = pe.matmul

            def turn(k, due):
                due()
                for g in range(8):
                    if g >= 2 or k > 0:
                        pe.wait_ge(x_lo_made, 8 * k + g - 1)
                    for kk in range(2):
                        for t in range(NT):
                            at = 2 * g + kk
                            last = pe.transpose(ps[:, 4 + g % 2, kk * S + t * P:kk * S + t * P + P],
                                                mix[:, t, at * P:at * P + P], ident)
                    last.then_inc(x_turned, 1)

            def chunk(B, parity, c, n, hi, lo):
                pe.wait_ge(lo_made, SUB * B + c + 1)
                for kk in range(2):
                    k = 2 * c + kk
                    wh = w_hi[:, c % RING, kk * n:kk * n + n]
                    wl = w_lo[:, c % RING, kk * n:kk * n + n]
                    for t in range(NT):
                        o = ps[:, bank(parity, t), 0:n]
                        xh, xl = hi[:, k, t * P:t * P + P], lo[:, k, t * P:t * P + P]
                        mm(o, xh, wh, start=(k == 0), stop=False)
                        mm(o, xh, wl, start=False, stop=False)
                        last = mm(o, xl, wh, start=False, stop=(k == KT - 1))
                last.then_inc(chunk_used, 1)

            def gemm(name, k, n, kind):
                b0, acts, adds, nb = sections[name]
                pe.wait_ge(x_lo_made, 8 * k + 8)
                sem_, base = (copied_out, acts) if kind == "act" else (added_out, adds)

                def blk(b, parity):
                    if not static(b) or b >= 2:
                        pe.wait_ge(sem_, base + b - 1)
                    for c in range(SUB):
                        chunk(b0 + b, parity, c, n, x_hi, x_lo)
                over_blocks(pe, nb, blk)

            def rounds(name, h0, count):
                b0, acts, adds, _ = sections[name]

                def turn_hidden(r, i):
                    pe.wait_ge(copied_out, acts + 4 * r + i + 1)
                    free = h0 + 4 * r + i - 1
                    if not static(free) or free > 0:
                        pe.wait_ge(hid_lo, free)
                    for jj in range(4):
                        for t in range(NT):
                            last = pe.transpose(ps[:, 4 + 2 * (i % 2) + jj // 2, (jj % 2) * S + t * P:(jj % 2) * S + t * P + P],
                                                hid[:, t, jj * P:jj * P + P], ident)
                    last.then_inc(hid_turned, 1)

                def one(r, first):
                    for i in range(8):
                        if i < 2 and first:
                            pe.wait_ge(copied_out, acts)
                            pe.wait_ge(added_out, adds)
                        elif 2 <= i < 6:
                            pe.wait_ge(copied_out, acts + 4 * r + i - 1)
                        else:
                            pe.wait_ge(added_out, adds + 4 * r + (i - 5 if i >= 6 else i - 1))
                        for c in range(SUB):
                            if i == 4 and c % 2 == 0:
                                if c == 4:
                                    turn_hidden(r, 3)
                                pe.wait_ge(hid_lo, h0 + 4 * r + c // 2 + 1)
                            chunk(b0 + 8 * r + i, i % 2, c, WIDE, x_hi if i < 4 else a_hi, x_lo if i < 4 else a_lo)
                        if 1 <= i < 4:
                            turn_hidden(r, i - 1)
                one(0, True)
                with pe.Fori(1, count) as r:
                    one(r, False)

            def turn_qk(i, src, q, k):
                if i >= 2:
                    pe.wait_ge(qk_copied, i - 1)
                for n, at in enumerate((q, k)):
                    for t in range(NT):
                        last = pe.transpose(ps[0:HD, 6 + i % 2, n * S + t * P:n * S + t * P + P], src[:, t, at:at + HD], ident)
                last.then_inc(qk_turned, 1)

            def score(i, fox=None, masked=True):
                pe.wait_ge(qk_copied, i + 1)
                if i >= 2:
                    pe.wait_ge(exp_made, i - 1)
                o, q, k = ps[:, 4 + i % 2], qkT[:, i % 2, 0:S], qkT[:, i % 2, S:2 * S]
                for t, at, w in ((0, 0, P), (1, P, S)):
                    o_t = o[:, at:at + w]
                    last = mm(o_t, q[:, t * P:t * P + P], k[:, 0:w], start=True, stop=not (masked or fox is not None))
                    if fox is not None:
                        mm(o_t, c_parts[:, 0, t * P:t * P + P], pick[:, fox, 0:w], start=False, stop=False)
                        mm(o_t, pick[:, fox, 0:P], c_parts[:, 1, 0:w], start=False, stop=False)
                        last = mm(o[:, at + w - P:at + w], ident_b[:], caus, start=False, stop=True)
                    elif masked:
                        last = mm(o_t, ident_b[:], mask_b[:, at:at + w], start=False, stop=True)
                last.then_inc(scored, 1)

            def turn_p(i, due, count):
                pe.wait_ge(due, count)
                if i >= 2:
                    pe.wait_ge(p_copied, i - 1)
                for b in range(3):
                    last = pe.transpose(ps[:, i % 2, b * P:b * P + P], prob[:, i % 2, b * P:b * P + P], ident)
                last.then_inc(p_turned, 1)

            def pv(i, due, count, pT, v0, v1):
                pe.wait_ge(due, count)
                if i >= 2:
                    pe.wait_ge(head_out, i - 1)
                o = ps[:, 2 + i % 2]
                mm(o[:, 0:HD], pT[:, 0:P], v0, start=True, stop=True)
                mm(o[:, HD:2 * HD], pT[:, P:2 * P], v0, start=True, stop=False)
                mm(o[:, HD:2 * HD], pT[:, 2 * P:3 * P], v1, start=False, stop=True).then_inc(pv_made, 1)

            pe.wait_ge(fix_loaded, 16)
            turn(0, lambda: pe.wait_ge(normed, NT * 1))
            gemm("in1", 0, N1, "act")
            pe.wait_ge(gate_log, 1)
            lf = fg[:, 0]
            mm(ps[0:16, 0, 0:P], lf[:, 0, :], KC(K_UTRI), start=True, stop=True)
            mm(ps[0:16, 0, P:S], lf[:, 0, :], KC(K_ONES), start=True, stop=False)
            mm(ps[0:16, 0, P:S], lf[:, 1, :], KC(K_UTRI), start=False, stop=True).then_inc(cum_made, 1)
            pe.wait_ge(cum_copied, 1)
            pe.wait_ge(masks_made, 2)
            pe.wait_ge(c_split, 1)
            pe.wait_ge(pick_made, 4)
            caus = mask_b[:, 0:P]
            pe.wait_ge(roped, NT)
            heads = FOX_H + DIL_H
            for n in range(heads + 3):
                if n < heads:
                    f = n < FOX_H
                    m = n if f else n - FOX_H
                    turn_qk(n, proj1, (FQ if f else DQ) + HD * m, (FK if f else DK) + HD * m)
                if 1 <= n <= heads:
                    score(n - 1, n - 1 if n - 1 < FOX_H else None)
                if 2 <= n <= heads + 1:
                    i = n - 2
                    if i < FOX_H:
                        turn_p(i, exp_made, i + 1)
                    else:
                        turn_p(i, counted, i - FOX_H + 1)
                if n >= 3:
                    i = n - 3
                    at = FV + HD * i if i < FOX_H else DV + HD * (i - FOX_H)
                    pv(i, p_copied, i + 1, probT[:, i % 2], proj1[:, 0, at:at + HD], proj1[:, 1, at:at + HD])
            turn(1, lambda: pe.wait_ge(normed, NT * 2))
            gemm("out1", 1, WIDE, "add")
            turn(2, lambda: pe.wait_ge(normed, NT * 3))
            gemm("query", 2, WIDE, "act")

            pe.wait_ge(copied_out, after("query")[1])
            for g in range(8):
                if g >= 2:
                    pe.wait_ge(pq_copied, g - 1)
                for kk in range(2):
                    for t in range(NT):
                        at = 2 * g + kk
                        last = pe.transpose(ps[:, 4 + g % 2, kk * S + t * P:kk * S + t * P + P], pq[:, t, at * P:at * P + P], ident)
                last.then_inc(pq_turned, 1)
            pe.wait_ge(pq_copied, 8)
            pe.wait_ge(small_loaded, 32)
            for n in range(8):
                t, g = n // 4, n % 4
                if n >= 2:
                    pe.wait_ge(sc_copied, n - 1)
                for j in range(4):
                    last = mm(ps[:, 6 + n % 2, j * P:j * P + P], pqT[:, 4 * g + j, t * P:t * P + P], skT[:, 4 * g + j, :],
                              start=True, stop=True)
                last.then_inc(sc_made, 1)
            pe.wait_ge(sc_copied, 8)
            b0, c0, d0, _ = sections["peer"]

            def turn_chosen():
                pe.wait_ge(chosen_made, 1)
                for s in range(3):
                    for t in range(NT):
                        last = pe.transpose(ps[:, 4 + s // 2, S * (s % 2) + t * P:S * (s % 2) + t * P + P], chosen[:, s, t], ident)
                    last.then_inc(ch_turned, 1)

            def batch(half, n):
                pe.wait_ge(one1_made, 32 * half + n + 1)
                pe.wait_ge(one2_made, 32 * half + n + 1)
                if half == 1 and n == 0:
                    pe.wait_ge(hid_lo, 16)
                if half or n >= 2:
                    pe.wait_ge(g_copied, 32 * half + n - 1)
                for j in range(8):
                    last = mm(ps[:, 6 + n % 2, HALF_J * j:HALF_J * (j + 1)], one1[:, n % 4, j, :], one2[:, n % 4, j, :],
                              start=True, stop=True)
                last.then_inc(g_summed, 1)

            def turn_back(n, g):
                pe.wait_ge(reloaded, 16 * (n + 1))
                if not static(n) or n >= 2:
                    pe.wait_ge(hid_lo, n - 1)
                for jj in range(4):
                    for t in range(NT):
                        last = pe.transpose(ps[:, 4 + 2 * (g % 2) + jj // 2, (jj % 2) * S + t * P:(jj % 2) * S + t * P + P],
                                            back[:, t, jj * P:jj * P + P], ident)
                last.then_inc(hid_turned, 1)

            def phase(up, nd, nu, prev_up, fill_next, extra=None):
                for i in range(4):
                    if (prev_up if i < 2 else up):
                        pe.wait_ge(added_out, d0 + 4 * nu + i - 1)
                    elif static(nd) and nd == 0 and i < 2:
                        pe.wait_ge(copied_out, c0)
                    else:
                        pe.wait_ge(copied_out, c0 + 4 * nd + i - 1)
                    for c in range(SUB):
                        if up and i == 0 and c % 2 == 0:
                            pe.wait_ge(hid_lo, 4 * nu + c // 2 + 1)
                        chunk(b0 + 4 * (nd + nu) + i, i % 2, c, WIDE, a_hi if up else x_hi, a_lo if up else x_lo)
                        if i == 3 and fill_next and c % 2:
                            turn_back(4 * (nu + 1 if up else nu) + c // 2, c // 2)
                        if extra:
                            extra(SUB * i + c)

            def beside(base, half):
                def extra(pos):
                    pos += base
                    if half == 0 and pos == 67:
                        turn_chosen()
                    for n in batches_at(half, pos + 1):
                        batch(half, n)
                    if half == 0 and pos == 122 or half == 1 and pos == 58:
                        pe.wait_ge(g_copied, 32 * half + 32)
                return extra

            for r in range(4):
                phase(False, r, 0, False, r == 3, beside(32 * r, 0) if r > 1 else None)
            with pe.Fori(0, 2) as r:
                phase(True, r + 4, r, False, False)
                phase(False, r + 4, r + 1, True, True)
            phase(True, 6, 2, False, True)
            phase(True, 6, 3, True, False)
            for r in range(2):
                phase(False, 6 + r, 4, r == 0, r == 1, beside(32 * r, 1))
            phase(True, 8, 4, False, True)
            with pe.Fori(0, 2) as r:
                phase(True, 8, r + 5, True, True)
            phase(True, 8, 7, True, False)

            pe.wait_ge(rel_ready, 1)
            pe.wait_ge(small_loaded, 16 * 7)
            mm(ps[0:SWA_H, 0, 0:TW + 1], rel[:], buck[:], start=True, stop=True).then_inc(rel_made, 1)
            turn(3, lambda: pe.wait_ge(normed, NT * 5))
            gemm("in2", 3, N2, "act")
            pe.wait_ge(copied_out, after("in2")[1])
            pe.wait_ge(masks_made, 3)
            i0, i1 = heads, heads + SWA_H
            for n in range(i0, i1 + 3):
                if n < i1:
                    m = n - i0
                    turn_qk(n, proj2, AQ + HD * m, AK + HD * (m // SWA_G))
                if i0 + 1 <= n <= i1:
                    score(n - 1, None, False)
                if i0 + 2 <= n <= i1 + 1:
                    turn_p(n - 2, exp_made, n - 1)
                if n >= i0 + 3:
                    i = n - 3
                    at = AV + HD * ((i - i0) // SWA_G)
                    pv(i, p_copied, i + 1, probT[:, i % 2], proj2[:, 0, at:at + HD], proj2[:, 1, at:at + HD])
            pe.wait_ge(head_out, i1)
            for t in range(NT):
                last = pe.transpose(ps[0:GLA_R, 0, t * P:t * P + P], proj2[:, t, BL:BL + GLA_R], ident)
            last.then_inc(bl_turned, 1)
            pe.wait_ge(bl_copied, 1)
            pe.wait_ge(pool_step, 3)
            for t in range(NT):
                mm(ps[:, 1 + t, 0:384], blT[:, t * P:t * P + P], gw[:], start=True, stop=True).then_inc(gpre_made, 1)
            pe.wait_ge(gla_log, NT)
            for t in range(NT):
                if t:
                    pe.wait_ge(gla_ops, 2 * t)
                mm(ps[:, 0, 0:384], KC(K_GTRI), g_log[:, t], start=True, stop=True)
                mm(ps[:, 1, 0:384], KC(K_GBLK), g_log[:, t], start=True, stop=True).then_inc(gla_sum, 1)
            pe.wait_ge(gla_ops, 2 * NT)
            for hh in range(GLA_H):
                c0 = GLA_K * hh
                if hh:
                    pe.wait_ge(gla_decexp, hh)
                for t in range(NT):
                    last = mm(ps[0:GLA_K, 0, 2 * t:2 * t + 2], g_log[:, t, c0:c0 + GLA_K], KC(K_HALF, 2), start=True, stop=True)
                last.then_inc(gla_dec, 1)
                for t in range(NT):
                    n = NT * hh + t
                    v = proj2[:, t, BV + GLA_V * hh:BV + GLA_V * (hh + 1)]
                    pe.transpose(ps[0:GLA_K, 1, 0:P], q_dec[:, t, c0:c0 + GLA_K], ident)
                    pe.transpose(ps[0:GLA_K, 1, P:S], k_inv[:, t, c0:c0 + GLA_K], ident).then_inc(gt_made, 1)
                    if n:
                        pe.wait_ge(state_made, n)
                    for c in range(2):
                        last = mm(ps[0:GLA_K, 3, GLA_V * c:GLA_V * (c + 1)], k_end[:, t, c, c0:c0 + GLA_K], v, start=True, stop=True)
                    last.then_inc(gd_made, 1)
                    pe.wait_ge(gt_copied, n + 1)
                    mm(ps[:, 2, 0:P], qdT[:, 3, :], qdT[:, 2, :], start=True, stop=True).then_inc(gs_made, 1)
                    pe.wait_ge(gs_masked, n + 1)
                    pe.wait_ge(state_made, n + 1)
                    if n:
                        pe.wait_ge(go_copied, n)
                    o = ps[:, 4, 0:GLA_V]
                    mm(o, g_sc[:], v, start=True, stop=False)
                    if t:
                        mm(o, qdT[:, 0, :], state[:, 2], start=False, stop=False)
                    last = mm(o, qdT[:, 1, :], state[:, 1 if t == 0 else 3], start=False, stop=True)
                    last.then_inc(go_made, 1)
            pe.wait_ge(go_copied, GLA_H * NT)
            for n in range(SB_H + 6):
                g = i1 + n
                if n < SB_H:
                    turn_qk(g, proj2, CQ + HD * n, CK + HD * n)
                if 1 <= n <= SB_H:
                    i = n - 1
                    g = i1 + i
                    pe.wait_ge(qk_copied, g + 1)
                    if i >= 2:
                        pe.wait_ge(sb_abs, i - 1)
                    o, q, k = ps[:, 4 + g % 2], qkT[:, g % 2, 0:S], qkT[:, g % 2, S:2 * S]
                    mm(o[:, 0:S], k[:, 0:P], q, start=True, stop=True)
                    mm(o[:, S:3 * P], k[:, P:S], q[:, P:S], start=True, stop=True).then_inc(scored, 1)
                if 3 <= n <= SB_H + 2:
                    i = n - 3
                    pe.wait_ge(sb_log, i + 1)
                    if i >= 2:
                        pe.wait_ge(sb_add, i - 1)
                    o, l1 = ps[:, i % 2], sb1[:, i % 4]
                    mm(o[:, 0:P], KC(K_SUF), l1[:, 0:P], start=True, stop=True)
                    mm(o[:, P:S], KC(K_SUF), l1[:, P:S], start=True, stop=False)
                    mm(o[:, P:S], KC(K_ONES), l1[:, S:3 * P], start=False, stop=True)
                    mm(o[:, S:3 * P], KC(K_SUF), l1[:, S:3 * P], start=True, stop=True).then_inc(sb_sum, 1)
                if 5 <= n <= SB_H + 4:
                    i = n - 5
                    at = CV + HD * i
                    pv(i1 + i, sb_w, i + 1, sbw[:, i % 4], proj2[:, 0, at:at + HD], proj2[:, 1, at:at + HD])
            turn(4, lambda: pe.wait_ge(mixed2, NT))
            gemm("out2", 4, WIDE, "add")
            turn(5, lambda: pe.wait_ge(normed, NT * 7))
            pe.wait_ge(x_lo_made, 48)
            rounds("mlp", 4 * PEER_ROUNDS, MLP_ROUNDS)


def blocks_of(w, n):
    k, m = w.shape
    return w.reshape(k // 256, 2, P, m // n, n).transpose(3, 0, 2, 1, 4)


def kernel(**inputs):
    import concourse.bacc as _bacc
    from concourse.bass_utils import run_bass_kernel_spmd as _run

    w = {k: np.asarray(v) for k, v in inputs.items()}
    arrays = {
        "w_in": blocks_of(w["w_in"][0], N1),
        "w_out": blocks_of(w["w_out"][0], WIDE),
        "peer_query": blocks_of(w["peer_query"][0], WIDE),
        "peer_down": w["peer_down"][0].reshape(P, 32, 4, SUB, 2, P).transpose(1, 3, 5, 4, 2, 0).reshape(32, SUB, P, 2, WIDE),
        "peer_up": w["peer_up"][0].reshape(P, 8, SUB, 2, 4, WIDE).transpose(1, 4, 2, 0, 3, 5).reshape(32, SUB, P, 2, WIDE),
        "w_in_2": blocks_of(w["w_in_2"][0], N2),
        "w_out_2": blocks_of(w["w_out_2"][0], WIDE),
        "w_mlp_in_2": blocks_of(w["w_mlp_in_2"][0], WIDE),
        "w_mlp_out_2": w["w_mlp_out_2"][0].reshape(4, SUB, 2, P, 4, WIDE).transpose(0, 4, 1, 3, 2, 5).reshape(16, SUB, P, 2, WIDE),
        "peer_sub_keys": w["peer_sub_keys"][0].reshape(16, NKEY, P).transpose(2, 0, 1),
        "fix": fixed_constants(), "kc": attention_constants(), "buck": bucket_constants(),
    }
    for name in ("x", "attn_norm_gain", "forget_bias", "fox_out_gain", "dil_out_gain", "ffn_norm_gain", "final_norm_gain",
                 "norm_mix_2", "swa_sinks_2", "rel_bias_2", "gla_gate_w_2", "gla_gate_b_2", "gla_norm_2", "swa_out_norm_2",
                 "sb_out_norm_2", "norm_mlp_2", "norm_final_2"):
        arrays[name] = w[name]
    nc = _bacc.Bacc("TRN2", target_bir_lowering=False, num_devices=1)
    maps, aps = {}, {}
    for name, v in arrays.items():
        maps[f"in_{name}"] = v = np.ascontiguousarray(v)
        aps[name] = nc.dram_tensor(f"in_{name}", v.shape, mybir.dt.from_np(v.dtype), kind="ExternalInput").ap()
    out = nc.dram_tensor("out_0", (1, S, D), F32, kind="ExternalOutput").ap()
    build(nc, aps, out)
    return _run(nc, [maps], core_ids=[0]).results[0]["out_0"]
```

```python
from contextlib import ExitStack

import numpy as np

import concourse.bass as bass
from concourse import mybir

ALU = mybir.AluOpType
ACT = mybir.ActivationFunctionType
F32 = mybir.dt.float32
F32R = mybir.dt.float32r
BF16 = mybir.dt.bfloat16
U32 = mybir.dt.uint32
AX = mybir.AxisListType.X

P = 128
S = 256
NT = S // P
NQ = 4
D = 2048
KT = D // P
HD = 64
EPS = 1e-6
NEG = -1e30

SUB = 8
RING = 4
WIDE = 512

IN1 = 6160
FQ, FK, FV, FG, DQ, DK, DV = 0, 1024, 2048, 3072, 3088, 4112, 5136
FOX_H = DIL_H = 16
IN2 = 5136
BQ, BK, BV, BL, AQ, AK, AV, BR, CQ, CK, CV = 0, 384, 768, 1536, 1552, 2320, 2576, 2832, 3600, 4112, 4624
SWA_H, SWA_G = 12, 3
GLA_H, GLA_K, GLA_V, GLA_R = 4, 96, 192, 16
SB_H = 8

PH, TOPK, NKEY = 8, 16, 128
HALF_J = 64

N1, NB1 = 440, 14
N2, NB2 = 428, 12
PEER_ROUNDS, MLP_ROUNDS = 8, 4

C_IDENT, C_IOTA = 0, 128
K_UTRI, K_ONES, K_SUF, K_GTRI, K_GBLK, K_COS, K_SIN, K_HALF, K_MASK, K_COUNT, K_STRICT = (
    0, 128, 256, 384, 512, 640, 656, 672, 674, 1058, 1442)
K_COLS = 1570
TW = 383


def fixed_constants():
    out = np.zeros((P, 256), np.float32)
    out[:, C_IDENT:C_IDENT + P] = np.eye(P)
    out[:, C_IOTA:C_IOTA + P] = np.arange(P)
    return out


def attention_constants():
    i, j = np.arange(P)[:, None], np.arange(P)[None, :]
    out = np.zeros((P, K_COLS), np.float32)
    out[:, K_UTRI:K_UTRI + P] = i <= j
    out[:, K_ONES:K_ONES + P] = 1
    out[:, K_SUF:K_SUF + P] = i > j
    same = i // 64 == j // 64
    out[:, K_GTRI:K_GTRI + P] = same & (i <= j)
    out[:, K_GBLK:K_GBLK + P] = same
    inv = (np.float32(500000.0) ** (-np.arange(0, 16, 2, dtype=np.float32) / np.float32(16))).astype(np.float32)
    for t in range(NT):
        ang = (np.arange(P, dtype=np.float32)[:, None] + t * P) * inv[None]
        out[:, K_COS + 8 * t:K_COS + 8 * t + 8] = np.cos(ang)
        out[:, K_SIN + 8 * t:K_SIN + 8 * t + 8] = np.sin(ang)
    out[:64, K_HALF] = 1
    out[64:, K_HALF + 1] = 1
    for n, (qt, kt) in enumerate(((0, 0), (1, 0), (1, 1))):
        q, k = qt * P + i, kt * P + j
        dist = q - k
        count = (dist >= 0) * ((dist <= 128) * 1.0 + (dist % 4 == 0) + (dist % 16 == 0))
        out[:, K_MASK + n * P:K_MASK + n * P + P] = np.where(count > 0, 0, NEG)
        out[:, K_COUNT + n * P:K_COUNT + n * P + P] = count
    out[:, K_STRICT:K_STRICT + P] = i < j
    return out


def bucket_constants():
    out = np.zeros((33, TW + 1), np.float32)
    for x in range(TW):
        dist = 255 - x
        if not 0 <= dist < 128:
            out[32, x] = NEG
            continue
        if dist < 16:
            b = dist
        else:
            ratio = np.float32(np.log(np.float32(dist) / np.float32(16))) / np.float32(np.log(8.0))
            b = min(16 + int(np.float32(ratio * np.float32(16))), 31)
        out[b, x] = 1
    return out


def build(nc, a, out):
    ctx = ExitStack()
    with ctx:
        def sb(name, shape, dt=F32, stack=ctx):
            return stack.enter_context(nc.sbuf_tensor(name, shape, dt))

        def sem(name):
            return ctx.enter_context(nc.semaphore(name))

        raw = sb("raw", [P, RING, 2 * WIDE])
        w_hi = sb("w_hi", [P, RING, 2 * WIDE], F32R)
        w_lo = sb("w_lo", [P, RING, 2 * WIDE], F32R)
        h = sb("h", [P, NT, D])
        fix = sb("fix", [P, 256])
        ident_b = sb("ident_b", [P, P], BF16)
        back = sb("back", [P, NT, WIDE])
        stats = sb("stats", [P, 4, 16])
        big = sb("big", [P, 18464])
        proj1 = big[:, 0:NT * IN1].rearrange("p (t n) -> p t n", t=NT)
        proj2 = big[:, 0:NT * IN2].rearrange("p (t n) -> p t n", t=NT)
        mix = big[:, 12320:16416].rearrange("p (t n) -> p t n", t=NT)
        gain = big[:, 16416:18464]
        g_log = big[:, 10272:11040].rearrange("p (t n) -> p t n", t=NT)
        q_dec = big[:, 11040:11808].rearrange("p (t n) -> p t n", t=NT)
        qdT = big[0:GLA_K, 11808:12320].rearrange("p (a s) -> p a s", a=4)
        state = mix[0:GLA_K, 0, 0:4 * GLA_V].rearrange("p (a n) -> p a n", a=4)
        g_tmp = mix[:, :, 1536:1536 + 384]
        back_flat = back[:].rearrange("p t n -> p (t n)")
        k_inv = back_flat[:, 0:768].rearrange("p (t n) -> p t n", t=NT)
        g_sc = back_flat[:, 768:896]
        g_dec = back_flat[0:GLA_K, 896:896 + 4 * GLA_H]
        last_gain = big[:, 0:D]
        pq = big[:, 0:4096].rearrange("p (t n) -> p t n", t=NT)
        pqT = big[:, 4096:8192].rearrange("p (g s) -> p g s", g=16)
        skT = big[:, 8192:10240].rearrange("p (g n) -> p g n", g=16)
        sc = big[:, 10240:14336].rearrange("p (t g n) -> p t g n", t=NT, g=16)
        cand = big[:, 14336:16384]
        top_v = big[:, 0:512].rearrange("p (t g k) -> p t g k", t=NT, g=16)
        top_i = big[:, 512:1024].rearrange("p (t g k) -> p t g k", t=NT, g=16)
        top_f = big[:, 1024:1536].rearrange("p (t g k) -> p t g k", t=NT, g=16)
        best_v = big[:, 1536:1792].rearrange("p (t g k) -> p t g k", t=NT, g=PH)
        best_c = big[:, 1792:2048].rearrange("p (t g k) -> p t g k", t=NT, g=PH)
        rank = big[:, 2048:2560].rearrange("p (s t n) -> p s t n", s=2, t=NT)
        ranku = big[:, 2560:2816]
        chosen = big[:, 2816:3584].rearrange("p (s t n) -> p s t n", s=3, t=NT)
        gsum = big[:, 3584:3616].rearrange("p (s n) -> p s n", s=2)
        scr = big[:, 3616:3872]
        chosenT = big[:, 16416:17184].rearrange("p (s n) -> p s n", s=3)
        gates = big[:, 0:S * HALF_J].rearrange("p (s j) -> p j s", j=HALF_J)
        gates_w = big[:, 0:S * HALF_J]
        hid = big[:, 17184:18208].rearrange("p (t n) -> p t n", t=NT)

        with ExitStack() as part:
            x_hi = sb("x_hi", [P, KT, S], F32R, part)
            x_lo = sb("x_lo", [P, KT, S], F32R, part)
            a_hi = sb("a_hi", [P, KT, S], F32R, part)
            a_lo = sb("a_lo", [P, KT, S], F32R, part)
        with ExitStack() as part:
            gain3 = sb("gain3", [P, D], F32, part)
            sb("between", [P, D], F32, part)
            sb("between2", [P, D], F32, part)
            gain4 = sb("gain4", [P, D], F32, part)
        with ExitStack() as part:
            sb("beside", [P, 2 * KT * S], F32, part)
            one1 = sb("one1", [P, 4, 8, P], BF16, part)
            is2 = sb("is2", [P, 4, 8, HALF_J], BF16, part)
            one2 = sb("one2", [P, 4, 3, 8, HALF_J], BF16, part)
            gate_b = sb("gate_b", [P, 3, S], BF16, part)
            index_b = sb("index_b", [P, 2, S], BF16, part)
            iota_b = sb("iota_b", [P, P], BF16, part)
            gate_left = sb("gate_left", [P, S], F32, part)
        with ExitStack() as part:
            qkT = sb("qkT", [HD, 2, 2 * S], F32, part)
            prob = sb("prob", [P, 2, 3 * P], F32, part)
            probT = sb("probT", [P, 2, 3 * P], F32, part)
            hs = sb("hs", [P, 4, 5, 2], F32, part)
            fg = sb("fg", [P, 4, 2, 16], F32, part)
            c8 = sb("c8", [16, S], F32, part)
            c_rest = sb("c_rest", [16, S], F32, part)
            c_mid = sb("c_mid", [16, S], BF16, part)
            c_parts = sb("c_parts", [80, 2, S], BF16, part)
            rope = sb("rope", [P, 4, 32, 8], F32, part)
            biased = sb("biased", [P, 2, 3 * P], F32, part)
        with ExitStack() as part:
            sb("beside_x", [P, 2 * KT * S], F32, part)
            kc = sb("kc", [P, K_COLS], F32, part)
            mask_b = sb("mask_b", [P, 3 * P], BF16, part)
            fbias = sb("fbias", [P, 16], F32, part)
            sinks = sb("sinks", [P, SWA_H], F32, part)
            buck = sb("buck", [33, TW + 1], F32, part)
            rel = sb("rel", [33, SWA_H], F32, part)
            relrow = sb("relrow", [SWA_H, TW + 1], F32, part)
            gw = sb("gw", [33, 384], F32, part)
            blT = sb("blT", [33, S], F32, part)
            k_end = sb("k_end", [P, NT, 2, 384], F32, part)
            with ExitStack() as fox:
                pick = sb("pick", [80, FOX_H, S], BF16, fox)
            with ExitStack() as swa:
                bias_t = sb("bias_t", [P, SWA_H, S], F32, swa)
            sbw = sb("sbw", [P, 4, 3 * P], F32, part)
        with ExitStack() as part:
            sb("beside_qk", [P, 1024], F32, part)
            sbz = sb("sbz", [P, 4, 3 * P], F32, part)
            sbt = sb("sbt", [P, 4, 3 * P], F32, part)
            sbb = sb("sbb", [P, 4, 3 * P], F32, part)
            sb1 = sb("sb1", [P, 4, 3 * P], F32, part)

        ps = ctx.enter_context(nc.psum_tensor("ps", [P, 8, 512], F32))
        ps_flat = ps[:].rearrange("p b n -> p (b n)")
        rel_rows = nc.dram_tensor("rel_rows", (SWA_H, P, TW + 1), F32, kind="Internal").ap()

        hid_rows = nc.dram_tensor("hid_rows", (4 * PEER_ROUNDS, P, NT * WIDE), F32, kind="Internal").ap()

        ident = fix[:, C_IDENT:C_IDENT + P]
        iota = fix[:, C_IOTA:C_IOTA + P]

        def KC(at, n=P):
            return kc[:, at:at + n]

        raw_loaded = [sem(f"raw_loaded{i}") for i in range(RING)]
        hi_made, lo_made, chunk_used = sem("hi_made"), sem("lo_made"), sem("chunk_used")
        copied_out, added_out = sem("copied_out"), sem("added_out")
        hid_turned, hid_full = sem("hid_turned"), sem("hid_full")
        hid_hi, hid_lo = sem("hid_hi"), sem("hid_lo")
        spilled, reloaded = sem("spilled"), sem("reloaded")
        fix_loaded, kc_loaded, x_loaded = sem("fix_loaded"), sem("kc_loaded"), sem("x_loaded")
        gain_loaded, small_loaded, stats_set = sem("gain_loaded"), sem("small_loaded"), sem("stats_set")
        rows_stored, bias_loaded = sem("rows_stored"), sem("bias_loaded")
        squared, var_made, rooted, normed = sem("squared"), sem("var_made"), sem("rooted"), sem("normed")
        x_turned, x_hi_made, x_lo_made = sem("x_turned"), sem("x_hi_made"), sem("x_lo_made")
        qk_turned, qk_copied, scored = sem("qk_turned"), sem("qk_copied"), sem("scored")
        max_made, exp_made, counted = sem("max_made"), sem("exp_made"), sem("counted")
        p_turned, p_copied, pv_made, head_out = sem("p_turned"), sem("p_copied"), sem("pv_made"), sem("head_out")
        gate_abs, gate_soft, gate_log = sem("gate_abs"), sem("gate_soft"), sem("gate_log")
        cum_made, cum_copied, roped = sem("cum_made"), sem("cum_copied"), sem("roped")
        pick_made, c_split = sem("pick_made"), sem("c_split")
        act_step, dve_step, pool_step = sem("act_step"), sem("dve_step"), sem("pool_step")
        masks_made, rel_ready, rel_made, row_copied = sem("masks_made"), sem("rel_ready"), sem("rel_made"), sem("row_copied")
        pq_turned, pq_copied, sc_made, sc_copied = sem("pq_turned"), sem("pq_copied"), sem("sc_made"), sem("sc_copied")
        gate_diff, gate_exp, chosen_made = sem("gate_diff"), sem("gate_exp"), sem("chosen_made")
        ch_turned, ch_copied = sem("ch_turned"), sem("ch_copied")
        one1_made, is2_made, one2_made, g_summed, g_copied = sem("one1_made"), sem("is2_made"), sem("one2_made"), sem("g_summed"), sem("g_copied")
        bl_turned, bl_copied, gpre_made = sem("bl_turned"), sem("bl_copied"), sem("gpre_made")
        gla_abs, gla_soft, gla_log = sem("gla_abs"), sem("gla_soft"), sem("gla_log")
        gla_sum, gla_exp, gla_ops = sem("gla_sum"), sem("gla_exp"), sem("gla_ops")
        gla_dec, gla_decexp = sem("gla_dec"), sem("gla_decexp")
        gt_made, gt_copied, gs_made, gs_masked = sem("gt_made"), sem("gt_copied"), sem("gs_made"), sem("gs_masked")
        gd_made, state_made, go_made, go_copied = sem("gd_made"), sem("state_made"), sem("go_made"), sem("go_copied")
        sb_abs, sb_soft, sb_log, sb_sum = sem("sb_abs"), sem("sb_soft"), sem("sb_log"), sem("sb_sum")
        sb_add, sb_exp, sb_w = sem("sb_add"), sem("sb_exp"), sem("sb_w")
        qdT_cleared = sem("qdT_cleared")
        br_exp = sem("br_exp")
        out_stored = sem("out_stored")

        sections = {}
        blocks = acts = adds = 0
        for name, nb, kind in (("in1", NB1, "act"), ("out1", 4, "add"), ("query", 4, "act"),
                               ("peer", 8 * PEER_ROUNDS, "both"),
                               ("in2", NB2, "act"), ("out2", 4, "add"), ("mlp", 8 * MLP_ROUNDS, "both")):
            sections[name] = (blocks, acts, adds, nb)
            blocks += nb
            acts += {"act": nb, "add": 0, "both": nb // 2}[kind]
            adds += {"act": 0, "add": nb, "both": nb // 2}[kind]
        all_blocks, all_acts, all_adds = blocks, acts, adds

        def after(name):
            b, x, y, nb = sections[name]
            kind = {"in1": (1, 0), "query": (1, 0), "in2": (1, 0), "out1": (0, 1), "out2": (0, 1)}.get(name, (.5, .5))
            return b + nb, x + int(nb * kind[0]), y + int(nb * kind[1])

        def bank(parity, t):
            return 2 * parity + t

        def over_blocks(eng, nb, block, first=2, last=0):
            first = 4 if nb == 4 else first
            for b in range(first):
                block(b, b % 2)
            if nb > first:
                with eng.Fori(0, (nb - first - last) // 2) as i:
                    block(2 * i + first, 0)
                    block(2 * i + first + 1, 1)
            for b in range(nb - last, nb):
                block(b, b % 2)

        GLA_STEPS = GLA_H * NT

        def gla_step(pos, at):
            n, odd = divmod(pos - at, 2)
            return n if not odd and 0 <= n < GLA_STEPS else -1

        GATES_AT = {0: 74, 1: 4}

        def batches_at(half, pos):
            return [m for m in range(32) if GATES_AT[half] + 3 * m // 2 == pos]

        def static(v):
            return isinstance(v, int)

        whole = [(0, D)]
        mix1_segs = [(0, 1024), (1024, 1024)]
        mix2_segs = [(0, 768)] + [(768 + GLA_V * i, GLA_V) for i in range(GLA_H)] + [(1536, 512)]
        norms = [(h, mix, whole), (mix, mix, mix1_segs), (h, mix, whole), (h, h, whole),
                 (h, mix, whole), (mix, mix, mix2_segs), (h, mix, whole), (h, h, whole)]
        gains = [gain, gain, gain, gain3[:], gain4[:], gain, gain, last_gain]

        def pieces(k, q):
            for n, (at, w) in enumerate(norms[k][2]):
                lo, hi = max(at, q * WIDE), min(at + w, (q + 1) * WIDE)
                if lo < hi:
                    yield lo, hi - lo, n

        widths = {"in1": N1, "in2": N2}

        AHEAD = 4
        NORM_OF = {"in1": 0, "out1": 1, "query": 2, "in2": 4, "out2": 5, "mlp": 6}
        TURNS = {"in1": 0, "out1": 1, "query": 2, "in2": 3, "out2": 4, "mlp": 5}

        block = ctx.enter_context(nc.Block())

        @block.sync
        def _(sp):
            def load(B, c, src):
                q = SUB * B + c
                if not static(q) or q >= RING:
                    sp.wait_ge(lo_made, q - RING + 1)
                n = src.shape[1] * src.shape[2]
                sp.dma_start(raw[:, c % RING, 0:n], src.rearrange("p k n -> p (k n)")).then_inc(raw_loaded[c % RING], 16)

            def gemm(name, w):
                b0, _, _, nb = sections[name]

                def blk(b, parity):
                    for c in range(SUB):
                        load(b0 + b, c, w[b, c])
                over_blocks(sp, nb, blk)

            def rounds(name, first_round, count, w_in, w_out):
                b0 = sections[name][0]

                def one(r):
                    for i in range(8):
                        for c in range(SUB):
                            w = w_in if i < 4 else w_out
                            load(b0 + 8 * r + i, c, w[4 * (first_round + r) + i % 4, c])
                one(0)
                with sp.Fori(1, count) as r:
                    one(r)

            for t in range(NT):
                sp.dma_start(h[:, t], a["x"][0, t * P:(t + 1) * P, :]).then_inc(x_loaded, 16)
            gemm("in1", a["w_in"])
            gemm("out1", a["w_out"])
            gemm("query", a["peer_query"])
            b0 = sections["peer"][0]

            def phase(up, nd, nu):
                for i in range(4):
                    for c in range(SUB):
                        w = a["peer_up"][4 * nu + i, c] if up else a["peer_down"][4 * nd + i, c]
                        load(b0 + 4 * (nd + nu) + i, c, w)
            with sp.Fori(0, 4) as r:
                phase(False, r, 0)
            with sp.Fori(0, 2) as r:
                phase(True, r + 4, r)
                phase(False, r + 4, r + 1)
            with sp.Fori(0, 2) as r:
                phase(True, 6, r + 2)
            with sp.Fori(0, 2) as r:
                phase(False, r + 6, 4)
            with sp.Fori(0, 4) as r:
                phase(True, 8, r + 4)
            gemm("in2", a["w_in_2"])
            gemm("out2", a["w_out_2"])
            rounds("mlp", 0, MLP_ROUNDS, a["w_mlp_in_2"], a["w_mlp_out_2"])
            for q in range(NQ):
                sp.wait_ge(normed, NQ * (len(norms) - 1) + q + 1)
                at = slice(q * WIDE, (q + 1) * WIDE)
                sp.dma_start(out[0].rearrange("(t p) d -> p t d", p=P)[:, :, at], h[:, :, at]).then_inc(out_stored, 16)
            sp.wait_ge(out_stored, 16 * NQ)

        @block.gpsimd
        def _(pool):
            steps = [0]

            def step(ins):
                steps[0] += 1
                ins.then_inc(pool_step, 1)
                pool.wait_ge(pool_step, steps[0])

            def spread(dst, row):
                return pool.dma_start(dst, row.partition_broadcast(P))

            pool.dma_start(fix[:], a["fix"]).then_inc(fix_loaded, 16)
            spread(gain, a["attn_norm_gain"][0]).then_inc(gain_loaded, 16)
            pool.dma_start(kc[:], a["kc"]).then_inc(kc_loaded, 16)
            spread(fbias[:], a["forget_bias"][0]).then_inc(small_loaded, 16)
            pool.wait_ge(fix_loaded, 16)
            nc.gpsimd.memset(pick[:], 0.0).then_inc(pick_made, 1)
            pool.wait_ge(pick_made, 1)
            for at in (0, 32, 64):
                nc.gpsimd.tensor_copy(pick[at:at + 16], fix[at:at + 16, C_IDENT + at:C_IDENT + at + 16].unsqueeze(2)
                                      .to_broadcast([16, FOX_H, S])).then_inc(pick_made, 1)
            pool.wait_ge(normed, NQ * 1)
            spread(gain[:, 0:1024], a["fox_out_gain"][0]).then_inc(gain_loaded, 16)
            spread(gain[:, 1024:2048], a["dil_out_gain"][0]).then_inc(gain_loaded, 16)
            pool.wait_ge(normed, NQ * 2)
            spread(gain, a["ffn_norm_gain"][0]).then_inc(gain_loaded, 16)
            pool.wait_ge(chunk_used, SUB * after("query")[0])
            pool.dma_start(skT, a["peer_sub_keys"]).then_inc(small_loaded, 16)

            for half in range(2):
                base = 32 * half

                def batch(n, slot, half=half, base=base):
                    pool.wait_ge(is2_made, base + n + 1)
                    at = bass.ds(8 * n, 8)
                    for part in range(3):
                        last = nc.gpsimd.tensor_tensor(
                            one2[:, slot, part], is2[:, slot],
                            gate_b[:, part, at].unsqueeze(2).to_broadcast([P, 8, HALF_J]), ALU.mult)
                    last.then_inc(one2_made, 1)
                with pool.Fori(0, 8) as i:
                    for slot in range(4):
                        batch(4 * i + slot, slot)

            pool.wait_ge(chunk_used, SUB * (sections["peer"][0] + 48))
            spread(gain3[:], a["final_norm_gain"]).then_inc(gain_loaded, 16)
            spread(gain4[:], a["norm_mix_2"][0]).then_inc(gain_loaded, 16)
            pool.wait_ge(added_out, after("peer")[2])
            step(nc.gpsimd.memset(gw[:], 0.0))
            step(nc.gpsimd.memset(blT[:], 0.0))
            step(nc.gpsimd.memset(blT[32:33, :], 1.0))
            nc.gpsimd.memset(rel[32:33, :], 1.0).then_inc(rel_ready, 1)
            pool.dma_start(kc[:], a["kc"]).then_inc(kc_loaded, 16)
            pool.dma_start(rel[0:32, :], a["rel_bias_2"]).then_inc(small_loaded, 16)
            pool.dma_start(buck[:], a["buck"]).then_inc(small_loaded, 16)
            pool.dma_start(gw[0:GLA_R, :], a["gla_gate_w_2"][0]).then_inc(small_loaded, 16)
            pool.dma_start(gw[32:33, :], a["gla_gate_b_2"]).then_inc(small_loaded, 16)
            spread(sinks[:], a["swa_sinks_2"][0]).then_inc(small_loaded, 16)
            pool.wait_ge(row_copied, 1)
            for p in range(4):
                pool.dma_start(rel_rows[:, 32 * p:32 * p + 32, :],
                               relrow[:].unsqueeze(1).to_broadcast([SWA_H, 32, TW + 1])).then_inc(rows_stored, 16)
            pool.wait_ge(rows_stored, 64)
            sheared = rel_rows.rearrange("h q x -> h (q x)")[:, 127:127 + P * TW]
            sheared = sheared.rearrange("h (q x) -> q h x", x=TW)[:, :, 0:S]
            pool.dma_start(bias_t[:], sheared).then_inc(bias_loaded, 16)

            pool.wait_ge(normed, NQ * 5)
            spread(gain[:, 0:768], a["swa_out_norm_2"][0]).then_inc(gain_loaded, 16)
            for i in range(GLA_H):
                spread(gain[:, 768 + GLA_V * i:768 + GLA_V * (i + 1)], a["gla_norm_2"][0]).then_inc(gain_loaded, 16)
            spread(gain[:, 1536:2048], a["sb_out_norm_2"][0]).then_inc(gain_loaded, 16)
            pool.wait_ge(normed, NQ * 6)
            spread(gain, a["norm_mlp_2"][0]).then_inc(gain_loaded, 16)
            pool.wait_ge(normed, NQ * 7)
            spread(last_gain, a["norm_final_2"]).then_inc(gain_loaded, 16)

        def split_hi(act, B, c, n):
            q = SUB * B + c
            act.wait_ge(raw_loaded[c % RING], 16 * (2 * B + c // RING + 1))
            if not static(q) or q >= RING:
                act.wait_ge(chunk_used, q - RING + 1)
            act.activation(w_hi[:, c % RING, 0:2 * n], raw[:, c % RING, 0:2 * n], ACT.Copy).then_inc(hi_made, 1)

        def split_lo(dve, B, c, n):
            q = SUB * B + c
            dve.wait_ge(hi_made, q + 1)
            nc.vector.tensor_tensor(w_lo[:, c % RING, 0:2 * n], raw[:, c % RING, 0:2 * n],
                                    w_hi[:, c % RING, 0:2 * n].bitcast(F32), ALU.subtract).then_inc(lo_made, 1)

        @block.scalar
        def _(act):
            steps = [0]

            def step(ins):
                steps[0] += 1
                ins.then_inc(act_step, 1)
                act.wait_ge(act_step, steps[0])

            def squares(k, quarters=range(NQ)):
                src, _, segs = norms[k]
                if k == 1:
                    act.wait_ge(head_out, FOX_H + DIL_H)
                if k == 5:
                    act.wait_ge(head_out, FOX_H + DIL_H + SWA_H + SB_H)
                if len(segs) == 1:
                    junk = hid if k == 3 else mix
                    for q in quarters:
                        if k in (2, 3, 6, 7):
                            act.wait_ge(added_out, after({2: "out1", 3: "peer", 6: "out2", 7: "mlp"}[k])[2] - 3 + q)
                        if k == 4:
                            act.wait_ge(normed, NQ * 3 + q + 1)
                        for t in range(NT):
                            if k == 0 and q == 0:
                                act.wait_ge(x_loaded, 16 * NT)
                            cols = slice(q * WIDE, (q + 1) * WIDE)
                            last = act.activation(junk[:, t, 0:WIDE] if k == 3 else junk[:, t, cols], src[:, t, cols],
                                                  ACT.Square, accum_out=stats[:, 0, t * 8 + q:t * 8 + q + 1])
                        if k == 3 and q < NQ - 1:
                            step(last)
                    if NQ - 1 in quarters:
                        last.then_inc(squared, 1)
                    return
                for t in range(NT):
                    for n, (at, w) in enumerate(segs):
                        last = act.activation(ps_flat[:, t * D + at:t * D + at + w], src[:, t, at:at + w],
                                              ACT.Square, accum_out=stats[:, 0, t * 8 + n:t * 8 + n + 1])
                last.then_inc(squared, 1)

            def roots(k):
                act.wait_ge(var_made, k + 1)
                act.activation(stats[:, 2, :], stats[:, 1, :], ACT.Sqrt).then_inc(rooted, 1)

            def ahead(name, chunks):
                for c in chunks:
                    split_hi(act, sections[name][0], c, widths.get(name, WIDE))

            def open_section(k, name):
                for g in range(8):
                    if name == "in1" and g < AHEAD:
                        ahead(name, (g,))
                    act.wait_ge(x_turned, 8 * k + g + 1)
                    act.activation(x_hi[:, 2 * g:2 * g + 2, :].rearrange("p k s -> p (k s)"), ps[:, 4 + g % 2, :],
                                   ACT.Copy).then_inc(x_hi_made, 1)
                    if AHEAD <= g + 1 < SUB:
                        split_hi(act, sections[name][0], g + 1, widths.get(name, WIDE))

            def drain(B, parity, n, dst):
                act.wait_ge(chunk_used, SUB * (B + 1))
                for t in range(NT):
                    last = act.activation(dst(t), ps[:, bank(parity, t), 0:n], ACT.Copy)
                last.then_inc(copied_out, 1)

            def gemm(name, n, dst, then=None, then_norm=None, first=2, last=0, extra=None):
                b0, _, _, nb = sections[name]

                def place(b):
                    return lambda t: dst[:, t, bass.ds(b * n, n)]

                def blk(b, parity):
                    if static(b) and b == 0:
                        open_section(TURNS[name], name)
                        return
                    for c in range(SUB):
                        if c == 3 and dst is not None:
                            drain(b0 + b - 1, 1 - parity, n, place(b - 1))
                        split_hi(act, b0 + b, c, n)
                        if extra and static(b) and b >= 4:
                            extra(SUB * (b - 4) + c)
                over_blocks(act, nb, blk, first, last)
                if then_norm:
                    squares(then_norm, range(NQ - 1))
                if then:
                    ahead(then, range(AHEAD - 1))
                if dst is not None:
                    drain(b0 + nb - 1, 1, n, place(nb - 1))
                if then:
                    ahead(then, (AHEAD - 1,))
                if then_norm:
                    squares(then_norm, (NQ - 1,))
                    roots(then_norm)

            def rounds(name, h0, count, func):
                b0 = sections[name][0]

                def one(r, first=False):
                    for i in range(8):
                        B = b0 + 8 * r + i
                        if first and i == 0:
                            open_section(TURNS[name], name)
                            continue
                        for c in range(SUB):
                            if c == 3 and 1 <= i <= 4:
                                act.wait_ge(chunk_used, SUB * B)
                                before = h0 + 4 * r + i - 1
                                if not static(before) or before > 0:
                                    act.wait_ge(hid_turned, before)
                                for t in range(NT):
                                    last = act.activation(hid[:, t], ps[:, bank((i - 1) % 2, t), :], func)
                                last.then_inc(copied_out, 1)
                            split_hi(act, B, c, WIDE)
                            if c == 4 and 2 <= i <= 4:
                                split_hidden(r, i - 2)
                            if c == 7 and i == 4:
                                split_hidden(r, 3)

                def split_hidden(r, i):
                    pair = ps[:, 4 + 2 * (i % 2):6 + 2 * (i % 2), :].rearrange("p b n -> p (b n)")
                    act.wait_ge(hid_turned, h0 + 4 * r + i + 1)
                    act.activation(pair, pair, ACT.Square).then_inc(hid_full, 1)
                    act.wait_ge(hid_full, h0 + 4 * r + i + 1)
                    act.activation(a_hi[:, 4 * i:4 * i + 4, :].rearrange("p k s -> p (k s)"), pair,
                                   ACT.Copy).then_inc(hid_hi, 1)
                one(0, True)
                with act.Fori(1, count) as r:
                    one(r)

            def copy_qk(i):
                act.wait_ge(qk_turned, i + 1)
                if i >= 2:
                    act.wait_ge(scored, i - 1)
                act.activation(qkT[:, i % 2, :], ps[0:HD, 6 + i % 2, :], ACT.Copy).then_inc(qk_copied, 1)

            def exp_head(i, sink=None):
                act.wait_ge(max_made, i + 1)
                if i >= 2:
                    act.wait_ge(p_turned, i - 1)
                s = hs[:, i % 4]
                src, scale = (ps[:, 4 + i % 2], HD ** -0.5) if sink is None else (biased[:, i % 2], 1.0)
                act.activation(prob[:, i % 2, 0:P], src[:, 0:P], ACT.Exp, bias=s[:, 1, 0:1],
                               scale=scale, accum_out=s[:, 2, 0:1])
                last = act.activation(prob[:, i % 2, P:3 * P], src[:, P:3 * P], ACT.Exp, bias=s[:, 1, 1:2],
                                      scale=scale, accum_out=s[:, 2, 1:2])
                if sink is not None:
                    last = act.activation(s[:, 4, :], s[:, 1, :], ACT.Exp, bias=sink)
                last.then_inc(exp_made, 1)

            act.wait_ge(fix_loaded, 16)
            act.activation(ident_b[:], ident, ACT.Copy).then_inc(masks_made, 1)
            act.wait_ge(stats_set, 1)
            squares(0)
            roots(0)
            gemm("in1", N1, proj1, then="out1")
            act.wait_ge(gate_abs, 1)
            step(act.activation(fg[:, 2], fg[:, 1], ACT.Exp, scale=-1.0))
            act.activation(fg[:, 3], fg[:, 2], ACT.Ln, bias=1.0).then_inc(gate_soft, 1)
            act.wait_ge(cum_made, 1)
            act.activation(c8[:], ps[0:16, 0, 0:S], ACT.Copy, scale=8.0).then_inc(cum_copied, 1)
            for n in range(FOX_H + DIL_H + 1):
                if n < FOX_H + DIL_H:
                    copy_qk(n)
                if n >= 1:
                    exp_head(n - 1)
            squares(1)
            roots(1)
            gemm("out1", WIDE, None, then="query", then_norm=2)
            gemm("query", WIDE, pq)

            for g in range(8):
                act.wait_ge(pq_turned, g + 1)
                act.activation(pqT[:, 2 * g:2 * g + 2, :].rearrange("p k s -> p (k s)"), ps[:, 4 + g % 2, :],
                               ACT.Copy).then_inc(pq_copied, 1)
            for n in range(8):
                t, g = n // 4, n % 4
                act.wait_ge(sc_made, n + 1)
                act.activation(sc[:, t, 4 * g:4 * g + 4, :].rearrange("p g n -> p (g n)"), ps[:, 6 + n % 2, :],
                               ACT.Copy).then_inc(sc_copied, 1)
            b0, c0, _, _ = sections["peer"]

            def spill(n):
                act.wait_ge(copied_out, c0 + n + 1)
                act.dma_start(hid_rows[n], hid.rearrange("p t n -> p (t n)")).then_inc(spilled, 16)

            def reload(n):
                act.wait_ge(spilled, 16 * (n + 1))
                if not static(n) or n > 0:
                    act.wait_ge(hid_turned, n)
                act.dma_start(back[:].rearrange("p t n -> p (t n)"), hid_rows[n]).then_inc(reloaded, 16)

            def split_gated(n, pair):
                act.wait_ge(hid_full, n + 1)
                act.activation(a_hi[:, 4 * pair[0]:4 * pair[0] + 4, :].rearrange("p k s -> p (k s)"),
                               ps[:, pair[1]:pair[1] + 2, :].rearrange("p b n -> p (b n)"), ACT.Copy).then_inc(hid_hi, 1)

            def copy_gates(half, n):
                act.wait_ge(g_summed, 32 * half + n + 1)
                act.activation(gates_w[:, 8 * HALF_J * n:8 * HALF_J * (n + 1)], ps[:, 6 + n % 2, :], ACT.Copy).then_inc(g_copied, 1)

            def phase(up, nd, nu, prev_up, fill_next, extra=None, more=True):
                for i in range(4):
                    for c in range(SUB):
                        if c == 3 and not (prev_up if i == 0 else up) and not (static(nd) and nd == 0 and i == 0):
                            n = 4 * nd + i - 1
                            act.wait_ge(chunk_used, SUB * (b0 + 4 * (nd + nu) + i))
                            if not static(n) or n > 0:
                                act.wait_ge(spilled, 16 * n)
                            for t in range(NT):
                                last = act.activation(hid[:, t], ps[:, bank((i - 1) % 2, t), :], ACT.Gelu_apprx_tanh)
                            last.then_inc(copied_out, 1)
                            spill(n)
                        split_hi(act, b0 + 4 * (nd + nu) + i, c, WIDE)
                        if i == 3 and fill_next:
                            f = 4 * (nu + 1 if up else nu)
                            if c == 5:
                                reload(f + 1)
                            if c == 6:
                                split_gated(f, (0, 4))
                            if c == 7:
                                reload(f + 2)
                        if i == 0 and up:
                            f = 4 * nu
                            if c == 0:
                                split_gated(f + 1, (1, 6))
                            if c == 1:
                                reload(f + 3)
                            if c == 2:
                                split_gated(f + 2, (2, 4))
                            if c == 3 and more:
                                reload(f + 4)
                            if c == 4:
                                split_gated(f + 3, (3, 6))
                        if extra:
                            extra(SUB * i + c)

            def beside(base, half):
                def extra(pos):
                    pos += base
                    if half == 0 and pos == 12:
                        reload(0)
                    if half == 0 and pos == 56:
                        act.wait_ge(gate_diff, 1)
                        act.activation(big[:, 1536:1792], big[:, 1536:1792], ACT.Exp).then_inc(gate_exp, 1)
                    if half == 0 and pos == 71:
                        act.wait_ge(ch_turned, 3)
                        for s in range(3):
                            act.activation(chosenT[:, s, :], ps[:, 4 + s // 2, S * (s % 2):S * (s % 2) + S], ACT.Copy).then_inc(ch_copied, 1)
                    for n in batches_at(half, pos - 4):
                        copy_gates(half, n)
                return extra

            for r in range(4):
                phase(False, r, 0, False, r == 3, beside(32 * r, 0))
            with act.Fori(0, 2) as r:
                phase(True, r + 4, r, False, False)
                phase(False, r + 4, r + 1, True, True)
            phase(True, 6, 2, False, True)
            phase(True, 6, 3, True, False)
            for r in range(2):
                phase(False, 6 + r, 4, r == 0, r == 1, beside(32 * r, 1))
            phase(True, 8, 4, False, True)
            with act.Fori(0, 2) as r:
                phase(True, 8, r + 5, True, True)
            phase(True, 8, 7, True, False, more=False)
            squares(3, range(NQ - 1))
            ahead("in2", range(AHEAD - 1))
            ahead("in2", (AHEAD - 1,))
            squares(3, (NQ - 1,))
            roots(3)

            squares(4)
            roots(4)

            def gla(pos):
                if pos == 3:
                    act.wait_ge(rel_made, 1)
                    act.activation(relrow[:], ps[0:SWA_H, 6, 0:TW + 1], ACT.Copy).then_inc(row_copied, 1)
                if pos == 6:
                    act.wait_ge(bl_turned, 1)
                    act.wait_ge(pool_step, 3)
                    act.activation(blT[0:GLA_R, :], ps[0:GLA_R, 4, 0:S], ACT.Copy).then_inc(bl_copied, 1)
                if pos == 8:
                    act.wait_ge(gla_abs, 1)
                    step(act.activation(k_inv, g_log, ACT.Exp, scale=-1.0))
                    act.activation(q_dec, k_inv, ACT.Ln, bias=1.0).then_inc(gla_soft, 1)
                if pos == 10:
                    act.wait_ge(gla_sum, 1)
                    act.activation(g_tmp, ps[:, 4:6, 0:384], ACT.Copy)
                    act.activation(q_dec, ps[:, 4:6, 0:384], ACT.Exp)
                    act.activation(k_inv, ps[:, 4:6, 0:384], ACT.Exp, scale=-1.0).then_inc(gla_exp, 1)
                if pos == 12:
                    act.wait_ge(gla_ops, 1)
                    act.activation(k_end[:, :, 1], k_end[:, :, 0], ACT.Exp).then_inc(gla_exp, 1)
                if pos == 14:
                    act.wait_ge(gla_dec, 1)
                    act.activation(g_dec, ps[0:GLA_K, 4, 0:4 * GLA_H], ACT.Exp).then_inc(gla_decexp, 1)
                if pos in (48, 56):
                    t = (pos - 48) // 8
                    act.wait_ge(copied_out, sections["in2"][1] + 9)
                    act.activation(proj2[:, t, BQ:BQ + 768], proj2[:, t, BR:BR + 768], ACT.Exp, scale=-1.0).then_inc(br_exp, 1)
                n = gla_step(pos, 15)
                if n >= 0:
                    act.wait_ge(gt_made, n + 1)
                    if n:
                        act.wait_ge(go_made, n)
                    act.activation(qdT[:, 2:4, :].rearrange("p a s -> p (a s)"), ps[0:GLA_K, 4, 0:S], ACT.Copy).then_inc(gt_copied, 1)
                n = gla_step(pos, 17)
                if n >= 0:
                    hh, t = divmod(n, NT)
                    act.wait_ge(go_made, n + 1)
                    act.activation(mix[:, t, 768 + GLA_V * hh:768 + GLA_V * (hh + 1)], ps[:, 7, 0:GLA_V],
                                   ACT.Copy).then_inc(go_copied, 1)

            gemm("in2", N2, proj2, "out2", None, 8, 2, gla)
            for n in range(FOX_H + DIL_H, FOX_H + DIL_H + SWA_H + 1):
                if n < FOX_H + DIL_H + SWA_H:
                    copy_qk(n)
                if n > FOX_H + DIL_H:
                    i = n - 1 - FOX_H - DIL_H
                    exp_head(n - 1, sinks[:, i:i + 1])
            first = FOX_H + DIL_H + SWA_H
            for n in range(SB_H + 4):
                if n < SB_H:
                    copy_qk(first + n)
                if 1 <= n <= SB_H:
                    i = n - 1
                    act.wait_ge(sb_abs, i + 1)
                    step(act.activation(sbt[:, i % 4], sbt[:, i % 4], ACT.Exp, scale=-1.0))
                    act.activation(sbt[:, i % 4], sbt[:, i % 4], ACT.Ln, bias=1.0).then_inc(sb_soft, 1)
                if 3 <= n <= SB_H + 2:
                    i = n - 3
                    act.wait_ge(sb_add, i + 1)
                    act.activation(sbw[:, i % 4], sbb[:, i % 4], ACT.Exp).then_inc(sb_exp, 1)
            squares(5)
            roots(5)
            gemm("out2", WIDE, None, then="mlp", then_norm=6)
            rounds("mlp", 4 * PEER_ROUNDS, MLP_ROUNDS, ACT.Relu)
            squares(7)
            roots(7)

        @block.vector
        def _(dve):
            V = nc.vector
            steps = [0]

            def step(ins):
                steps[0] += 1
                ins.then_inc(dve_step, 1)
                dve.wait_ge(dve_step, steps[0])

            gains_due = [16, 48, 64, 96, 96, 192, 208, 224]

            def norm_scale(k):
                segs = norms[k][2]
                dve.wait_ge(squared, k + 1)
                var, ssq = (stats[:, n].rearrange("p (t n) -> p t n", t=NT) for n in (1, 0))
                if len(segs) == 1:
                    step(V.tensor_reduce(var[:, :, 0], ssq[:, :, 0:NQ], AX, ALU.add))
                    V.tensor_scalar(var[:, :, 0:1], var[:, :, 0:1], 1.0 / D, EPS, ALU.mult, ALU.add).then_inc(var_made, 1)
                elif len(segs) == 2:
                    V.tensor_scalar(stats[:, 1, :], stats[:, 0, :], 1.0 / 1024, EPS, ALU.mult, ALU.add).then_inc(var_made, 1)
                else:
                    V.tensor_scalar(var[:, :, 0:1], ssq[:, :, 0:1], 1.0 / 768, EPS, ALU.mult, ALU.add)
                    V.tensor_scalar(var[:, :, 5:6], ssq[:, :, 5:6], 1.0 / 512, EPS, ALU.mult, ALU.add)
                    V.tensor_scalar(var[:, :, 1:5], ssq[:, :, 1:5], 1.0 / GLA_V, EPS, ALU.mult, ALU.add).then_inc(var_made, 1)
                dve.wait_ge(rooted, k + 1)
                step(V.reciprocal(stats[:, 3, :], stats[:, 2, :]))
                dve.wait_ge(gain_loaded, gains_due[k])

            def norm_quarter(k, q):
                src, dst, _ = norms[k]
                for t in range(NT):
                    for at, w, n in pieces(k, q):
                        last = V.scalar_tensor_tensor(out=dst[:, t, at:at + w], in0=src[:, t, at:at + w],
                                                      scalar=stats[:, 3, t * 8 + n:t * 8 + n + 1],
                                                      in1=gains[k][:, at:at + w], op0=ALU.mult, op1=ALU.mult)
                if k == 5 and q in (1, 2):
                    step(last)
                    lo, hi = max(768, q * WIDE), min(1536, (q + 1) * WIDE)
                    last = V.tensor_tensor(mix[:, :, lo:hi], mix[:, :, lo:hi], proj2[:, :, BQ + lo - 768:BQ + hi - 768], ALU.mult)
                last.then_inc(normed, 1)

            def ahead(name, chunks):
                for c in chunks:
                    split_lo(dve, sections[name][0], c, widths.get(name, WIDE))

            def open_section(k, norm, name):
                norm_scale(norm)
                norm_quarter(norm, 0)
                for g in range(8):
                    if g < NQ - 1:
                        norm_quarter(norm, g + 1)
                    if name == "in1" and g < AHEAD:
                        ahead(name, (g,))
                    dve.wait_ge(x_hi_made, 8 * k + g + 1)
                    V.tensor_tensor(x_lo[:, 2 * g:2 * g + 2, :].rearrange("p k s -> p (k s)"), ps[:, 4 + g % 2, :],
                                    x_hi[:, 2 * g:2 * g + 2, :].rearrange("p k s -> p (k s)").bitcast(F32),
                                    ALU.subtract).then_inc(x_lo_made, 1)
                    if AHEAD <= g + 1 < SUB:
                        split_lo(dve, sections[name][0], g + 1, widths.get(name, WIDE))

            def add_block(B, parity, at):
                dve.wait_ge(chunk_used, SUB * (B + 1))
                for t in range(NT):
                    last = V.tensor_tensor(h[:, t, at * WIDE:(at + 1) * WIDE], ps[:, bank(parity, t), :],
                                           h[:, t, at * WIDE:(at + 1) * WIDE], ALU.add)
                last.then_inc(added_out, 1)

            def gemm(name, n, adds, then=None, first=2, last=0, extra=None):
                b0, _, _, nb = sections[name]

                def blk(b, parity):
                    if static(b) and b == 0:
                        open_section(TURNS[name], NORM_OF[name], name)
                        return
                    for c in range(SUB):
                        if c == 3 and adds and b > 0:
                            add_block(b0 + b - 1, 1 - parity, b - 1)
                        split_lo(dve, b0 + b, c, n)
                        if extra and static(b) and b >= 4:
                            extra(SUB * (b - 4) + c)
                over_blocks(dve, nb, blk, first, last)
                if then:
                    ahead(then, range(AHEAD - 1))
                if adds:
                    add_block(b0 + nb - 1, 1, nb - 1)
                if then:
                    ahead(then, (AHEAD - 1,))

            def rounds(name, h0, count):
                b0 = sections[name][0]

                def rest(r, i):
                    dve.wait_ge(hid_hi, h0 + 4 * r + i + 1)
                    pair = ps[:, 4 + 2 * (i % 2):6 + 2 * (i % 2), :].rearrange("p b n -> p (b n)")
                    V.tensor_tensor(a_lo[:, 4 * i:4 * i + 4, :].rearrange("p k s -> p (k s)"), pair,
                                    a_hi[:, 4 * i:4 * i + 4, :].rearrange("p k s -> p (k s)").bitcast(F32),
                                    ALU.subtract).then_inc(hid_lo, 1)

                def one(r, first):
                    for i in range(8):
                        B = b0 + 8 * r + i
                        if first and i == 0:
                            open_section(TURNS[name], NORM_OF[name], name)
                            continue
                        for c in range(SUB):
                            if c == 3 and (i >= 5 or (i == 0 and not first)):
                                add_block(B - 1, (i - 1) % 2, (i - 5) % 4 if i else 3)
                            split_lo(dve, B, c, WIDE)
                            if c == 4 and 2 <= i <= 4:
                                rest(r, i - 2)
                            if c == 7 and i == 4:
                                rest(r, 3)
                one(0, True)
                with dve.Fori(1, count) as r:
                    one(r, False)
                add_block(b0 + 8 * count - 1, 1, 3)

            def max_head(i):
                dve.wait_ge(scored, i + 1)
                if i >= 4:
                    dve.wait_ge(head_out, i - 3)
                s, src = hs[:, i % 4], ps[:, 4 + i % 2]
                V.reduce_max(s[:, 0, 0:1], src[:, 0:P], AX)
                step(V.reduce_max(s[:, 0, 1:2], src[:, P:3 * P], AX))
                V.tensor_scalar(s[:, 1, :], s[:, 0, :], -(HD ** -0.5), None, ALU.mult).then_inc(max_made, 1)

            def max_swa(i):
                j = i - FOX_H - DIL_H
                dve.wait_ge(scored, i + 1)
                dve.wait_ge(head_out, i - 3)
                s, src, dst = hs[:, i % 4], ps[:, 4 + i % 2], biased[:, i % 2]
                V.scalar_tensor_tensor(out=dst[:, 0:P], in0=src[:, 0:P], scalar=HD ** -0.5, in1=bias_t[:, j, P:2 * P],
                                       op0=ALU.mult, op1=ALU.add)
                step(V.scalar_tensor_tensor(out=dst[:, P:3 * P], in0=src[:, P:3 * P], scalar=HD ** -0.5,
                                            in1=bias_t[:, j, :], op0=ALU.mult, op1=ALU.add))
                V.reduce_max(s[:, 0, 0:1], dst[:, 0:P], AX)
                step(V.reduce_max(s[:, 0, 1:2], dst[:, P:3 * P], AX))
                V.tensor_scalar(s[:, 1, :], s[:, 0, :], sinks[:, j:j + 1], -1.0, ALU.max, ALU.mult).then_inc(max_made, 1)

            def count_head(i):
                dve.wait_ge(exp_made, i + 1)
                s = hs[:, i % 4]
                for n, (at, w) in enumerate(((0, P), (P, 2 * P))):
                    last = V.tensor_tensor_reduce(prob[:, i % 2, at:at + w], prob[:, i % 2, at:at + w],
                                                  KC(K_COUNT + at, w), 1.0, 0.0, ALU.mult, ALU.add, s[:, 2, n:n + 1])
                last.then_inc(counted, 1)

            def copy_p(i):
                dve.wait_ge(p_turned, i + 1)
                if i >= 2:
                    dve.wait_ge(pv_made, i - 1)
                V.tensor_copy(probT[:, i % 2, :], ps[:, i % 2, 0:3 * P]).then_inc(p_copied, 1)

            def out_head(i, at, sink=False):
                s = hs[:, i % 4]
                dve.wait_ge(pv_made, i + 1)
                if sink:
                    step(V.tensor_tensor(s[:, 2, :], s[:, 2, :], s[:, 4, :], ALU.add))
                step(V.reciprocal(s[:, 3, :], s[:, 2, :]))
                for t in range(NT):
                    last = V.tensor_scalar(mix[:, t, at:at + HD], ps[:, 2 + i % 2, HD * t:HD * t + HD],
                                           s[:, 3, t:t + 1], None, ALU.mult)
                last.then_inc(head_out, 1)

            V.memset(stats[:], 1.0).then_inc(stats_set, 1)
            gemm("in1", N1, False, "out1")
            dve.wait_ge(copied_out, after("in1")[1])
            dve.wait_ge(small_loaded, 16)
            step(V.tensor_tensor(fg[:, 0], proj1[:, :, FG:FG + 16], fbias[:].unsqueeze(1).to_broadcast([P, NT, 16]), ALU.add))
            step(V.tensor_scalar(fg[:, 1], fg[:, 0], -1.0, None, ALU.mult))
            V.tensor_tensor(fg[:, 1], fg[:, 1], fg[:, 0], ALU.max).then_inc(gate_abs, 1)
            dve.wait_ge(gate_soft, 1)
            V.scalar_tensor_tensor(out=fg[:, 0], in0=fg[:, 0], scalar=0.0, in1=fg[:, 3], op0=ALU.min,
                                   op1=ALU.subtract).then_inc(gate_log, 1)
            step(V.memset(c_parts[:], 0.0))
            dve.wait_ge(kc_loaded, 16)
            V.tensor_copy(mask_b[:], KC(K_MASK, 3 * P)).then_inc(masks_made, 1)
            dve.wait_ge(cum_copied, 1)
            step(V.tensor_copy(c_parts[0:16, 0], c8[:]))
            step(V.tensor_tensor(c_rest[:], c8[:], c_parts[0:16, 0], ALU.subtract))
            step(V.tensor_copy(c_mid[:], c_rest[:]))
            V.tensor_copy(c_parts[32:48, 0], c_mid[:])
            step(V.tensor_tensor(c8[:], c_rest[:], c_mid[:], ALU.subtract))
            step(V.tensor_copy(c_parts[64:80, 0], c8[:]))
            V.tensor_scalar(c_parts[:, 1], c_parts[:, 0], -1.0, None, ALU.mult).then_inc(c_split, 1)
            for t in range(NT):
                qk = proj1[:, t, DQ:DQ + 2 * 1024].rearrange("p (n d) -> p n d", d=HD)
                x1, x2 = qk[:, :, 0:8], qk[:, :, 8:16]
                cos = KC(K_COS + 8 * t, 8).unsqueeze(1).to_broadcast([P, 32, 8])
                sin = KC(K_SIN + 8 * t, 8).unsqueeze(1).to_broadcast([P, 32, 8])
                V.tensor_tensor(rope[:, 0], x1, cos, ALU.mult)
                V.tensor_tensor(rope[:, 1], x2, sin, ALU.mult)
                V.tensor_tensor(rope[:, 2], x2, cos, ALU.mult)
                step(V.tensor_tensor(rope[:, 3], x1, sin, ALU.mult))
                V.tensor_tensor(x1, rope[:, 0], rope[:, 1], ALU.subtract)
                V.tensor_tensor(x2, rope[:, 2], rope[:, 3], ALU.add).then_inc(roped, 1)
                dve.wait_ge(roped, t + 1)
            for n in range(1, FOX_H + DIL_H + 3):
                if n <= FOX_H + DIL_H:
                    max_head(n - 1)
                if 2 <= n <= FOX_H + DIL_H + 1:
                    copy_p(n - 2)
                if n >= 3:
                    i = n - 3
                    out_head(i, HD * i)
                if FOX_H < n <= FOX_H + DIL_H:
                    count_head(n - 1)
            gemm("out1", WIDE, True, "query")
            gemm("query", WIDE, False)

            def best(v, i, vals, work):
                step(V.max(v[:, 0:8], vals))
                V.max_index(i[:, 0:8].bitcast(U32), v[:, 0:8], vals)
                step(V.match_replace(work, v[:, 0:8], vals, -3.0e38))
                step(V.max(v[:, 8:16], work))
                step(V.max_index(i[:, 8:16].bitcast(U32), v[:, 8:16], work))

            def best_keys(t, g):
                if g % 4 == 0:
                    dve.wait_ge(sc_copied, 4 * t + g // 4 + 1)
                best(top_v[:, t, g], top_i[:, t, g], sc[:, t, g, :], scr[:, 0:NKEY])

            def all_sums(t):
                sums = cand.rearrange("p (g a b) -> p g a b", g=PH, a=TOPK)
                for g in range(PH):
                    last = V.tensor_tensor(sums[:, g], top_v[:, t, 2 * g].unsqueeze(2).to_broadcast([P, TOPK, TOPK]),
                                           top_v[:, t, 2 * g + 1].unsqueeze(1).to_broadcast([P, TOPK, TOPK]), ALU.add)
                step(last)

            def best_pairs(t, g):
                best(best_v[:, t, g], best_c[:, t, g], cand[:, 256 * g:256 * g + 256], scr)

            bv = big[:, 1536:1792].rearrange("p (g k) -> p g k", k=TOPK)

            def ranks():
                step(V.tensor_copy(big[:, 1024:1536], big[:, 512:1024].bitcast(U32)))
                code = big[:, 1792:2048].bitcast(U32)
                step(V.tensor_scalar(ranku.bitcast(U32), code, 4, None, ALU.logical_shift_right))
                step(V.tensor_copy(big[:, 2048:2304], ranku.bitcast(U32)))
                step(V.tensor_scalar(ranku.bitcast(U32), code, 15, None, ALU.bitwise_and))
                step(V.tensor_copy(big[:, 2304:2560], ranku.bitcast(U32)))
                step(V.tensor_copy(gsum[:, 0, :].unsqueeze(2), bv[:, :, 0:1]))
                V.tensor_tensor(bv, bv, gsum[:, 0, :].unsqueeze(2).to_broadcast([P, 16, TOPK]), ALU.subtract).then_inc(gate_diff, 1)

            def look_up(s, t, part):
                hot = cand.rearrange("p (n k) -> p n k", k=TOPK)
                if part == 0:
                    step(V.tensor_tensor(hot, rank[:, s, t].unsqueeze(2).to_broadcast([P, P, TOPK]),
                                         iota[:, 0:TOPK].unsqueeze(1).to_broadcast([P, P, TOPK]), ALU.is_equal))
                if part == 1:
                    for g in range(PH):
                        hg = hot[:, TOPK * g:TOPK * g + TOPK, :]
                        last = V.tensor_tensor(hg, hg, top_f[:, t, 2 * g + s].unsqueeze(1).to_broadcast([P, TOPK, TOPK]), ALU.mult)
                    step(last)
                if part == 2:
                    step(V.tensor_reduce(chosen[:, s, t], hot, AX, ALU.add))

            def softmax_gates():
                dve.wait_ge(gate_exp, 1)
                step(V.tensor_reduce(gsum[:, 0, :], bv, AX, ALU.add))
                step(V.reciprocal(gsum[:, 1, :], gsum[:, 0, :]))
                V.tensor_tensor(chosen[:, 2].rearrange("p t (g k) -> p (t g) k", k=TOPK), bv,
                                gsum[:, 1, :].unsqueeze(2).to_broadcast([P, 16, TOPK]), ALU.mult).then_inc(chosen_made, 1)

            def search(pos):
                if pos < 32:
                    best_keys(pos // 16, pos % 16)
                elif pos < 50:
                    t, g = divmod(pos - 32, 9)
                    all_sums(t) if g == 0 else best_pairs(t, g - 1)
                elif pos == 50:
                    ranks()
                elif pos < 63:
                    n = pos - 51
                    look_up(n // 6, n // 3 % 2, n % 3)
                elif pos == 63:
                    softmax_gates()

            def batch(half, n):
                if half == 0 and n == 0:
                    dve.wait_ge(ch_copied, 3)
                if half == 1 and n == 0:
                    dve.wait_ge(chunk_used, SUB * (b0 + 40))
                if n == 0:
                    V.tensor_copy(index_b[:], chosenT[:, 0:2, :])
                    V.tensor_copy(iota_b[:], iota)
                    step(V.tensor_copy(gate_b[:, 0], chosenT[:, 2, :]))
                    step(V.tensor_tensor(gate_left[:], chosenT[:, 2, :], gate_b[:, 0], ALU.subtract))
                    step(V.tensor_copy(gate_b[:, 1], gate_left[:]))
                    step(V.tensor_tensor(gate_left[:], gate_left[:], gate_b[:, 1], ALU.subtract))
                    step(V.tensor_copy(gate_b[:, 2], gate_left[:]))
                if half or n >= 4:
                    dve.wait_ge(g_summed, 32 * half + n - 3)
                at = slice(8 * n, 8 * n + 8)
                V.tensor_tensor(one1[:, n % 4], iota_b[:].unsqueeze(1).to_broadcast([P, 8, P]),
                                index_b[:, 0, at].unsqueeze(2).to_broadcast([P, 8, P]), ALU.is_equal).then_inc(one1_made, 1)
                V.tensor_tensor(is2[:, n % 4],
                                iota_b[:, HALF_J * half:HALF_J * half + HALF_J].unsqueeze(1).to_broadcast([P, 8, HALF_J]),
                                index_b[:, 1, at].unsqueeze(2).to_broadcast([P, 8, HALF_J]), ALU.is_equal).then_inc(is2_made, 1)

            b0 = sections["peer"][0]

            def fill(n, g, local):
                dve.wait_ge(hid_turned, n + 1)
                pair = ps[:, 4 + 2 * (g % 2):6 + 2 * (g % 2), :].rearrange("p b (k s) -> p (b k) s", s=S)
                V.tensor_tensor(pair, pair, gates[:, bass.ds(16 * local + 4 * g, 4), :], ALU.mult).then_inc(hid_full, 1)

            def rest(n, g):
                dve.wait_ge(hid_hi, n + 1)
                pair = ps[:, 4 + 2 * (g % 2):6 + 2 * (g % 2), :].rearrange("p b n -> p (b n)")
                V.tensor_tensor(a_lo[:, 4 * g:4 * g + 4, :].rearrange("p k s -> p (k s)"), pair,
                                a_hi[:, 4 * g:4 * g + 4, :].rearrange("p k s -> p (k s)").bitcast(F32),
                                ALU.subtract).then_inc(hid_lo, 1)

            def phase(up, nd, nu, prev_up, fill_next, half, extra=None):
                for i in range(4):
                    B = b0 + 4 * (nd + nu) + i
                    for c in range(SUB):
                        if c == 3 and (prev_up if i == 0 else up):
                            add_block(B - 1, (i - 1) % 2, (i - 1) % 4)
                        split_lo(dve, B, c, WIDE)
                        if i == 3 and fill_next:
                            f = nu + 1 if up else nu
                            if c == 5:
                                fill(4 * f, 0, f - 4 * half)
                            if c == 6:
                                rest(4 * f, 0)
                            if c == 7:
                                fill(4 * f + 1, 1, f - 4 * half)
                        if i == 0 and up:
                            if c == 0:
                                rest(4 * nu + 1, 1)
                            if c == 1:
                                fill(4 * nu + 2, 2, nu - 4 * half)
                            if c == 2:
                                rest(4 * nu + 2, 2)
                            if c == 3:
                                fill(4 * nu + 3, 3, nu - 4 * half)
                            if c == 4:
                                rest(4 * nu + 3, 3)
                        if extra:
                            extra(SUB * i + c)

            def beside(base, half):
                def extra(pos):
                    pos += base
                    if half == 0:
                        search(pos)
                    for n in batches_at(half, pos):
                        batch(half, n)
                    if half == 0 and pos == 124 or half == 1 and pos == 60:
                        dve.wait_ge(g_copied, 32 * half + 32)
                return extra

            for r in range(4):
                phase(False, r, 0, False, r == 3, 0, beside(32 * r, 0))
            with dve.Fori(0, 2) as r:
                phase(True, r + 4, r, False, False, 0)
                phase(False, r + 4, r + 1, True, True, 0)
            phase(True, 6, 2, False, True, 0)
            phase(True, 6, 3, True, False, 0)
            for r in range(2):
                phase(False, 6 + r, 4, r == 0, r == 1, 1, beside(32 * r, 1))
            phase(True, 8, 4, False, True, 1)
            with dve.Fori(0, 2) as r:
                phase(True, 8, r + 5, True, True, 1)
            phase(True, 8, 7, True, False, 1)
            ahead("in2", range(AHEAD - 1))
            add_block(b0 + 63, 1, 3)
            ahead("in2", (AHEAD - 1,))
            norm_scale(3)
            for q in range(NQ):
                norm_quarter(3, q)


            def gla(pos):
                if pos == 5:
                    dve.wait_ge(bl_turned, 1)
                    dve.wait_ge(kc_loaded, 32)
                    V.memset(qdT[:, 0:2, :], 0.0).then_inc(qdT_cleared, 1)
                if pos == 7:
                    dve.wait_ge(gpre_made, 1)
                    step(V.tensor_scalar(g_log, ps[:, 5:7, 0:384], -1.0, None, ALU.mult))
                    V.tensor_tensor(g_log, ps[:, 5:7, 0:384], g_log, ALU.max).then_inc(gla_abs, 1)
                if pos == 9:
                    dve.wait_ge(gla_soft, 1)
                    step(V.scalar_tensor_tensor(out=g_tmp, in0=ps[:, 5:7, 0:384], scalar=0.0, in1=q_dec,
                                                op0=ALU.min, op1=ALU.subtract))
                    V.tensor_scalar(g_log, g_tmp, 1.0 / 16.0, -1.0, ALU.mult, ALU.max).then_inc(gla_log, 1)
                if pos == 11:
                    dve.wait_ge(gla_exp, 1)
                    V.tensor_tensor(k_end[:, :, 0], ps[:, 6:8, 0:384], g_tmp, ALU.subtract).then_inc(gla_ops, 1)
                    V.scalar_tensor_tensor(out=q_dec, in0=q_dec, scalar=GLA_K ** -0.5, in1=proj2[:, :, BQ:BQ + 384],
                                           op0=ALU.mult, op1=ALU.mult)
                    V.tensor_tensor(k_inv, k_inv, proj2[:, :, BK:BK + 384], ALU.mult).then_inc(gla_ops, 1)
                if pos == 13:
                    dve.wait_ge(gla_exp, 2)
                    step(V.tensor_tensor(g_tmp, k_end[:, :, 1], proj2[:, :, BK:BK + 384], ALU.mult))
                    V.tensor_scalar(k_end[:, :, 0], g_tmp, KC(K_HALF, 1), None, ALU.mult)
                    V.tensor_scalar(k_end[:, :, 1], g_tmp, KC(K_HALF + 1, 1), None, ALU.mult).then_inc(gla_ops, 1)
                if pos >= 49 and pos % 2:
                    t, part = divmod((pos - 49) // 2, 4)
                    e, r = proj2[:, t, BQ:BQ + 768], proj2[:, t, BR:BR + 768]
                    if part == 0:
                        dve.wait_ge(br_exp, t + 1)
                        step(V.tensor_scalar(e, e, 1.0, None, ALU.add))
                    if part == 1:
                        step(V.reciprocal(e, e))
                    if part == 2:
                        step(V.tensor_tensor(e, e, r, ALU.mult))
                n = gla_step(pos, 15)
                if n >= 0:
                    hh, t = divmod(n, NT)
                    if n == 0:
                        dve.wait_ge(gla_decexp, 1)
                        dve.wait_ge(qdT_cleared, 1)
                    dve.wait_ge(gt_copied, n + 1)
                    V.tensor_copy(qdT[:, 0, 0:64], qdT[:, 2, 0:64])
                    V.tensor_copy(qdT[:, 1, 64:128], qdT[:, 2, 64:128])
                    dve.wait_ge(gd_made, n + 1)
                    if t == 0:
                        step(V.tensor_copy(state[:, 1], ps[0:GLA_K, 6, 0:GLA_V]))
                        V.scalar_tensor_tensor(out=state[:, 2], in0=state[:, 1], scalar=g_dec[:, 4 * hh + 1:4 * hh + 2],
                                               in1=ps[0:GLA_K, 6, GLA_V:2 * GLA_V], op0=ALU.mult,
                                               op1=ALU.add).then_inc(state_made, 1)
                    else:
                        V.scalar_tensor_tensor(out=state[:, 3], in0=state[:, 2], scalar=g_dec[:, 4 * hh + 2:4 * hh + 3],
                                               in1=ps[0:GLA_K, 6, 0:GLA_V], op0=ALU.mult,
                                               op1=ALU.add).then_inc(state_made, 1)
                n = gla_step(pos, 16)
                if n >= 0:
                    dve.wait_ge(gs_made, n + 1)
                    V.tensor_tensor(g_sc, ps[:, 5, 0:P], KC(K_GTRI), ALU.mult).then_inc(gs_masked, 1)

            gemm("in2", N2, False, "out2", 8, 2, gla)
            dve.wait_ge(copied_out, after("in2")[1])
            dve.wait_ge(kc_loaded, 32)
            V.tensor_copy(mask_b[:], KC(K_MASK, 3 * P)).then_inc(masks_made, 1)
            dve.wait_ge(small_loaded, 16 * 7)
            dve.wait_ge(bias_loaded, 16)
            i0, i1 = FOX_H + DIL_H, FOX_H + DIL_H + SWA_H
            for n in range(i0 + 1, i1 + 3):
                if n <= i1:
                    max_swa(n - 1)
                if i0 + 2 <= n <= i1 + 1:
                    copy_p(n - 2)
                if n >= i0 + 3:
                    out_head(n - 3, HD * (n - 3 - i0), True)
            for n in range(1, SB_H + 6):
                if n <= SB_H:
                    i = n - 1
                    g = i1 + i
                    dve.wait_ge(scored, g + 1)
                    if i >= 4:
                        dve.wait_ge(pv_made, g - 3)
                    V.tensor_scalar(sbz[:, i % 4], ps[:, 4 + g % 2, 0:3 * P], HD ** -0.5, None, ALU.mult)
                    step(V.tensor_scalar(sbt[:, i % 4], ps[:, 4 + g % 2, 0:3 * P], -(HD ** -0.5), None, ALU.mult))
                    V.tensor_tensor(sbt[:, i % 4], sbt[:, i % 4], sbz[:, i % 4], ALU.max).then_inc(sb_abs, 1)
                if 3 <= n <= SB_H + 2:
                    i = n - 3
                    dve.wait_ge(sb_sum, i + 1)
                    V.tensor_tensor(sbb[:, i % 4], ps[:, i % 2, 0:3 * P], sbb[:, i % 4], ALU.add).then_inc(sb_add, 1)
                if 2 <= n <= SB_H + 1:
                    i = n - 2
                    dve.wait_ge(sb_soft, i + 1)
                    step(V.scalar_tensor_tensor(out=sbb[:, i % 4], in0=sbz[:, i % 4], scalar=0.0, in1=sbt[:, i % 4],
                                                op0=ALU.min, op1=ALU.subtract))
                    step(V.tensor_tensor(sb1[:, i % 4], sbb[:, i % 4], sbz[:, i % 4], ALU.subtract))
                    V.tensor_tensor(sb1[:, i % 4, 0:P], sb1[:, i % 4, 0:P], KC(K_STRICT), ALU.mult)
                    V.tensor_tensor(sb1[:, i % 4, 2 * P:3 * P], sb1[:, i % 4, 2 * P:3 * P], KC(K_STRICT),
                                    ALU.mult).then_inc(sb_log, 1)
                if 4 <= n <= SB_H + 3:
                    i = n - 4
                    dve.wait_ge(sb_exp, i + 1)
                    V.tensor_tensor(sbw[:, i % 4, 0:P], sbw[:, i % 4, 0:P], KC(K_STRICT), ALU.mult)
                    V.tensor_tensor(sbw[:, i % 4, 2 * P:3 * P], sbw[:, i % 4, 2 * P:3 * P], KC(K_STRICT),
                                    ALU.mult).then_inc(sb_w, 1)
                if n >= 6:
                    i = n - 6
                    g = i1 + i
                    dve.wait_ge(pv_made, g + 1)
                    for t in range(NT):
                        last = V.tensor_copy(mix[:, t, 1536 + HD * i:1536 + HD * i + HD], ps[:, 2 + g % 2, HD * t:HD * t + HD])
                    last.then_inc(head_out, 1)
            gemm("out2", WIDE, True, "mlp")
            rounds("mlp", 4 * PEER_ROUNDS, MLP_ROUNDS)
            norm_scale(7)
            for q in range(NQ):
                norm_quarter(7, q)

        @block.tensor
        def _(pe):
            mm = pe.matmul

            def turn(k, norm, g):
                if g % 2 == 0:
                    pe.wait_ge(normed, NQ * norm + g // 2 + 1)
                if g >= 2 or k > 0:
                    pe.wait_ge(x_lo_made, 8 * k + g - 1)
                for kk in range(2):
                    for t in range(NT):
                        at = 2 * g + kk
                        last = pe.transpose(ps[:, 4 + g % 2, kk * S + t * P:kk * S + t * P + P],
                                            mix[:, t, at * P:at * P + P], ident)
                last.then_inc(x_turned, 1)

            def open_section(k, norm, name):
                turn(k, norm, 0)
                turn(k, norm, 1)
                for c in range(SUB):
                    pe.wait_ge(x_lo_made, 8 * k + c + 1)
                    chunk(sections[name][0], 0, c, widths.get(name, WIDE), x_hi, x_lo)
                    if c + 2 < SUB:
                        turn(k, norm, c + 2)

            def chunk(B, parity, c, n, hi, lo):
                pe.wait_ge(lo_made, SUB * B + c + 1)
                for kk in range(2):
                    k = 2 * c + kk
                    wh = w_hi[:, c % RING, kk * n:kk * n + n]
                    wl = w_lo[:, c % RING, kk * n:kk * n + n]
                    for t in range(NT):
                        o = ps[:, bank(parity, t), 0:n]
                        xh, xl = hi[:, k, t * P:t * P + P], lo[:, k, t * P:t * P + P]
                        mm(o, xh, wh, start=(k == 0), stop=False)
                        mm(o, xh, wl, start=False, stop=False)
                        last = mm(o, xl, wh, start=False, stop=(k == KT - 1))
                last.then_inc(chunk_used, 1)

            def gemm(name, k, n, kind, first=2, last=0, extra=None):
                b0, acts, adds, nb = sections[name]
                sem_, base = (copied_out, acts) if kind == "act" else (added_out, adds)

                def blk(b, parity):
                    if static(b) and b == 0:
                        open_section(k, NORM_OF[name], name)
                        return
                    if not static(b) or b >= 2:
                        pe.wait_ge(sem_, base + b - 1)
                    for c in range(SUB):
                        chunk(b0 + b, parity, c, n, x_hi, x_lo)
                        if extra and static(b) and b >= 4:
                            extra(SUB * (b - 4) + c)
                over_blocks(pe, nb, blk, first, last)

            def rounds(name, h0, count):
                b0, acts, adds, _ = sections[name]

                def turn_hidden(r, i):
                    pe.wait_ge(copied_out, acts + 4 * r + i + 1)
                    free = h0 + 4 * r + i - 1
                    if not static(free) or free > 0:
                        pe.wait_ge(hid_lo, free)
                    for jj in range(4):
                        for t in range(NT):
                            last = pe.transpose(ps[:, 4 + 2 * (i % 2) + jj // 2, (jj % 2) * S + t * P:(jj % 2) * S + t * P + P],
                                                hid[:, t, jj * P:jj * P + P], ident)
                    last.then_inc(hid_turned, 1)

                def one(r, first):
                    for i in range(8):
                        if i < 2 and first:
                            pe.wait_ge(copied_out, acts)
                            pe.wait_ge(added_out, adds)
                            if i == 0:
                                open_section(TURNS[name], NORM_OF[name], name)
                                continue
                        elif 2 <= i < 6:
                            pe.wait_ge(copied_out, acts + 4 * r + i - 1)
                        else:
                            pe.wait_ge(added_out, adds + 4 * r + (i - 5 if i >= 6 else i - 1))
                        for c in range(SUB):
                            if i == 4 and c % 2 == 0:
                                if c == 4:
                                    turn_hidden(r, 3)
                                pe.wait_ge(hid_lo, h0 + 4 * r + c // 2 + 1)
                            chunk(b0 + 8 * r + i, i % 2, c, WIDE, x_hi if i < 4 else a_hi, x_lo if i < 4 else a_lo)
                        if 1 <= i < 4:
                            turn_hidden(r, i - 1)
                one(0, True)
                with pe.Fori(1, count) as r:
                    one(r, False)

            def turn_qk(i, src, q, k):
                if i >= 2:
                    pe.wait_ge(qk_copied, i - 1)
                for n, at in enumerate((q, k)):
                    for t in range(NT):
                        last = pe.transpose(ps[0:HD, 6 + i % 2, n * S + t * P:n * S + t * P + P], src[:, t, at:at + HD], ident)
                last.then_inc(qk_turned, 1)

            def score(i, fox=None, masked=True):
                pe.wait_ge(qk_copied, i + 1)
                if i >= 2:
                    pe.wait_ge(exp_made, i - 1)
                o, q, k = ps[:, 4 + i % 2], qkT[:, i % 2, 0:S], qkT[:, i % 2, S:2 * S]
                for t, at, w in ((0, 0, P), (1, P, S)):
                    o_t = o[:, at:at + w]
                    last = mm(o_t, q[:, t * P:t * P + P], k[:, 0:w], start=True, stop=not (masked or fox is not None))
                    if fox is not None:
                        mm(o_t, c_parts[:, 0, t * P:t * P + P], pick[:, fox, 0:w], start=False, stop=False)
                        mm(o_t, pick[:, fox, 0:P], c_parts[:, 1, 0:w], start=False, stop=False)
                        last = mm(o[:, at + w - P:at + w], ident_b[:], caus, start=False, stop=True)
                    elif masked:
                        last = mm(o_t, ident_b[:], mask_b[:, at:at + w], start=False, stop=True)
                last.then_inc(scored, 1)

            def turn_p(i, due, count):
                pe.wait_ge(due, count)
                if i >= 2:
                    pe.wait_ge(p_copied, i - 1)
                for b in range(3):
                    last = pe.transpose(ps[:, i % 2, b * P:b * P + P], prob[:, i % 2, b * P:b * P + P], ident)
                last.then_inc(p_turned, 1)

            def pv(i, due, count, pT, v0, v1):
                pe.wait_ge(due, count)
                if i >= 2:
                    pe.wait_ge(head_out, i - 1)
                o = ps[:, 2 + i % 2]
                mm(o[:, 0:HD], pT[:, 0:P], v0, start=True, stop=True)
                mm(o[:, HD:2 * HD], pT[:, P:2 * P], v0, start=True, stop=False)
                mm(o[:, HD:2 * HD], pT[:, 2 * P:3 * P], v1, start=False, stop=True).then_inc(pv_made, 1)

            pe.wait_ge(fix_loaded, 16)
            gemm("in1", 0, N1, "act")
            pe.wait_ge(gate_log, 1)
            lf = fg[:, 0]
            mm(ps[0:16, 0, 0:P], lf[:, 0, :], KC(K_UTRI), start=True, stop=True)
            mm(ps[0:16, 0, P:S], lf[:, 0, :], KC(K_ONES), start=True, stop=False)
            mm(ps[0:16, 0, P:S], lf[:, 1, :], KC(K_UTRI), start=False, stop=True).then_inc(cum_made, 1)
            pe.wait_ge(cum_copied, 1)
            pe.wait_ge(masks_made, 2)
            pe.wait_ge(c_split, 1)
            pe.wait_ge(pick_made, 4)
            caus = mask_b[:, 0:P]
            pe.wait_ge(roped, NT)
            heads = FOX_H + DIL_H
            for n in range(heads + 3):
                if n < heads:
                    f = n < FOX_H
                    m = n if f else n - FOX_H
                    turn_qk(n, proj1, (FQ if f else DQ) + HD * m, (FK if f else DK) + HD * m)
                if 1 <= n <= heads:
                    score(n - 1, n - 1 if n - 1 < FOX_H else None)
                if 2 <= n <= heads + 1:
                    i = n - 2
                    if i < FOX_H:
                        turn_p(i, exp_made, i + 1)
                    else:
                        turn_p(i, counted, i - FOX_H + 1)
                if n >= 3:
                    i = n - 3
                    at = FV + HD * i if i < FOX_H else DV + HD * (i - FOX_H)
                    pv(i, p_copied, i + 1, probT[:, i % 2], proj1[:, 0, at:at + HD], proj1[:, 1, at:at + HD])
            gemm("out1", 1, WIDE, "add")
            gemm("query", 2, WIDE, "act")

            pe.wait_ge(copied_out, after("query")[1])
            for g in range(8):
                if g >= 2:
                    pe.wait_ge(pq_copied, g - 1)
                for kk in range(2):
                    for t in range(NT):
                        at = 2 * g + kk
                        last = pe.transpose(ps[:, 4 + g % 2, kk * S + t * P:kk * S + t * P + P], pq[:, t, at * P:at * P + P], ident)
                last.then_inc(pq_turned, 1)
            pe.wait_ge(pq_copied, 8)
            pe.wait_ge(small_loaded, 32)
            for n in range(8):
                t, g = n // 4, n % 4
                if n >= 2:
                    pe.wait_ge(sc_copied, n - 1)
                for j in range(4):
                    last = mm(ps[:, 6 + n % 2, j * P:j * P + P], pqT[:, 4 * g + j, t * P:t * P + P], skT[:, 4 * g + j, :],
                              start=True, stop=True)
                last.then_inc(sc_made, 1)
            pe.wait_ge(sc_copied, 8)
            b0, c0, d0, _ = sections["peer"]

            def turn_chosen():
                pe.wait_ge(chosen_made, 1)
                for s in range(3):
                    for t in range(NT):
                        last = pe.transpose(ps[:, 4 + s // 2, S * (s % 2) + t * P:S * (s % 2) + t * P + P], chosen[:, s, t], ident)
                    last.then_inc(ch_turned, 1)

            def batch(half, n):
                pe.wait_ge(one1_made, 32 * half + n + 1)
                pe.wait_ge(one2_made, 32 * half + n + 1)
                if half == 1 and n == 0:
                    pe.wait_ge(hid_lo, 16)
                if half or n >= 2:
                    pe.wait_ge(g_copied, 32 * half + n - 1)
                for j in range(8):
                    for part in range(3):
                        last = mm(ps[:, 6 + n % 2, HALF_J * j:HALF_J * (j + 1)], one1[:, n % 4, j, :],
                                  one2[:, n % 4, part, j, :], start=(part == 0), stop=(part == 2))
                last.then_inc(g_summed, 1)

            def turn_back(n, g):
                pe.wait_ge(reloaded, 16 * (n + 1))
                if not static(n) or n >= 2:
                    pe.wait_ge(hid_lo, n - 1)
                for jj in range(4):
                    for t in range(NT):
                        last = pe.transpose(ps[:, 4 + 2 * (g % 2) + jj // 2, (jj % 2) * S + t * P:(jj % 2) * S + t * P + P],
                                            back[:, t, jj * P:jj * P + P], ident)
                last.then_inc(hid_turned, 1)

            def phase(up, nd, nu, prev_up, fill_next, extra=None):
                for i in range(4):
                    if (prev_up if i < 2 else up):
                        pe.wait_ge(added_out, d0 + 4 * nu + i - 1)
                    elif static(nd) and nd == 0 and i < 2:
                        pe.wait_ge(copied_out, c0)
                    else:
                        pe.wait_ge(copied_out, c0 + 4 * nd + i - 1)
                    for c in range(SUB):
                        if up and i == 0 and c % 2 == 0:
                            pe.wait_ge(hid_lo, 4 * nu + c // 2 + 1)
                        chunk(b0 + 4 * (nd + nu) + i, i % 2, c, WIDE, a_hi if up else x_hi, a_lo if up else x_lo)
                        if i == 3 and fill_next and c % 2:
                            turn_back(4 * (nu + 1 if up else nu) + c // 2, c // 2)
                        if extra:
                            extra(SUB * i + c)

            def beside(base, half):
                def extra(pos):
                    pos += base
                    if half == 0 and pos == 67:
                        turn_chosen()
                    for n in batches_at(half, pos + 1):
                        batch(half, n)
                    if half == 0 and pos == 122 or half == 1 and pos == 58:
                        pe.wait_ge(g_copied, 32 * half + 32)
                return extra

            for r in range(4):
                phase(False, r, 0, False, r == 3, beside(32 * r, 0) if r > 1 else None)
            with pe.Fori(0, 2) as r:
                phase(True, r + 4, r, False, False)
                phase(False, r + 4, r + 1, True, True)
            phase(True, 6, 2, False, True)
            phase(True, 6, 3, True, False)
            for r in range(2):
                phase(False, 6 + r, 4, r == 0, r == 1, beside(32 * r, 1))
            phase(True, 8, 4, False, True)
            with pe.Fori(0, 2) as r:
                phase(True, 8, r + 5, True, True)
            phase(True, 8, 7, True, False)


            def gla(pos):
                if pos == 0:
                    pe.wait_ge(rel_ready, 1)
                    pe.wait_ge(small_loaded, 16 * 7)
                    mm(ps[0:SWA_H, 6, 0:TW + 1], rel[:], buck[:], start=True, stop=True).then_inc(rel_made, 1)
                if pos == 3:
                    pe.wait_ge(copied_out, sections["in2"][1] + 4)
                    for t in range(NT):
                        last = pe.transpose(ps[0:GLA_R, 4, t * P:t * P + P], proj2[:, t, BL:BL + GLA_R], ident)
                    last.then_inc(bl_turned, 1)
                if pos == 4:
                    pe.wait_ge(bl_copied, 1)
                    pe.wait_ge(row_copied, 1)
                    pe.wait_ge(pool_step, 3)
                    for t in range(NT):
                        last = mm(ps[:, 5 + t, 0:384], blT[:, t * P:t * P + P], gw[:], start=True, stop=True)
                    last.then_inc(gpre_made, 1)
                if pos == 7:
                    pe.wait_ge(gla_log, 1)
                    for t in range(NT):
                        mm(ps[:, 4 + t, 0:384], KC(K_GTRI), g_log[:, t], start=True, stop=True)
                        last = mm(ps[:, 6 + t, 0:384], KC(K_GBLK), g_log[:, t], start=True, stop=True)
                    last.then_inc(gla_sum, 1)
                if pos == 11:
                    pe.wait_ge(gla_exp, 1)
                    for hh in range(GLA_H):
                        for t in range(NT):
                            at = 4 * hh + 2 * t
                            last = mm(ps[0:GLA_K, 4, at:at + 2], g_log[:, t, GLA_K * hh:GLA_K * (hh + 1)], KC(K_HALF, 2),
                                      start=True, stop=True)
                    last.then_inc(gla_dec, 1)
                n = gla_step(pos, 14)
                if n >= 0:
                    hh, t = divmod(n, NT)
                    pe.wait_ge(gs_masked, n + 1)
                    pe.wait_ge(state_made, n + 1)
                    if n:
                        pe.wait_ge(go_copied, n)
                    o = ps[:, 7, 0:GLA_V]
                    mm(o, g_sc, proj2[:, t, BV + GLA_V * hh:BV + GLA_V * (hh + 1)], start=True, stop=False)
                    if t:
                        mm(o, qdT[:, 0, :], state[:, 2], start=False, stop=False)
                    mm(o, qdT[:, 1, :], state[:, 1 if t == 0 else 3], start=False, stop=True).then_inc(go_made, 1)
                n = gla_step(pos, 12)
                if n >= 0:
                    hh, t = divmod(n, NT)
                    c0 = GLA_K * hh
                    if n == 0:
                        pe.wait_ge(gla_ops, 3)
                        pe.wait_ge(gla_decexp, 1)
                    pe.transpose(ps[0:GLA_K, 4, 0:P], q_dec[:, t, c0:c0 + GLA_K], ident)
                    pe.transpose(ps[0:GLA_K, 4, P:S], k_inv[:, t, c0:c0 + GLA_K], ident).then_inc(gt_made, 1)
                    if n:
                        pe.wait_ge(state_made, n)
                    for c in range(2):
                        last = mm(ps[0:GLA_K, 6, GLA_V * c:GLA_V * (c + 1)], k_end[:, t, c, c0:c0 + GLA_K],
                                  proj2[:, t, BV + GLA_V * hh:BV + GLA_V * (hh + 1)], start=True, stop=True)
                    last.then_inc(gd_made, 1)
                n = gla_step(pos, 13)
                if n >= 0:
                    pe.wait_ge(gt_copied, n + 1)
                    if n:
                        pe.wait_ge(gs_masked, n)
                    mm(ps[:, 5, 0:P], qdT[:, 3, :], qdT[:, 2, :], start=True, stop=True).then_inc(gs_made, 1)

            gemm("in2", 3, N2, "act", 8, 2, gla)
            pe.wait_ge(copied_out, after("in2")[1])
            pe.wait_ge(go_copied, GLA_STEPS)
            pe.wait_ge(masks_made, 3)
            i0, i1 = heads, heads + SWA_H
            for n in range(i0, i1 + 3):
                if n < i1:
                    m = n - i0
                    turn_qk(n, proj2, AQ + HD * m, AK + HD * (m // SWA_G))
                if i0 + 1 <= n <= i1:
                    score(n - 1, None, False)
                if i0 + 2 <= n <= i1 + 1:
                    turn_p(n - 2, exp_made, n - 1)
                if n >= i0 + 3:
                    i = n - 3
                    at = AV + HD * ((i - i0) // SWA_G)
                    pv(i, p_copied, i + 1, probT[:, i % 2], proj2[:, 0, at:at + HD], proj2[:, 1, at:at + HD])
            pe.wait_ge(head_out, i1)
            for n in range(SB_H + 6):
                g = i1 + n
                if n < SB_H:
                    turn_qk(g, proj2, CQ + HD * n, CK + HD * n)
                if 1 <= n <= SB_H:
                    i = n - 1
                    g = i1 + i
                    pe.wait_ge(qk_copied, g + 1)
                    if i >= 2:
                        pe.wait_ge(sb_abs, i - 1)
                    o, q, k = ps[:, 4 + g % 2], qkT[:, g % 2, 0:S], qkT[:, g % 2, S:2 * S]
                    mm(o[:, 0:S], k[:, 0:P], q, start=True, stop=True)
                    mm(o[:, S:3 * P], k[:, P:S], q[:, P:S], start=True, stop=True).then_inc(scored, 1)
                if 3 <= n <= SB_H + 2:
                    i = n - 3
                    pe.wait_ge(sb_log, i + 1)
                    if i >= 2:
                        pe.wait_ge(sb_add, i - 1)
                    o, l1 = ps[:, i % 2], sb1[:, i % 4]
                    mm(o[:, 0:P], KC(K_SUF), l1[:, 0:P], start=True, stop=True)
                    mm(o[:, P:S], KC(K_SUF), l1[:, P:S], start=True, stop=False)
                    mm(o[:, P:S], KC(K_ONES), l1[:, S:3 * P], start=False, stop=True)
                    mm(o[:, S:3 * P], KC(K_SUF), l1[:, S:3 * P], start=True, stop=True).then_inc(sb_sum, 1)
                if 5 <= n <= SB_H + 4:
                    i = n - 5
                    at = CV + HD * i
                    pv(i1 + i, sb_w, i + 1, sbw[:, i % 4], proj2[:, 0, at:at + HD], proj2[:, 1, at:at + HD])
            gemm("out2", 4, WIDE, "add")
            rounds("mlp", 4 * PEER_ROUNDS, MLP_ROUNDS)


def blocks_of(w, n):
    k, m = w.shape
    return w.reshape(k // 256, 2, P, m // n, n).transpose(3, 0, 2, 1, 4)


def kernel(**inputs):
    import concourse.bacc as _bacc
    from concourse.bass_utils import run_bass_kernel_spmd as _run

    w = {k: np.asarray(v) for k, v in inputs.items()}
    arrays = {
        "w_in": blocks_of(w["w_in"][0], N1),
        "w_out": blocks_of(w["w_out"][0], WIDE),
        "peer_query": blocks_of(w["peer_query"][0], WIDE),
        "peer_down": w["peer_down"][0].reshape(P, 32, 4, SUB, 2, P).transpose(1, 3, 5, 4, 2, 0).reshape(32, SUB, P, 2, WIDE),
        "peer_up": w["peer_up"][0].reshape(P, 8, SUB, 2, 4, WIDE).transpose(1, 4, 2, 0, 3, 5).reshape(32, SUB, P, 2, WIDE),
        "w_in_2": blocks_of(np.concatenate([w["w_in_2"][0][:, at:end] for at, end in (
            (1280, 2816), (3584, 3600), (0, 1280), (2816, 3584), (3600, IN2))], axis=1), N2),
        "w_out_2": blocks_of(w["w_out_2"][0], WIDE),
        "w_mlp_in_2": blocks_of(w["w_mlp_in_2"][0], WIDE),
        "w_mlp_out_2": w["w_mlp_out_2"][0].reshape(4, SUB, 2, P, 4, WIDE).transpose(0, 4, 1, 3, 2, 5).reshape(16, SUB, P, 2, WIDE),
        "peer_sub_keys": w["peer_sub_keys"][0].reshape(16, NKEY, P).transpose(2, 0, 1),
        "fix": fixed_constants(), "kc": attention_constants(), "buck": bucket_constants(),
    }
    for name in ("x", "attn_norm_gain", "forget_bias", "fox_out_gain", "dil_out_gain", "ffn_norm_gain", "final_norm_gain",
                 "norm_mix_2", "swa_sinks_2", "rel_bias_2", "gla_gate_w_2", "gla_gate_b_2", "gla_norm_2", "swa_out_norm_2",
                 "sb_out_norm_2", "norm_mlp_2", "norm_final_2"):
        arrays[name] = w[name]
    nc = _bacc.Bacc("TRN2", target_bir_lowering=False, num_devices=1)
    maps, aps = {}, {}
    for name, v in arrays.items():
        maps[f"in_{name}"] = v = np.ascontiguousarray(v)
        aps[name] = nc.dram_tensor(f"in_{name}", v.shape, mybir.dt.from_np(v.dtype), kind="ExternalInput").ap()
    out = nc.dram_tensor("out_0", (1, S, D), F32, kind="ExternalOutput").ap()
    build(nc, aps, out)
    return _run(nc, [maps], core_ids=[0]).results[0]["out_0"]
```
